# Optimizing a Trainium2 kernel written in Bass

```python
import math
import jax, jax.numpy as jnp
from jax import lax
import numpy as np

D_MODEL = 1024
BATCH = 1
SEQ = 256
DEPTH = 2

RET_HEADS = 4
RET_DK = 128
RET_DV = 128
GDN_HEADS = 4
GDN_DK = 128
GDN_DV = 128
CONV_K = 4
CHUNK = 64
ROPE_BASE = 10000.0
N_BRANCH = 2
BRANCH_W = 512
D_FF = 2816
N_EXPERTS = 8
TOP_K = 2
MOE_BLOCK = 256
EPS = 1e-6
N_DENSE = (DEPTH + 1) // 2
N_MOE = DEPTH // 2
RET_QK_W = RET_HEADS * RET_DK
RET_V_W = RET_HEADS * RET_DV
GDN_QK_W = GDN_HEADS * GDN_DK
GDN_V_W = GDN_HEADS * GDN_DV
CONV_CH = 2 * GDN_QK_W + GDN_V_W
IN_SPLITS = (RET_QK_W, RET_QK_W, RET_V_W, RET_V_W, CONV_CH, GDN_V_W, GDN_HEADS, GDN_HEADS, D_MODEL, D_MODEL)
IN_COLS = sum(IN_SPLITS)

kernel_name = 'hybrid_retention_gdn_moe_block'

def rms_norm(x, w):
    xf = x.astype(jnp.float32)
    y = xf * lax.rsqrt(jnp.mean(xf * xf, axis=-1, keepdims=True) + EPS)
    return (y * w.astype(jnp.float32)).astype(x.dtype)

def head_rms(o):
    return o * lax.rsqrt(jnp.mean(o * o, axis=-1, keepdims=True) + EPS)

def l2_normalize(t):
    return t * lax.rsqrt(jnp.sum(t * t, axis=-1, keepdims=True) + EPS)

def swiglu(x, w_gate, w_up, w_down):
    return (jax.nn.silu(x @ w_gate) * (x @ w_up)) @ w_down

def split_columns(t, sizes):
    offsets = np.cumsum(sizes)[:-1].tolist()
    return jnp.split(t, offsets, axis=-1)

def rotary_tables(seq_len):
    inv_freq = ROPE_BASE ** (-jnp.arange(0, RET_DK, 2, dtype=jnp.float32) / RET_DK)
    ang = jnp.arange(seq_len, dtype=jnp.float32)[:, None] * inv_freq[None, :]
    return jnp.cos(ang), jnp.sin(ang)

def apply_rotary(t, cos, sin):
    t1, t2 = jnp.split(t, 2, axis=-1)
    c = cos[None, :, None, :]
    s = sin[None, :, None, :]
    return jnp.concatenate([t1 * c - t2 * s, t2 * c + t1 * s], axis=-1)

def to_chunks(t, n_chunks):
    b, h = t.shape[0], t.shape[2]
    t = t.reshape((b, n_chunks, CHUNK, h) + t.shape[3:])
    return jnp.moveaxis(t, 3, 1)

def from_chunks(o):
    b, h, n, c, d = o.shape
    return jnp.transpose(o, (0, 2, 3, 1, 4)).reshape(b, n * c, h, d)

def causal_depthwise_conv(x, w):
    k, c = w.shape
    return lax.conv_general_dilated(x, w[:, None, :], window_strides=(1,), padding=[(k - 1, 0)],
                                    dimension_numbers=('NWC', 'WIO', 'NWC'), feature_group_count=c)

def retention_chunkwise(q, k, v):
    b, s, h, dk = q.shape
    dv = v.shape[-1]
    n = s // CHUNK
    log_gamma = jnp.log(1.0 - jnp.exp2(-5.0 - jnp.arange(RET_HEADS, dtype=jnp.float32)))
    q, k, v = to_chunks(q, n), to_chunks(k, n), to_chunks(v, n)
    pos = jnp.arange(CHUNK, dtype=jnp.float32)
    diff = pos[:, None] - pos[None, :]
    decay = jnp.where(diff >= 0, jnp.exp(jnp.maximum(diff, 0.0)[None] * log_gamma[:, None, None]), 0.0)
    scores = jnp.einsum('bhnid,bhnjd->bhnij', q, k) * decay[None, :, None]
    o_intra = jnp.einsum('bhnij,bhnjv->bhniv', scores, v)
    k_dec = k * jnp.exp((CHUNK - 1 - pos)[None, :] * log_gamma[:, None])[None, :, None, :, None]
    kv = jnp.einsum('bhncd,bhncv->bhndv', k_dec, v)
    chunk_decay = jnp.exp(CHUNK * log_gamma)[None, :, None, None]

    def step(state, kv_n):
        return state * chunk_decay + kv_n, state

    _, prev = lax.scan(step, jnp.zeros((b, h, dk, dv), q.dtype), jnp.moveaxis(kv, 2, 0))
    q_dec = q * jnp.exp((pos + 1.0)[None, :] * log_gamma[:, None])[None, :, None, :, None]
    o_inter = jnp.einsum('bhncd,nbhdv->bhncv', q_dec, prev)
    return from_chunks(o_intra + o_inter)

def gated_delta_chunkwise(q, k, v, g, beta):
    b, s, h, dk = q.shape
    dv = v.shape[-1]
    n = s // CHUNK
    q, k, v = to_chunks(q, n), to_chunks(k, n), to_chunks(v, n)
    g, beta = to_chunks(g, n), to_chunks(beta, n)
    g_cum = jnp.cumsum(g, axis=-1)
    causal = jnp.tril(jnp.ones((CHUNK, CHUNK), dtype=bool))
    strict = jnp.tril(jnp.ones((CHUNK, CHUNK), dtype=bool), -1)
    diff = g_cum[..., :, None] - g_cum[..., None, :]
    decay = jnp.where(causal, jnp.exp(jnp.where(causal, diff, 0.0)), 0.0)
    k_beta = k * beta[..., None]
    a_mat = jnp.where(strict, jnp.einsum('bhnid,bhnjd->bhnij', k_beta, k) * decay, 0.0)
    t_mat = a_mat + jnp.eye(CHUNK, dtype=a_mat.dtype)
    u = lax.linalg.triangular_solve(t_mat, v * beta[..., None], left_side=True, lower=True, unit_diagonal=True)
    w = lax.linalg.triangular_solve(t_mat, k_beta * jnp.exp(g_cum)[..., None], left_side=True, lower=True,
                                    unit_diagonal=True)
    attn = jnp.where(causal, jnp.einsum('bhnid,bhnjd->bhnij', q, k) * decay, 0.0)
    q_dec = q * jnp.exp(g_cum)[..., None]
    g_last = g_cum[..., -1]
    k_dec = k * jnp.exp(g_last[..., None] - g_cum)[..., None]

    def step(state, xs):
        w_n, u_n, q_n, k_n, attn_n, gl_n = xs
        v_new = u_n - jnp.einsum('bhcd,bhdv->bhcv', w_n, state)
        o_n = jnp.einsum('bhcd,bhdv->bhcv', q_n, state) + jnp.einsum('bhij,bhjv->bhiv', attn_n, v_new)
        state = state * jnp.exp(gl_n)[..., None, None] + jnp.einsum('bhcd,bhcv->bhdv', k_n, v_new)
        return state, o_n

    xs = (jnp.moveaxis(w, 2, 0), jnp.moveaxis(u, 2, 0), jnp.moveaxis(q_dec, 2, 0), jnp.moveaxis(k_dec, 2, 0),
          jnp.moveaxis(attn, 2, 0), jnp.moveaxis(g_last, 2, 0))
    _, o = lax.scan(step, jnp.zeros((b, h, dk, dv), q.dtype), xs)
    return from_chunks(jnp.moveaxis(o, 0, 2))

def hybrid_mixer(hn, w_in, conv_w, a_log, dt_bias, gdn_norm, w_branch, w_out, cos, sin):
    b, s, _ = hn.shape
    f32 = jnp.float32
    proj = hn @ w_in
    rq, rk, rv, rg, gqkv, gz, ga, gb, gate_a, gate_b = split_columns(proj, IN_SPLITS)

    rq = apply_rotary(rq.astype(f32).reshape(b, s, RET_HEADS, RET_DK), cos, sin)
    rk = apply_rotary(rk.astype(f32).reshape(b, s, RET_HEADS, RET_DK), cos, sin) * (RET_DK ** -0.5)
    rv = rv.astype(f32).reshape(b, s, RET_HEADS, RET_DV)
    ret = head_rms(retention_chunkwise(rq, rk, rv)).reshape(b, s, RET_V_W)
    ret = (jax.nn.silu(rg.astype(f32)) * ret).astype(hn.dtype)

    gqkv = jax.nn.silu(causal_depthwise_conv(gqkv, conv_w))
    dq, dk_, dv_ = split_columns(gqkv, (GDN_QK_W, GDN_QK_W, GDN_V_W))
    dq = l2_normalize(dq.astype(f32).reshape(b, s, GDN_HEADS, GDN_DK)) * (GDN_DK ** -0.5)
    dk_ = l2_normalize(dk_.astype(f32).reshape(b, s, GDN_HEADS, GDN_DK))
    dv_ = dv_.astype(f32).reshape(b, s, GDN_HEADS, GDN_DV)
    beta = jax.nn.sigmoid(gb.astype(f32))
    g = -jnp.exp(a_log.astype(f32)) * jax.nn.softplus(ga.astype(f32) + dt_bias.astype(f32))
    gdn = gated_delta_chunkwise(dq, dk_, dv_, g, beta)
    gdn = head_rms(gdn) * gdn_norm.astype(f32) * jax.nn.silu(gz.astype(f32).reshape(b, s, GDN_HEADS, GDN_DV))
    gdn = gdn.reshape(b, s, GDN_V_W).astype(hn.dtype)

    y_a = ret @ w_branch[0]
    y_b = gdn @ w_branch[1]
    merged = jax.nn.sigmoid(gate_a) * y_a + jax.nn.sigmoid(gate_b) * y_b
    return merged @ w_out

def moe_swiglu(hn, router, w_gate, w_up, w_down):
    b, s, d = hn.shape
    t = b * s
    a = t * TOP_K
    n_rows = a + N_EXPERTS * MOE_BLOCK
    n_blocks = n_rows // MOE_BLOCK
    xt = hn.reshape(t, d)
    logits = (xt @ router).astype(jnp.float32)
    top_vals, top_idx = lax.top_k(logits, TOP_K)
    gate = jax.nn.softmax(top_vals, axis=-1)
    flat_e = top_idx.reshape(a)
    order = jnp.argsort(flat_e)
    sorted_e = flat_e[order]
    sorted_tok = (order // TOP_K).astype(jnp.int32)
    sorted_w = gate.reshape(a)[order]
    counts = jnp.zeros((N_EXPERTS,), jnp.int32).at[flat_e].add(1)
    padded = ((counts + MOE_BLOCK - 1) // MOE_BLOCK) * MOE_BLOCK
    start = jnp.cumsum(counts) - counts
    pend = jnp.cumsum(padded)
    pstart = pend - padded
    dest = pstart[sorted_e] + (jnp.arange(a, dtype=jnp.int32) - start[sorted_e])
    row_tok = jnp.full((n_rows,), t, jnp.int32).at[dest].set(sorted_tok)
    row_w = jnp.zeros((n_rows,), jnp.float32).at[dest].set(sorted_w)
    block_start = jnp.arange(n_blocks, dtype=jnp.int32) * MOE_BLOCK
    block_e = jnp.clip(jnp.searchsorted(pend, block_start, side='right'), 0, N_EXPERTS - 1)
    x_pad = jnp.concatenate([xt, jnp.zeros((1, d), xt.dtype)], axis=0)
    xg = x_pad[row_tok].reshape(n_blocks, MOE_BLOCK, d)

    def expert_block(args):
        xb, e = args
        return swiglu(xb, w_gate[e], w_up[e], w_down[e])

    yg = lax.map(expert_block, (xg, block_e)).reshape(n_rows, d)
    out = jax.ops.segment_sum(yg.astype(jnp.float32) * row_w[:, None], row_tok, num_segments=t + 1)[:t]
    return out.astype(hn.dtype).reshape(b, s, d)

def setup_inputs(seed: int = 0) -> dict:
    key = jax.random.key(seed)
    ks = jax.random.split(key, 20)
    f32 = jnp.float32

    def nrm(k, shape, fan_in):
        return jax.random.normal(k, shape, f32) * (fan_in ** -0.5)

    def gain(k, shape):
        return 1.0 + 0.02 * jax.random.normal(k, shape, f32)

    x = jax.random.normal(ks[0], (BATCH, SEQ, D_MODEL), f32)
    norm_mix = gain(ks[1], (DEPTH, D_MODEL))
    w_in = nrm(ks[2], (DEPTH, D_MODEL, IN_COLS), D_MODEL)
    conv_w = nrm(ks[3], (DEPTH, CONV_K, CONV_CH), CONV_K)
    a_log = jnp.log(jax.random.uniform(ks[4], (DEPTH, GDN_HEADS), f32, minval=1.0, maxval=16.0))
    dt = jnp.exp(jax.random.uniform(ks[5], (DEPTH, GDN_HEADS), f32, minval=math.log(1e-3), maxval=math.log(1e-1)))
    dt_bias = dt + jnp.log(-jnp.expm1(-dt))
    gdn_norm = gain(ks[6], (DEPTH, GDN_DV))
    w_branch = nrm(ks[7], (DEPTH, N_BRANCH, BRANCH_W, D_MODEL), BRANCH_W)
    w_out = nrm(ks[8], (DEPTH, D_MODEL, D_MODEL), D_MODEL)
    norm_ffn = gain(ks[9], (DEPTH, D_MODEL))
    dense_w_gate = nrm(ks[10], (N_DENSE, D_MODEL, D_FF), D_MODEL)
    dense_w_up = nrm(ks[11], (N_DENSE, D_MODEL, D_FF), D_MODEL)
    dense_w_down = nrm(ks[12], (N_DENSE, D_FF, D_MODEL), D_FF)
    router = nrm(ks[13], (N_MOE, D_MODEL, N_EXPERTS), D_MODEL)
    moe_w_gate = nrm(ks[14], (N_MOE, N_EXPERTS, D_MODEL, D_FF), D_MODEL)
    moe_w_up = nrm(ks[15], (N_MOE, N_EXPERTS, D_MODEL, D_FF), D_MODEL)
    moe_w_down = nrm(ks[16], (N_MOE, N_EXPERTS, D_FF, D_MODEL), D_FF)
    final_norm = gain(ks[17], (D_MODEL,))
    return {'x': x, 'norm_mix': norm_mix, 'w_in': w_in, 'conv_w': conv_w, 'a_log': a_log, 'dt_bias': dt_bias,
            'gdn_norm': gdn_norm, 'w_branch': w_branch, 'w_out': w_out, 'norm_ffn': norm_ffn,
            'dense_w_gate': dense_w_gate, 'dense_w_up': dense_w_up, 'dense_w_down': dense_w_down,
            'router': router, 'moe_w_gate': moe_w_gate, 'moe_w_up': moe_w_up, 'moe_w_down': moe_w_down,
            'final_norm': final_norm}

def reference(x, norm_mix, w_in, conv_w, a_log, dt_bias, gdn_norm, w_branch, w_out, norm_ffn,
              dense_w_gate, dense_w_up, dense_w_down, router, moe_w_gate, moe_w_up, moe_w_down, final_norm):
    cos, sin = rotary_tables(x.shape[1])
    h = x
    for layer in range(DEPTH):
        hn = rms_norm(h, norm_mix[layer])
        h = h + hybrid_mixer(hn, w_in[layer], conv_w[layer], a_log[layer], dt_bias[layer], gdn_norm[layer],
                             w_branch[layer], w_out[layer], cos, sin)
        hn = rms_norm(h, norm_ffn[layer])
        i = layer // 2
        if layer % 2 == 0:
            h = h + swiglu(hn, dense_w_gate[i], dense_w_up[i], dense_w_down[i])
        else:
            h = h + moe_swiglu(hn, router[i], moe_w_gate[i], moe_w_up[i], moe_w_down[i])
    return rms_norm(h, final_norm)


_drawn_inputs = setup_inputs


def setup_inputs(seed=0):
    import zlib

    import numpy as np

    out = dict(_drawn_inputs(seed))
    spreads = {}
    factors = {}
    for name, (base, spread) in spreads.items():
        noise = np.random.default_rng([zlib.crc32(name.encode()), seed]).standard_normal(out[name].shape)
        drawn = base * np.exp(spread * noise) if base else spread * noise
        out[name] = __import__('jax').numpy.asarray(drawn.astype(out[name].dtype))
    for name, factor in factors.items():
        out[name] = (out[name] * factor).astype(out[name].dtype)
    return out
```

```python
import math
from contextlib import ExitStack

import numpy as np
import concourse.bass as bass
from concourse import mybir

DM = 1024
SEQ = 256
DEPTH = 2
H = 4
DH = 128
CONV_K = 4
DFF = 2816
NEXP = 8
EPS = 1e-6
IN_COLS = 6152
P = 128
NT = SEQ // P
KD = DM // P
TH = NT * H

COL_RQ, COL_RK, COL_RV, COL_RG, COL_CONV, COL_GZ, COL_AB, COL_GATE = 0, 512, 1024, 1536, 2048, 3584, 4096, 4104

UNIT = 2048
SLOTS = 11
FF_CHUNK = 256
NCHUNK = DFF // FF_CHUNK
PASS_UNITS = 3 * NCHUNK
assert PASS_UNITS % SLOTS == 0
CONV_GROUPS = 3
FILL_GROUPS = [COL_RQ, COL_RK, COL_RV, COL_RG, COL_GZ]
GATE_GROUPS = 4
MIX_UNITS = 2 * (CONV_GROUPS + len(FILL_GROUPS) + GATE_GROUPS) + 4 + 4
LAYER0_UNITS = MIX_UNITS + PASS_UNITS
STATIC_UNITS = LAYER0_UNITS + MIX_UNITS

LEVELS = [1, 2, 4, 8, 16, 32, 64]
C_ID, C_ONE, C_TRI, C_MASK = 0, 128, 256, 384
C_ROT = C_MASK + 128 * len(LEVELS)
C_DEC = C_ROT + NT * 256
C_LOW = C_DEC + H * 256
C_COLS = C_LOW + NEXP * NEXP


def shape_constants():
    c = np.zeros((P, C_COLS), np.float32)
    j = np.arange(P)[:, None]
    i = np.arange(P)[None, :]
    c[:, C_ID:C_ID + P] = (i == j)
    c[:, C_ONE:C_ONE + P] = 1.0
    c[:, C_TRI:C_TRI + P] = (j <= i)
    for n, b in enumerate(LEVELS):
        same = (i // (2 * b)) == (j // (2 * b))
        c[:, C_MASK + n * P:C_MASK + (n + 1) * P] = same & (i // b > j // b)
    inv_freq = np.float32(10000.0) ** (-np.arange(0, DH, 2, dtype=np.float32) / np.float32(DH))
    ang = np.arange(SEQ, dtype=np.float32)[:, None] * inv_freq[None, :].astype(np.float32)
    cos, sin = np.cos(ang), np.sin(ang)
    for t in range(NT):
        o = C_ROT + t * 256
        rows = slice(t * P, (t + 1) * P)
        c[:, o:o + 64] = cos[rows]
        c[:, o + 64:o + 128] = cos[rows]
        c[:, o + 128:o + 192] = -sin[rows]
        c[:, o + 192:o + 256] = sin[rows]
    i2 = np.arange(2 * P)[None, :]
    for h in range(H):
        lg = math.log(1.0 - 2.0 ** (-5.0 - h))
        c[:, C_DEC + h * 256:C_DEC + (h + 1) * 256] = np.where(
            i2 >= j, np.exp(np.maximum(i2 - j, 0) * lg) * DH ** -0.5, 0.0)
    e = np.arange(NEXP)
    c[:, C_LOW:C_LOW + NEXP * NEXP] = (e[None, :] < e[:, None]).reshape(1, -1)
    return c


def build(nc, x, norm_mix, w_in, conv_w, a_log, dt_bias, gdn_norm, w_branch, w_out, norm_ffn,
          dense_w_gate, dense_w_up, dense_w_down, router, moe_w_gate, moe_w_up, moe_w_down,
          final_norm, consts, out):
    f32 = mybir.dt.float32
    ALU = mybir.AluOpType
    ACT = mybir.ActivationFunctionType
    AX = mybir.AxisListType

    ctx = ExitStack()
    with ctx:
        def sb(name, *shape):
            return ctx.enter_context(nc.sbuf_tensor(name, [P, *shape], f32))

        def sem(name):
            return ctx.enter_context(nc.semaphore(name))

        ring = sb("ring", SLOTS, UNIT)
        h = sb("h", NT, DM)
        hs = sb("hs", NT, DM)
        hnT = sb("hnT", KD, SEQ)
        cst = sb("cst", C_COLS)
        rows = sb("rows", P)
        par = sb("par", P)
        wab = sb("wab", DEPTH, KD, 8)
        wrt = sb("wrt", KD, NEXP)
        alog = sb("alog", DEPTH * H)
        dtb = sb("dtb", DEPTH * H)
        gnorm = sb("gnorm", DEPTH, DH)
        qkvT = sb("qkvT", 12, SEQ)
        th = sb("th", 2, 512)
        sq = sb("sq", 2, H, SEQ)
        work = sb("work", 4, TH * P)
        attnT = sb("attnT", TH, P)
        prod = qkvT[:, 8:12, :].rearrange("p a b -> p (a b)").rearrange("p (a b) -> p a b", b=P)
        umask = sb("umask", TH, P)
        rT = sb("rT", 2, H, SEQ)
        rv = sb("rv", NT, H * DH)
        rgs = sb("rgs", NT, H * DH)
        gzs = sb("gzs", NT, H * DH)
        st0 = umask[:, :, :].rearrange("p a b -> p (a b)").rearrange("p (h n) -> p h n", h=H)
        st1 = sb("st1", H, P)
        bv = sb("bv", NT, H * DH)
        kdec = sb("kdec", H, DH)
        sm = sb("sm", 640)
        decay, un, dinv, einv = (work[:, n, :].rearrange("p (a b) -> p a b", b=P) for n in range(4))
        vnew = work[:, 2, :].rearrange("p (t n) -> p t n", t=NT)
        fnorm = work[:, 0, :]
        gates = work[:, :, :].rearrange("p a n -> p (a n)").rearrange("p (t n) -> p t n", t=NT)
        rrot = hs[:, :, :].rearrange("p a (b n) -> p a b n", b=NT)
        o_ret = sq[:, 0, :, :].rearrange("p a b -> p (a b)").rearrange("p (t n) -> p t n", t=NT)
        o_gdn = sq[:, 1, :, :].rearrange("p a b -> p (a b)").rearrange("p (t n) -> p t n", t=NT)
        state = sb("state", H, DH)
        rhs1 = prod[:, 0:4, :].rearrange("p a b -> p (a b)")
        qs_sb = prod[:, 4:8, :].rearrange("p a b -> p (a b)")
        a1 = rT[:, :, :, :].rearrange("p a b c -> p (a b c)").rearrange("p (a n) -> p a n", n=512)
        act_sb = a1[:, 2:4, :].rearrange("p a (j n) -> p a j n", j=2)

        ident = cst[:, C_ID:C_ID + P]
        ones = cst[:, C_ONE:C_ONE + P]
        tri = cst[:, C_TRI:C_TRI + P]

        at = [0]

        def small(n):
            at[0] += n
            assert at[0] <= 640
            return sm[:, at[0] - n:at[0]]

        ss, rs = small(NT), small(NT)
        mhalf = small(16)
        gx, nx, e1, den, s1, s2, poly, sp = (small(TH) for _ in range(8))
        ea = small(DEPTH * H)
        tb, beta, gcol, gcs, ngc, cneg, hbeta = (small(TH) for _ in range(7))
        rr0, rr = small(2 * TH), small(2 * TH)
        kdarg, kdfac, eg, ceg = (small(H) for _ in range(4))
        rqs = small(TH)
        oss, ors = small(2 * TH), small(2 * TH)
        rqsq = small(TH)
        logit, rank, sel = small(NT * NEXP), small(NT * NEXP), small(NT * NEXP)
        gw = small(NT * NEXP)
        top = small(NT * 8)
        pd, p0, p1 = small(NT), small(NT), small(NT)
        gcur = small(NT)
        cmp1 = prod[:, 0, :].rearrange("p (t n) -> p t n", t=NT)
        cmp2 = prod[:, 1, :].rearrange("p (t n) -> p t n", t=NT)

        ps = [ctx.enter_context(nc.psum_tensor(f"ps{n}", [P, 512], f32)) for n in range(8)]

        def quad(ap, n=4):
            return ap.rearrange("p (a b) -> p a b", a=n)

        def over(ap, n):
            return ap.unsqueeze(2).to_broadcast([P, ap.shape[1], n])

        def tiled(ap, n):
            return ap.unsqueeze(1).to_broadcast([P, n, ap.shape[1]])

        PER_LAYER = dict(
            sumsq=2, rstd=2, hs_ready=4, hT_ps=8, hnT_ready=8,
            ab_ps=1, gat_in=1, gat_e=1, g_ready=1, beta_ready=1, trig_ready=1, diagc_ready=1,
            gc_ps=1, bc_ps=2, bcc_ps=2, dec_arg=1, kd_in=1, dec_exp=3, decay_ready=1,
            tap0=12, conv_out=3, th_conv=3, qkv_act=3, sq_ready=2, ssq_ps=1, rr_in=1, rr_ready=1,
            vtok_ps=2, ktok_ps=1, bv_ready=2, kdec_ready=1, dec_beta=2,
            kk_ps=2, qk_ps=2, un_ready=2, attn_ready=2, umask_ready=7, e1_ready=1, d1_ps=2, d1_ready=2,
            p_ps=12, p_ready=12, de_ps=12, de_ready=12,
            proj_first=9, rope_done=4, rv_done=2, th_g=4, rg_done=2, gz_half=2, gz_done=2, gate_done=8,
            vn_ps=2, vn_ready=2, st_ps=1, st_ready=1, ks_ps=1, rhs1_ready=1, qs_ps=1,
            rqT_ps=1, rkT_ps=1, rqT_ready=1, rkT_ready=1, s_ps=3, s_ready=3,
            ro_ps=2, go_ps=2, ro_sb=2, go_sb=2, rms_in=1, rms_ready=1, br_ready=2, rt_ps=2, rt_ready=2,
            ya_use=1, m_ready=2, mT_ps=4, mT_ready=4, h_upd=4,
            rope_ps=4, qs_done=1)
        S = {name: sem("s_" + name) for name in PER_LAYER}
        N_CONST = 11
        s_const = sem("s_const")
        s_fnorm = sem("s_fnorm")
        s_zero = sem("s_zero")
        s_par_ps = sem("s_par_ps")
        s_par = sem("s_par")
        s_ea = sem("s_ea")
        unit_used = sem("unit_used")
        loaded = [sem(f"loaded{n}") for n in range(SLOTS)]
        dve_chain = sem("dve_chain")
        pool_chain = sem("pool_chain")
        ffn_th = sem("ffn_th")
        ffn_a1 = sem("ffn_a1")
        ffn_act = sem("ffn_act")
        ffn_drained = sem("ffn_drained")
        gcur_ready = sem("gcur_ready")
        router_ps = sem("router_ps")
        router_e = sem("router_e")
        router_in = sem("router_in")
        s_fin_ss = sem("s_fin_ss")
        s_fin_rs = sem("s_fin_rs")
        s_final = sem("s_final")
        s_out = sem("s_out")

        def upto(layer, name, k):
            assert 0 <= k < PER_LAYER[name], (name, k)
            return layer * PER_LAYER[name] + k + 1

        def unit(i):
            return ring[:, i % SLOTS, :]

        def block_of(i):
            return unit(i).rearrange("p (k n) -> p k n", k=4)

        def w_in_units(layer, col):
            v = w_in[layer, :, col:col + 512].rearrange("(k p) n -> p k n", p=P)
            return [v[:, 0:4, :], v[:, 4:8, :]]

        def mixer_units(layer):
            u = []
            for g in range(CONV_GROUPS):
                u += w_in_units(layer, COL_CONV + 512 * g)
            for col in FILL_GROUPS:
                u += w_in_units(layer, col)
            for g in range(GATE_GROUPS):
                u += w_in_units(layer, COL_GATE + 512 * g)
            for r in range(2):
                v = w_branch[layer, r, :, :].rearrange("(k p) n -> p k n", p=P)
                u += [v[:, 0:2, :], v[:, 2:4, :]]
            v = w_out[layer, :, :].rearrange("(k p) n -> p k n", p=P)
            u += [v[:, 2 * n:2 * n + 2, :] for n in range(4)]
            assert len(u) == MIX_UNITS
            return u

        def pass_order():
            o = []
            for c in range(NCHUNK):
                o += [("gate", c), ("up", c)]
                if c:
                    o.append(("down", c - 1))
            return o + [("down", NCHUNK - 1)]

        def pass_unit(wg, wu, wd, kind, c):
            cols = slice(c * FF_CHUNK, (c + 1) * FF_CHUNK)
            if kind == "down":
                return wd(cols).rearrange("(j p) n -> p j n", p=P)
            return (wg if kind == "gate" else wu)(cols).rearrange("(k p) n -> p k n", p=P)

        block = ctx.enter_context(nc.Block())

        @block.sync
        def _(sp):
            for dst, src in [
                    (h[:, :, :], x[0, :, :].rearrange("(t p) n -> p t n", p=P)),
                    (cst[:, :], consts),
                    (rows[0:16, :], norm_mix.rearrange("l (k p) -> (l k) p", p=P)),
                    (rows[16:32, :], norm_ffn.rearrange("l (k p) -> (l k) p", p=P)),
                    (rows[32:128, :], conv_w.rearrange("l t (k p) -> (l t k) p", p=P)),
                    (wab[:, 0, :, :], w_in[0, :, COL_AB:COL_AB + 8].rearrange("(k p) n -> p k n", p=P)),
                    (wab[:, 1, :, :], w_in[1, :, COL_AB:COL_AB + 8].rearrange("(k p) n -> p k n", p=P)),
                    (wrt[:, :, :], router[0, :, :].rearrange("(k p) n -> p k n", p=P)),
                    (alog[:, :], a_log.rearrange("(o l) n -> o (l n)", o=1).to_broadcast([P, DEPTH * H])),
                    (dtb[:, :], dt_bias.rearrange("(o l) n -> o (l n)", o=1).to_broadcast([P, DEPTH * H])),
                    (gnorm[:, :, :].rearrange("p l n -> p (l n)"),
                     gdn_norm.rearrange("(o l) n -> o (l n)", o=1).to_broadcast([P, DEPTH * DH]))]:

                sp.dma_start(dst, src).then_inc(s_const, 16)

            def load(i, src):
                if i >= SLOTS:
                    sp.wait_ge(unit_used, i - SLOTS + 1)
                shape = unit(i).rearrange("p (k n) -> p k n", k=src.shape[1])
                sp.dma_start(shape, src).then_inc(loaded[i % SLOTS], 16)

            i = 0
            for layer in range(DEPTH):
                for src in mixer_units(layer):
                    load(i, src)
                    i += 1
                if layer == 0:
                    for kind, c in pass_order():
                        load(i, pass_unit(lambda s: dense_w_gate[0, :, s], lambda s: dense_w_up[0, :, s],
                                          lambda s: dense_w_down[0, s, :], kind, c))
                        i += 1
            assert i == STATIC_UNITS
            with sp.Fori(0, NEXP) as e:
                for j, (kind, c) in enumerate(pass_order()):
                    i = STATIC_UNITS + j
                    src = pass_unit(lambda s: moe_w_gate[0, e, :, s], lambda s: moe_w_up[0, e, :, s],
                                    lambda s: moe_w_down[0, e, s, :], kind, c)
                    sp.wait_ge(unit_used, e * PASS_UNITS + (i - SLOTS + 1))
                    shape = unit(i).rearrange("p (k n) -> p k n", k=src.shape[1])
                    sp.dma_start(shape, src).then_inc(loaded[i % SLOTS], 16)

            for t in range(NT):
                sp.wait_ge(s_final, t + 1)
                sp.dma_start(out[0, t * P:(t + 1) * P, :], hs[:, t, :]).then_inc(s_out, 16)
            sp.wait_ge(s_out, 16 * NT)

        @block.tensor
        def _(pe):
            mm = nc.tensor.matmul
            used = [0]

            def arrived(i):
                pe.wait_ge(loaded[i % SLOTS], 16 * (i // SLOTS + 1))

            def w(layer, name, k):
                pe.wait_ge(S[name], upto(layer, name, k))

            def norm_transposes(layer, n):
                w(layer, "hs_ready", 2 * n + 1)
                for m in range(4):
                    for k in (2 * m, 2 * m + 1):
                        for t in range(NT):
                            last = nc.tensor.transpose(ps[m][:, (k % 2) * SEQ + t * P:(k % 2) * SEQ + (t + 1) * P],
                                                       hs[:, t, k * P:(k + 1) * P], ident)
                    last.then_inc(S["hT_ps"], 1)

            def proj_block(layer, i, t, bank):
                if t == 0:
                    arrived(i)
                    arrived(i + 1)
                for k in range(KD):
                    m = mm(ps[bank][:, :], hnT[:, k, t * P:(t + 1) * P], block_of(i + k // 4)[:, k % 4, :],
                           start=(k == 0), stop=(k == KD - 1))
                    if t == 1 and k in (3, 7):
                        m.then_inc(unit_used, 1)
                    elif k == KD - 1:
                        m.then_inc(S["proj_first"], 1)

            def mixer(layer, base):
                norm_transposes(layer, 0)
                w(layer, "hnT_ready", 3)
                for t in range(NT):
                    for k in range(KD):
                        last = mm(ps[6][:, 8 * t:8 * t + 8], hnT[:, k, t * P:(t + 1) * P], wab[:, layer, k, :],
                                  start=(k == 0), stop=(k == KD - 1))
                last.then_inc(S["ab_ps"], 1)
                for g in range(CONV_GROUPS):
                    i = base + 2 * g
                    arrived(i)
                    arrived(i + 1)
                    for ct in range(4):
                        for k in range(KD):
                            m = mm(ps[2 * g + ct // 2][:, (ct % 2) * SEQ:(ct % 2 + 1) * SEQ],
                                   block_of(i + k // 4)[:, k % 4, ct * P:(ct + 1) * P], hnT[:, k, :],
                                   start=(k == 0), stop=(k == KD - 1))
                            if ct == 3 and k in (3, 7):
                                m.then_inc(unit_used, 1)
                w(layer, "g_ready", 0)
                mm(ps[6][:, 64:64 + TH], tri, gcol, start=True, stop=True).then_inc(S["gc_ps"], 1)
                w(layer, "trig_ready", 0)
                w(layer, "conv_out", 0)
                for t in range(NT):
                    mm(ps[t][:, :], ones, einv[:, 4 * t:4 * t + 4, :].rearrange("p a b -> p (a b)"),
                       start=True, stop=True).then_inc(S["bc_ps"], 1)
                w(layer, "sq_ready", 1)
                for g in range(2):
                    for t in range(NT):
                        for hh in range(H):
                            c = 32 + g * TH + t * H + hh
                            last = mm(ps[7][:, c:c + 1], sq[:, g, hh, t * P:(t + 1) * P], ones[:, 0:1],
                                      start=True, stop=True)
                last.then_inc(S["ssq_ps"], 1)
                w(layer, "conv_out", 1)
                for t in range(NT):
                    for hh in range(H):
                        kt = qkvT[:, 4 + hh, t * P:(t + 1) * P]
                        last = mm(ps[2 + t][:, hh * P:(hh + 1) * P], kt, kt, start=True, stop=True)
                    last.then_inc(S["kk_ps"], 1)
                w(layer, "qkv_act", 2)
                for t in range(NT):
                    for hh in range(H):
                        last = nc.tensor.transpose(ps[4 + t][:, hh * P:(hh + 1) * P],
                                                   qkvT[:, 8 + hh, t * P:(t + 1) * P], ident)
                    last.then_inc(S["vtok_ps"], 1)
                w(layer, "rr_in", 0)
                for hh in range(H):
                    last = nc.tensor.transpose(ps[7][:, hh * P:(hh + 1) * P], qkvT[:, 4 + hh, 0:P], ident)
                last.then_inc(S["ktok_ps"], 1)
                w(layer, "diagc_ready", 0)
                w(layer, "dec_arg", 0)
                for t in range(NT):
                    mm(ps[t][:, :], ones, umask[:, 4 * t:4 * t + 4, :].rearrange("p a b -> p (a b)"),
                       start=True, stop=True).then_inc(S["bcc_ps"], 1)
                w(layer, "bv_ready", 1)
                for t in range(NT):
                    for hh in range(H):
                        last = mm(ps[4 + t][:, hh * P:(hh + 1) * P], qkvT[:, 4 + hh, t * P:(t + 1) * P],
                                  qkvT[:, hh, t * P:(t + 1) * P], start=True, stop=True)
                    last.then_inc(S["qk_ps"], 1)
                w(layer, "e1_ready", 0)
                w(layer, "un_ready", 1)
                for t in range(NT):
                    for hh in range(H):
                        last = nc.tensor.transpose(ps[2 + t][:, hh * P:(hh + 1) * P], einv[:, 4 * t + hh, :], ident)
                    last.then_inc(S["d1_ps"], 1)
                fill = [(g, t) for g in range(len(FILL_GROUPS)) for t in range(NT)]
                fill_base = base + 2 * CONV_GROUPS
                free = {0: "rope_done", 1: "rope_done", 2: "rv_done", 3: "rg_done"}

                def filler():
                    if not fill:
                        return
                    g, t = fill.pop(0)
                    if g == 0:
                        w(layer, "un_ready", 1)
                    else:
                        name = free[g - 1]
                        w(layer, name, (2 * (g - 1) if name == "rope_done" else 0) + t)
                    proj_block(layer, fill_base + 2 * g, t, t)

                for lv in range(1, len(LEVELS)):
                    n = 2 * (lv - 1)
                    w(layer, "umask_ready", lv)
                    for t in range(NT):
                        if lv == 1:
                            w(layer, "d1_ready", t)
                        else:
                            w(layer, "de_ready", n - 2 + t)
                        for hh in range(H):
                            a = 4 * t + hh
                            last = mm(ps[2 + t][:, hh * P:(hh + 1) * P], umask[:, a, :], dinv[:, a, :],
                                      start=True, stop=True)
                        last.then_inc(S["p_ps"], 1)
                    filler()
                    for t in range(NT):
                        w(layer, "p_ready", n + t)
                        if lv == 1:
                            w(layer, "attn_ready", t)
                            w(layer, "kdec_ready", 0)
                        if lv < len(LEVELS) - 1:
                            for hh in range(H):
                                a = 4 * t + hh
                                mm(ps[4 + t][:, hh * P:(hh + 1) * P], einv[:, a, :], prod[:, a, :],
                                   start=True, stop=True)
                        for hh in range(H):
                            a = 4 * t + hh
                            last = mm(ps[6 + t][:, hh * P:(hh + 1) * P], prod[:, a, :], einv[:, a, :],
                                      start=True, stop=True)
                        last.then_inc(S["de_ps"], 1)
                    filler()
                assert not fill
                w(layer, "de_ready", 10)
                w(layer, "bv_ready", 1)
                for hh in range(H):
                    last = mm(ps[2][:, hh * P:(hh + 1) * P], einv[:, hh, :], bv[:, 0, hh * P:(hh + 1) * P],
                              start=True, stop=True)
                last.then_inc(S["vn_ps"], 1)
                w(layer, "rope_done", 3)
                w(layer, "gz_half", 1)
                for hh in range(H):
                    for t in range(NT):
                        last = nc.tensor.transpose(
                            ps[hh // 2][:, (hh % 2) * SEQ + t * P:(hh % 2) * SEQ + (t + 1) * P],
                            rrot[:, 0, t, hh * P:(hh + 1) * P], ident)
                last.then_inc(S["rqT_ps"], 1)
                w(layer, "vn_ready", 0)
                w(layer, "kdec_ready", 0)
                for hh in range(H):
                    last = mm(ps[3][:, hh * P:(hh + 1) * P], kdec[:, hh, :], vnew[:, 0, hh * P:(hh + 1) * P],
                              start=True, stop=True)
                last.then_inc(S["st_ps"], 1)
                for hh in range(H):
                    for t in range(NT):
                        last = nc.tensor.transpose(
                            ps[4 + hh // 2][:, (hh % 2) * SEQ + t * P:(hh % 2) * SEQ + (t + 1) * P],
                            rrot[:, 1, t, hh * P:(hh + 1) * P], ident)
                last.then_inc(S["rkT_ps"], 1)
                w(layer, "st_ready", 0)
                for hh in range(H):
                    last = mm(ps[2][:, hh * P:(hh + 1) * P], qkvT[:, 4 + hh, P:SEQ], state[:, hh, :],
                              start=True, stop=True)
                last.then_inc(S["ks_ps"], 1)
                w(layer, "rqT_ready", 0)
                w(layer, "rkT_ready", 0)
                for hh in range(H):
                    last = mm(ps[hh // 2][:, (hh % 2) * SEQ:(hh % 2 + 1) * SEQ], rT[:, 1, hh, 0:P], rT[:, 0, hh, :],
                              start=True, stop=True)
                    if hh % 2:
                        last.then_inc(S["s_ps"], 1)
                for hh in range(H):
                    last = mm(ps[3][:, hh * P:(hh + 1) * P], rT[:, 1, hh, P:SEQ], rT[:, 0, hh, P:SEQ],
                              start=True, stop=True)
                last.then_inc(S["s_ps"], 1)
                for hh in range(H):
                    last = mm(ps[5][:, hh * P:(hh + 1) * P], qkvT[:, hh, P:SEQ], state[:, hh, :],
                              start=True, stop=True)
                last.then_inc(S["qs_ps"], 1)
                w(layer, "rhs1_ready", 0)
                w(layer, "de_ready", 11)
                for hh in range(H):
                    last = mm(ps[4][:, hh * P:(hh + 1) * P], einv[:, 4 + hh, :], rhs1[:, hh * P:(hh + 1) * P],
                              start=True, stop=True)
                last.then_inc(S["vn_ps"], 1)
                w(layer, "s_ready", 2)
                w(layer, "rv_done", 1)
                for t in range(NT):
                    for hh in range(H):
                        c = slice(hh * P, (hh + 1) * P)
                        last = mm(ps[t][:, c], st0[:, hh, t * P:(t + 1) * P], rv[:, 0, c],
                                  start=True, stop=(t == 0))
                        if t == 1:
                            last = mm(ps[t][:, c], st1[:, hh, :], rv[:, 1, c], start=False, stop=True)
                    last.then_inc(S["ro_ps"], 1)
                for t in range(NT):
                    w(layer, "vn_ready", t)
                    for hh in range(H):
                        c = slice(hh * P, (hh + 1) * P)
                        last = mm(ps[6 + t][:, c], attnT[:, 4 * t + hh, :], vnew[:, t, c], start=True, stop=True)
                    last.then_inc(S["go_ps"], 1)
                i = fill_base + 2 * len(FILL_GROUPS)
                w(layer, "rhs1_ready", 0)
                for g in range(GATE_GROUPS):
                    for t in range(NT):
                        if g:
                            w(layer, "gate_done", 2 * (g - 1) + t)
                        proj_block(layer, i + 2 * g, t, 2 + t)
                w(layer, "qs_done", 0)
                for r, src in enumerate((o_ret, o_gdn)):
                    w(layer, "br_ready", r)
                    for hh in range(H):
                        for t in range(NT):
                            last = nc.tensor.transpose(
                                ps[4 + 2 * r + hh // 2][:, (hh % 2) * SEQ + t * P:(hh % 2) * SEQ + (t + 1) * P],
                                src[:, t, hh * P:(hh + 1) * P], ident)
                    last.then_inc(S["rt_ps"], 1)
                i += 2 * GATE_GROUPS
                w(layer, "gate_done", 7)
                for r in range(2):
                    w(layer, "rt_ready", r)
                    if r:
                        w(layer, "rt_ready", 1)
                    for n in range(2):
                        arrived(i)
                        v = unit(i).rearrange("p (k n) -> p k n", k=2)
                        for k in (2 * n, 2 * n + 1):
                            for t in range(NT):
                                for f in range(2):
                                    last = mm(ps[4 * r + 2 * t + f][:, :], rT[:, r, k, t * P:(t + 1) * P],
                                              v[:, k % 2, f * 512:(f + 1) * 512], start=(k == 0), stop=(k == 3))
                        last.then_inc(unit_used, 1)
                        i += 1
                w(layer, "m_ready", 1)
                for m in range(4):
                    for k in (2 * m, 2 * m + 1):
                        for t in range(NT):
                            last = nc.tensor.transpose(ps[m][:, (k % 2) * SEQ + t * P:(k % 2) * SEQ + (t + 1) * P],
                                                       hs[:, t, k * P:(k + 1) * P], ident)
                    last.then_inc(S["mT_ps"], 1)
                for n in range(4):
                    arrived(i)
                    w(layer, "mT_ready", n)
                    v = unit(i).rearrange("p (k n) -> p k n", k=2)
                    for k in (2 * n, 2 * n + 1):
                        for t in range(NT):
                            for f in range(2):
                                last = mm(ps[4 + 2 * t + f][:, :], hnT[:, k, t * P:(t + 1) * P],
                                          v[:, k % 2, f * 512:(f + 1) * 512], start=(k == 0), stop=(k == KD - 1))
                    last.then_inc(unit_used, 1)
                    i += 1
                assert i == base + MIX_UNITS

            def ffn_pass(base, first, it, e):
                def wait_unit(i):
                    if e is None:
                        arrived(i)
                    else:
                        pe.wait_ge(loaded[i % SLOTS], e * (16 * PASS_UNITS // SLOTS) + 16 * (i // SLOTS + 1))

                for j, (kind, c) in enumerate(pass_order()):
                    i = base + j
                    wait_unit(i)
                    if kind == "down":
                        pe.wait_ge(ffn_act, it * NCHUNK + c + 1)
                        if c == 0 and not first:
                            pe.wait_ge(ffn_drained, it * 4)
                        v = unit(i).rearrange("p (j n) -> p j n", j=2)
                        for jj in range(2):
                            for t in range(NT):
                                for f in range(2):
                                    last = mm(ps[4 + 2 * t + f][:, :], act_sb[:, c % 2, jj, t * P:(t + 1) * P],
                                              v[:, jj, f * 512:(f + 1) * 512],
                                              start=(c == 0 and jj == 0), stop=(c == NCHUNK - 1 and jj == 1))
                    else:
                        n = 2 * (c % 2) + (kind == "up")
                        if c >= 2:
                            pe.wait_ge(ffn_act, it * NCHUNK + c - 1)
                        elif not first:
                            pe.wait_ge(ffn_act, it * NCHUNK + c - 1)
                        v = unit(i).rearrange("p (k n) -> p k n", k=KD)
                        for jj in range(2):
                            for k in range(KD):
                                last = mm(ps[n][:, jj * SEQ:(jj + 1) * SEQ], v[:, k, jj * P:(jj + 1) * P],
                                          hnT[:, k, :], start=(k == 0), stop=(k == KD - 1))
                    last.then_inc(unit_used, 1)

            pe.wait_ge(s_const, 16 * N_CONST)
            nc.tensor.transpose(ps[7][:, 0:P], rows[:, :], ident).then_inc(s_par_ps, 1)
            mixer(0, 0)
            norm_transposes(0, 1)
            w(0, "hnT_ready", 7)
            ffn_pass(MIX_UNITS, True, 0, None)
            mixer(1, LAYER0_UNITS)
            norm_transposes(1, 1)
            w(1, "hnT_ready", 7)
            for t in range(NT):
                for k in range(KD):
                    last = mm(ps[0][:, t * 8:(t + 1) * 8], hnT[:, k, t * P:(t + 1) * P], wrt[:, k, :],
                              start=(k == 0), stop=(k == KD - 1))
            last.then_inc(router_ps, 1)
            pe.wait_ge(router_in, 1)
            with pe.Fori(0, NEXP) as e:
                ffn_pass(STATIC_UNITS, False, e + 1, e)

        @block.scalar
        def _(act):
            go = nc.scalar.activation

            def w(layer, name, k):
                act.wait_ge(S[name], upto(layer, name, k))

            def scale_rows(layer, n):
                for t in range(NT):
                    w(layer, "rstd", n)
                    go(hs[:, t, :], h[:, t, :], ACT.Copy, scale=rs[:, t:t + 1]).then_inc(S["hs_ready"], 1)

            def mixer(layer, base):
                scale_rows(layer, 0)
                w(layer, "gat_in", 0)
                go(e1, nx, ACT.Exp)
                go(tb, ps[6][:, 0:16].rearrange("p (t n) -> p t n", t=NT)[:, :, 4:8], ACT.Tanh,
                   scale=0.5).then_inc(S["gat_e"], 1)
                for g in range(CONV_GROUPS):
                    act.wait_ge(unit_used, base + 2 * g + 2)
                    for ct in range(4):
                        col = 32 + layer * 48 + 3 * 12 + 4 * g + ct
                        go(qkvT[:, 4 * g + ct, :], ps[2 * g + ct // 2][:, (ct % 2) * SEQ:(ct % 2 + 1) * SEQ],
                           ACT.Copy, scale=par[:, col:col + 1]).then_inc(S["tap0"], 1)
                    w(layer, "conv_out", g)
                    if g:
                        w(layer, "qkv_act", g - 1)
                    go(th[:, :, :].rearrange("p a b -> p (a b)"),
                       qkvT[:, 4 * g:4 * g + 4, :].rearrange("p a b -> p (a b)"), ACT.Tanh,
                       scale=0.5).then_inc(S["th_conv"], 1)
                w(layer, "dec_arg", 0)
                go(decay, decay, ACT.Exp).then_inc(S["dec_exp"], 1)
                w(layer, "kd_in", 0)
                go(kdfac, kdarg, ACT.Exp).then_inc(S["dec_exp"], 1)
                go(eg, gcs[:, H:TH], ACT.Exp).then_inc(S["dec_exp"], 1)
                for t in range(NT):
                    w(layer, "d1_ps", t)
                    go(dinv[:, 4 * t:4 * t + 4, :].rearrange("p a b -> p (a b)"), ps[2 + t][:, :],
                       ACT.Copy).then_inc(S["d1_ready"], 1)
                fill = [(g, t) for g in range(len(FILL_GROUPS)) for t in range(NT)]

                def filler():
                    if not fill:
                        return
                    g, t = fill.pop(0)
                    if g < 2:
                        return
                    if t == 0:
                        w(layer, "proj_first", g)
                    else:
                        act.wait_ge(unit_used, base + 2 * CONV_GROUPS + 2 * g + 2)
                    if g == 2:
                        go(rv[:, t, :], ps[t][:, :], ACT.Copy).then_inc(S["rv_done"], 1)
                    else:
                        n = 2 * (g - 3) + t
                        w(layer, "rope_done" if g == 3 else "rg_done", 3 if g == 3 else t)
                        go(th[:, t, :], ps[t][:, :], ACT.Tanh, scale=0.5).then_inc(S["th_g"], 1)

                for lv in range(1, len(LEVELS)):
                    for t in range(NT):
                        n = 2 * (lv - 1) + t
                        w(layer, "p_ps", n)
                        if n >= 2:
                            w(layer, "de_ps", n - 2)
                        go(prod[:, 4 * t:4 * t + 4, :].rearrange("p a b -> p (a b)"), ps[2 + t][:, :],
                           ACT.Copy).then_inc(S["p_ready"], 1)
                    filler()
                    filler()
                w(layer, "vn_ps", 0)
                go(vnew[:, 0, :], ps[2][:, :], ACT.Copy).then_inc(S["vn_ready"], 1)
                w(layer, "rqT_ps", 0)
                go(rT[:, 0, 0:2, :], quad(ps[0][:, :], 2), ACT.Copy)
                go(rT[:, 0, 2:4, :], quad(ps[1][:, :], 2), ACT.Copy).then_inc(S["rqT_ready"], 1)
                w(layer, "st_ps", 0)
                go(state[:, :, :], quad(ps[3][:, :]), ACT.Copy).then_inc(S["st_ready"], 1)
                w(layer, "rkT_ps", 0)
                go(rT[:, 1, 0:2, :], quad(ps[4][:, :], 2), ACT.Copy)
                go(rT[:, 1, 2:4, :], quad(ps[5][:, :], 2), ACT.Copy).then_inc(S["rkT_ready"], 1)
                w(layer, "vn_ps", 1)
                go(vnew[:, 1, :], ps[4][:, :], ACT.Copy).then_inc(S["vn_ready"], 1)
                w(layer, "go_ps", 1)
                for g in range(GATE_GROUPS):
                    for t in range(NT):
                        if t == 0:
                            w(layer, "proj_first", 5 + g)
                        else:
                            act.wait_ge(unit_used, base + 2 * (CONV_GROUPS + len(FILL_GROUPS) + g) + 2)
                        go(gates[:, t, g * 512:(g + 1) * 512], ps[2 + t][:, :], ACT.Tanh,
                           scale=0.5).then_inc(S["gate_done"], 1)
                for r in range(2):
                    w(layer, "rt_ps", r)
                    go(rT[:, r, 0:2, :], quad(ps[4 + 2 * r][:, :], 2), ACT.Copy)
                    go(rT[:, r, 2:4, :], quad(ps[5 + 2 * r][:, :], 2), ACT.Copy).then_inc(S["rt_ready"], 1)
                for m in range(4):
                    w(layer, "mT_ps", m)
                    go(hnT[:, 2 * m:2 * m + 2, :], quad(ps[m][:, :], 2), ACT.Copy).then_inc(S["mT_ready"], 1)

            def ffn_pass(base, first, it, off):
                order = pass_order()
                for c in range(NCHUNK):
                    act.wait_ge(unit_used, off + base + order.index(("gate", c)) + 1)
                    if not (first and c < 2):
                        act.wait_ge(ffn_a1, it * NCHUNK + c - 1)
                    go(th[:, c % 2, :], ps[2 * (c % 2)][:, :], ACT.Tanh, scale=0.5).then_inc(ffn_th, 1)

            act.wait_ge(s_const, 16 * N_CONST)
            go(ea, alog[:, :], ACT.Exp).then_inc(s_ea, 1)
            act.wait_ge(s_par, 1)
            mixer(0, 0)
            scale_rows(0, 1)
            ffn_pass(MIX_UNITS, True, 0, 0)
            mixer(1, LAYER0_UNITS)
            scale_rows(1, 1)
            act.wait_ge(S["m_ready"], upto(1, "m_ready", 1))
            act.dma_start(fnorm, final_norm.rearrange("(o n) -> o n", o=1).to_broadcast([P, DM])).then_inc(s_fnorm, 16)
            act.wait_ge(router_in, 1)
            go(pd, p0, ACT.Exp).then_inc(router_e, 1)
            with act.Fori(0, NEXP) as e:
                ffn_pass(STATIC_UNITS, False, e + 1, e * PASS_UNITS)

        @block.gpsimd
        def _(pool):
            tt, tsc = nc.gpsimd.tensor_tensor, nc.gpsimd.tensor_scalar
            n_chain = [0]

            def link(ins):
                n_chain[0] += 1
                ins.then_inc(pool_chain, 1)
                pool.wait_ge(pool_chain, n_chain[0])

            def w(layer, name, k):
                pool.wait_ge(S[name], upto(layer, name, k))

            def rstd(layer, n):
                w(layer, "sumsq", n)
                link(tsc(rs, ss, 1.0 / DM, EPS, ALU.mult, ALU.add))
                tt(rs, rs, mhalf[:, 0:NT], ALU.pow).then_inc(S["rstd"], 1)

            def mixer(layer, base):
                rstd(layer, 0)
                w(layer, "g_ready", 0)
                tt(einv, tiled(tri, TH), over(gcol, P), ALU.mult).then_inc(S["trig_ready"], 1)
                w(layer, "dec_exp", 0)
                tt(decay, decay, tiled(tri, TH), ALU.mult).then_inc(S["decay_ready"], 1)
                w(layer, "rr_in", 0)
                tt(rr, rr0, mhalf, ALU.pow).then_inc(S["rr_ready"], 1)
                w(layer, "rr_ready", 0)
                w(layer, "beta_ready", 0)
                link(tt(cneg, rr[:, TH:2 * TH], beta, ALU.mult))
                link(tsc(cneg, cneg, -1.0, None, ALU.mult))
                tt(umask[:, :, :], tiled(ident, TH), over(cneg, P), ALU.mult).then_inc(S["diagc_ready"], 1)
                w(layer, "un_ready", 1)
                for lv in range(len(LEVELS)):
                    if lv == 0:
                        w(layer, "bcc_ps", 1)
                    elif lv == 1:
                        w(layer, "e1_ready", 0)
                    else:
                        w(layer, "p_ps", 2 * (lv - 2) + 1)
                    tt(umask[:, :, :], un, tiled(cst[:, C_MASK + lv * P:C_MASK + (lv + 1) * P], TH),
                       ALU.mult).then_inc(S["umask_ready"], 1)
                for t in range(NT):
                    w(layer, "gz_half", t)
                    tt(quad(gzs[:, t, :]), quad(gzs[:, t, :]), tiled(gnorm[:, layer, :], H),
                       ALU.mult).then_inc(S["gz_done"], 1)
                w(layer, "rms_in", 0)
                tt(ors, oss, mhalf, ALU.pow).then_inc(S["rms_ready"], 1)

            pool.memset(mhalf, -0.5).then_inc(s_zero, 1)
            pool.wait_ge(s_zero, 1)
            pool.wait_ge(s_const, 16 * N_CONST)
            for layer in range(DEPTH):
                mixer(layer, 0)
                rstd(layer, 1)
            pool.wait_ge(s_fin_ss, 1)
            link(tsc(rs, ss, 1.0 / DM, EPS, ALU.mult, ALU.add))
            tt(rs, rs, mhalf[:, 0:NT], ALU.pow).then_inc(s_fin_rs, 1)

        @block.vector
        def _(dve):
            V = nc.vector
            tt, tsc, stt = V.tensor_tensor, V.tensor_scalar, V.scalar_tensor_tensor
            n_chain = [0]

            def link(ins):
                n_chain[0] += 1
                ins.then_inc(dve_chain, 1)
                dve.wait_ge(dve_chain, n_chain[0])

            def sig(ins, name):
                return ins.then_inc(S[name], 1)

            def w(layer, name, k):
                dve.wait_ge(S[name], upto(layer, name, k))

            def sumsq(signal):
                for t in range(NT):
                    last = V.tensor_tensor_reduce(out=hs[:, t, :], in0=h[:, t, :], in1=h[:, t, :], scale=1.0,
                                                  scalar=0.0, op0=ALU.mult, op1=ALU.add, accum_out=ss[:, t:t + 1])
                last.then_inc(signal, 1)

            def norm(layer, n):
                sumsq(S["sumsq"])
                for m in range(4):
                    w(layer, "hT_ps", 4 * n + m)
                    col = 16 * n + layer * KD + 2 * m
                    sig(tt(hnT[:, 2 * m:2 * m + 2, :], quad(ps[m][:, :], 2), over(par[:, col:col + 2], SEQ),
                           ALU.mult), "hnT_ready")

            def mixer(layer, base):
                norm(layer, 0)
                w(layer, "ab_ps", 0)
                ab = ps[6][:, 0:16].rearrange("p (t n) -> p t n", t=NT)
                dt2 = tiled(dtb[:, layer * H:(layer + 1) * H], NT)
                ea2 = tiled(ea[:, layer * H:(layer + 1) * H], NT)
                gx2 = quad(gx, NT)
                link(tt(gx2, ab[:, :, 0:H], dt2, ALU.add))
                link(tsc(nx, gx, -1.0, None, ALU.mult))
                sig(tt(nx, nx, gx, ALU.min), "gat_in")
                w(layer, "gat_e", 0)
                link(tsc(beta, tb, 0.5, 0.5, ALU.mult, ALU.add))
                link(tsc(hbeta, beta, 0.5, None, ALU.mult))
                link(tsc(den, e1, 2.0, None, ALU.add))
                link(V.reciprocal(den, den))
                link(tt(s1, e1, den, ALU.mult))
                link(tt(s2, s1, s1, ALU.mult))
                link(tsc(poly, s2, 1.0 / 19, None, ALU.mult))
                for k in range(8, 0, -1):
                    link(stt(poly, poly, 1.0 / (2 * k + 1), s2, ALU.add, ALU.mult))
                link(stt(poly, poly, 1.0, s1, ALU.add, ALU.mult))
                link(tsc(sp, gx, 0.0, None, ALU.max))
                link(stt(sp, poly, 2.0, sp, ALU.mult, ALU.add))
                if layer == 0:
                    dve.wait_ge(s_ea, 1)
                sig(stt(quad(gcol, NT), quad(sp, NT), -1.0, ea2, ALU.mult, ALU.mult), "g_ready")
                w(layer, "g_ready", 0)
                sig(V.tensor_copy(hbeta, hbeta), "beta_ready")
                for g in range(CONV_GROUPS):
                    for s in range(1, CONV_K):
                        for ct in range(4):
                            n = 4 * g + ct
                            if s == 1 and ct % 2 == 0:
                                w(layer, "tap0", n + 1)
                            col = 32 + layer * 48 + (3 - s) * 12 + n
                            src = ps[2 * g + ct // 2][:, (ct % 2) * SEQ:(ct % 2 + 1) * SEQ - s]
                            ins = stt(qkvT[:, n, s:SEQ], src, par[:, col:col + 1], qkvT[:, n, s:SEQ],
                                      ALU.mult, ALU.add)
                        if s < CONV_K - 1:
                            link(ins)
                        else:
                            sig(ins, "conv_out")
                    w(layer, "th_conv", g)
                    grp = qkvT[:, 4 * g:4 * g + 4, :].rearrange("p a b -> p (a b)")
                    sig(stt(grp, th[:, :, :].rearrange("p a b -> p (a b)"), 1.0, grp, ALU.add, ALU.mult),
                        "qkv_act")
                    w(layer, "qkv_act", g)
                    if g < 2:
                        sig(tt(sq[:, g, :, :].rearrange("p a b -> p (a b)"), grp, grp, ALU.mult), "sq_ready")
                w(layer, "gc_ps", 0)
                link(V.tensor_copy(gcs, ps[6][:, 64:64 + TH]))
                link(tsc(ngc, gcs, -1.0, None, ALU.mult))
                for t in range(NT):
                    w(layer, "bc_ps", t)
                    for hh in range(H):
                        a = 4 * t + hh
                        last = tsc(decay[:, a, :], ps[t][:, hh * P:(hh + 1) * P], ngc[:, a:a + 1], 0.0,
                                   ALU.add, ALU.min)
                    if t == 0:
                        sig(tt(kdarg, quad(ps[0][:, :])[:, :, P - 1], gcs[:, 0:H], ALU.subtract), "kd_in")
                sig(last, "dec_arg")
                w(layer, "ssq_ps", 0)
                sig(tsc(rr0, ps[7][:, 32:48], 4 * EPS, None, ALU.add), "rr_in")
                for t in range(NT):
                    w(layer, "vtok_ps", t)
                    sig(tt(quad(bv[:, t, :]), quad(ps[4 + t][:, :]), over(hbeta[:, 4 * t:4 * t + 4], DH),
                           ALU.mult), "bv_ready")
                w(layer, "rr_ready", 0)
                w(layer, "dec_exp", 2)
                w(layer, "ktok_ps", 0)
                w(layer, "diagc_ready", 0)
                link(tt(kdfac, kdfac, rr[:, TH:TH + H], ALU.mult))
                sig(tt(kdec[:, :, :], quad(ps[7][:, :]), over(kdfac, DH), ALU.mult), "kdec_ready")
                link(tt(ceg, cneg[:, H:TH], eg, ALU.mult))
                link(tsc(rqs, rr[:, 0:TH], DH ** -0.5, None, ALU.mult))
                link(tt(rqsq, rqs, rqs, ALU.mult))
                w(layer, "decay_ready", 0)
                for t in range(NT):
                    w(layer, "bcc_ps", t)
                    sig(tt(quad(attnT[:, 4 * t:4 * t + 4, :].rearrange("p a b -> p (a b)")),
                           quad(ps[t][:, :]), decay[:, 4 * t:4 * t + 4, :], ALU.mult), "dec_beta")
                for t in range(NT):
                    w(layer, "kk_ps", t)
                    w(layer, "dec_beta", t)
                    for hh in range(H):
                        a = 4 * t + hh
                        last = stt(un[:, a, :], ps[2 + t][:, hh * P:(hh + 1) * P], rr[:, TH + a:TH + a + 1],
                                   attnT[:, a, :], ALU.mult, ALU.mult)
                    sig(last, "un_ready")
                w(layer, "un_ready", 1)
                for t in range(NT):
                    w(layer, "qk_ps", t)
                    for hh in range(H):
                        a = 4 * t + hh
                        last = stt(attnT[:, a, :], ps[4 + t][:, hh * P:(hh + 1) * P], rr[:, TH + a:TH + a + 1],
                                   decay[:, a, :], ALU.mult, ALU.mult)
                    sig(last, "attn_ready")
                w(layer, "umask_ready", 0)
                sig(tt(einv, umask[:, :, :], tiled(ident, TH), ALU.add), "e1_ready")
                fill = [(g, t) for g in range(len(FILL_GROUPS)) for t in range(NT)]

                def filler():
                    if not fill:
                        return
                    g, t = fill.pop(0)
                    if g == 2:
                        return
                    if g < 2:
                        if t == 0:
                            w(layer, "proj_first", g)
                        else:
                            dve.wait_ge(unit_used, base + 2 * CONV_GROUPS + 2 * g + 2)
                        rot = C_ROT + t * 256
                        v = ps[t][:, :].rearrange("p (h s n) -> p h s n", h=H, s=2)
                        tv = th[:, t, :].rearrange("p (h s n) -> p h s n", h=H, s=2)
                        dst = rrot[:, g, t, :]
                        for s in range(2):
                            last = tt(tv[:, :, s, :], v[:, :, 1 - s, :],
                                      tiled(cst[:, rot + 128 + 64 * s:rot + 192 + 64 * s], H), ALU.mult)
                        link(last)
                        link(tt(quad(dst), quad(ps[t][:, :]), tiled(cst[:, rot:rot + 128], H), ALU.mult))
                        sig(tt(dst, dst, th[:, t, :], ALU.add), "rope_done")
                    else:
                        n = 2 * (g - 3) + t
                        w(layer, "th_g", n)
                        dst, name = (rgs, "rg_done") if g == 3 else (gzs, "gz_half")
                        sig(stt(dst[:, t, :], th[:, t, :], 1.0, ps[t][:, :], ALU.add, ALU.mult), name)

                for lv in range(1, len(LEVELS)):
                    filler()
                    if lv == 1:
                        w(layer, "e1_ready", 0)
                    for t in range(NT):
                        n = 2 * (lv - 1) + t
                        w(layer, "de_ps", n)
                        if n >= 2:
                            w(layer, "de_ready", n - 2)
                        sl = slice(4 * t, 4 * t + 4)
                        if lv < len(LEVELS) - 1:
                            tt(dinv[:, sl, :], dinv[:, sl, :], quad(ps[4 + t][:, :]), ALU.add)
                        sig(tt(einv[:, sl, :], einv[:, sl, :], quad(ps[6 + t][:, :]), ALU.add), "de_ready")
                    filler()
                w(layer, "ks_ps", 0)
                for hh in range(H):
                    c = slice(hh * P, (hh + 1) * P)
                    last = stt(rhs1[:, c], ps[2][:, c], ceg[:, hh:hh + 1], bv[:, 1, c], ALU.mult, ALU.add)
                sig(last, "rhs1_ready")
                for n in range(2):
                    w(layer, "s_ps", n)
                    dec = cst[:, C_DEC + n * 512:C_DEC + (n + 1) * 512]
                    sig(tt(st0[:, 2 * n:2 * n + 2, :].rearrange("p a b -> p (a b)"), ps[n][:, :], dec, ALU.mult),
                        "s_ready")
                w(layer, "s_ps", 2)
                dec = cst[:, C_DEC:C_DEC + H * 256].rearrange("p (a b) -> p a b", a=H)[:, :, 0:P]
                sig(tt(st1[:, :, :], quad(ps[3][:, :]), dec, ALU.mult), "s_ready")
                w(layer, "qs_ps", 0)
                sig(tt(quad(qs_sb[:, :]), quad(ps[5][:, :]), over(eg, DH), ALU.mult), "qs_done")
                for t in range(NT):
                    w(layer, "ro_ps", t)
                    sig(V.tensor_copy(o_ret[:, t, :], ps[t][:, :]), "ro_sb")
                w(layer, "go_ps", 0)
                sig(V.tensor_copy(o_gdn[:, 0, :], ps[6][:, :]), "go_sb")
                w(layer, "go_ps", 1)
                w(layer, "qs_done", 0)
                sig(tt(o_gdn[:, 1, :], ps[7][:, :], qs_sb[:, :], ALU.add), "go_sb")
                w(layer, "ro_sb", 1)
                w(layer, "go_sb", 1)
                sqv = st0[:, :, :].rearrange("p a b -> p (a b)")
                for r, src in enumerate((o_ret, o_gdn)):
                    flat = src.rearrange("p t n -> p (t n)")
                    link(tt(sqv, flat, flat, ALU.mult))
                    link(V.tensor_reduce(oss[:, r * TH:(r + 1) * TH], quad(sqv, TH), AX.X, ALU.add))
                link(tt(oss[:, TH:2 * TH], oss[:, TH:2 * TH], rqsq, ALU.mult))
                sig(tsc(oss, oss, 1.0 / DH, EPS, ALU.mult, ALU.add), "rms_in")
                w(layer, "rms_ready", 0)
                link(tt(ors[:, TH:2 * TH], ors[:, TH:2 * TH], rqs, ALU.mult))
                link(tsc(ors, ors, 0.5, None, ALU.mult))
                w(layer, "gz_done", 1)
                w(layer, "gz_half", 1)
                for r, (src, gate) in enumerate(((o_ret, rgs), (o_gdn, gzs))):
                    v = src.rearrange("p t n -> p (t n)")
                    link(tt(quad(v, TH), quad(v, TH), over(ors[:, r * TH:(r + 1) * TH], DH), ALU.mult))
                    sig(tt(v, v, gate[:, :, :].rearrange("p t n -> p (t n)"), ALU.mult), "br_ready")
                dve.wait_ge(unit_used, base + MIX_UNITS - 6)
                w(layer, "gate_done", 7)
                for t in range(NT):
                    for f in range(2):
                        g = gates[:, t, f * 512:(f + 1) * 512]
                        last = stt(g, g, 1.0, ps[2 * t + f][:, :], ALU.add, ALU.mult)
                sig(last, "ya_use")
                dve.wait_ge(unit_used, base + MIX_UNITS - 4)
                for t in range(NT):
                    for f in range(2):
                        g = gates[:, t, DM + f * 512:DM + (f + 1) * 512]
                        last = stt(g, g, 1.0, ps[4 + 2 * t + f][:, :], ALU.add, ALU.mult)
                link(last)
                w(layer, "ya_use", 0)
                for t in range(NT):
                    sig(tt(hs[:, t, :], gates[:, t, 0:DM], gates[:, t, DM:2 * DM], ALU.add), "m_ready")
                dve.wait_ge(unit_used, base + MIX_UNITS)
                for t in range(NT):
                    for f in range(2):
                        c = slice(f * 512, (f + 1) * 512)
                        sig(stt(h[:, t, c], ps[4 + 2 * t + f][:, :], 0.5, h[:, t, c], ALU.mult, ALU.add), "h_upd")
                w(layer, "h_upd", 3)

            def ffn_pass(base, first, it, off, e):
                order = pass_order()
                for c in range(NCHUNK):
                    b = c % 2
                    dve.wait_ge(ffn_th, it * NCHUNK + c + 1)
                    stt(a1[:, b, :], th[:, b, :], 1.0, ps[2 * b][:, :], ALU.add, ALU.mult).then_inc(ffn_a1, 1)
                    dve.wait_ge(ffn_a1, it * NCHUNK + c + 1)
                    dve.wait_ge(unit_used, off + base + order.index(("up", c)) + 1)
                    if c >= 2:
                        dve.wait_ge(unit_used, off + base + order.index(("down", c - 2)) + 1)
                    stt(act_sb[:, b, :, :].rearrange("p j n -> p (j n)"), a1[:, b, :], 0.5, ps[2 * b + 1][:, :],
                        ALU.mult, ALU.mult).then_inc(ffn_act, 1)
                if e is not None:
                    V.tensor_copy(gcur.unsqueeze(2), quad(gw, NT)[:, :, bass.ds(e, 1)]).then_inc(gcur_ready, 1)
                    dve.wait_ge(gcur_ready, e + 1)
                dve.wait_ge(unit_used, off + base + PASS_UNITS)
                for t in range(NT):
                    for f in range(2):
                        c = slice(f * 512, (f + 1) * 512)
                        src = ps[4 + 2 * t + f][:, :]
                        if e is None:
                            ins = tt(h[:, t, c], h[:, t, c], src, ALU.add)
                        else:
                            ins = stt(h[:, t, c], src, gcur[:, t:t + 1], h[:, t, c], ALU.mult, ALU.add)
                        ins.then_inc(ffn_drained, 1)
                dve.wait_ge(ffn_drained, it * 4 + 4)

            dve.wait_ge(s_par_ps, 1)
            V.tensor_copy(par[:, :], ps[7][:, 0:P]).then_inc(s_par, 1)
            dve.wait_ge(s_par, 1)
            mixer(0, 0)
            norm(0, 1)
            ffn_pass(MIX_UNITS, True, 0, 0, None)
            mixer(1, LAYER0_UNITS)
            norm(1, 1)
            dve.wait_ge(router_ps, 1)
            link(V.tensor_copy(logit, ps[0][:, 0:16]))
            for t in range(NT):
                lg = logit[:, t * NEXP:(t + 1) * NEXP]
                a, b = over(lg, NEXP), tiled(lg, NEXP)
                g1, g2 = quad(cmp1[:, t, :], NEXP), quad(cmp2[:, t, :], NEXP)
                tt(g1, b, a, ALU.is_gt)
                link(tt(g2, b, a, ALU.is_equal))
                link(tt(g2, g2, quad(cst[:, C_LOW:C_LOW + 64], NEXP), ALU.mult))
                link(tt(g1, g1, g2, ALU.add))
                link(V.tensor_reduce(rank[:, t * NEXP:(t + 1) * NEXP], g1, AX.X, ALU.add))
                link(V.max(top[:, t * 8:(t + 1) * 8], lg))
            tv = quad(top, NT)
            tt(p0, tv[:, :, 1], tv[:, :, 0], ALU.subtract).then_inc(router_in, 1)
            dve.wait_ge(router_e, 1)
            link(tsc(p0, pd, 1.0, None, ALU.add))
            link(V.reciprocal(p0, p0))
            link(tt(p1, pd, p0, ALU.mult))
            link(tsc(sel, rank, 0.0, None, ALU.is_equal))
            link(tt(quad(gw, NT), quad(sel, NT), over(p0, NEXP), ALU.mult))
            link(tsc(sel, rank, 1.0, None, ALU.is_equal))
            link(tt(quad(sel, NT), quad(sel, NT), over(p1, NEXP), ALU.mult))
            link(tt(gw, gw, sel, ALU.add))
            with dve.Fori(0, NEXP) as e:
                ffn_pass(STATIC_UNITS, False, e + 1, e * PASS_UNITS, e)
            sumsq(s_fin_ss)
            dve.wait_ge(s_fnorm, 16)
            dve.wait_ge(s_fin_rs, 1)
            for t in range(NT):
                stt(hs[:, t, :], h[:, t, :], rs[:, t:t + 1], fnorm, ALU.mult, ALU.mult).then_inc(s_final, 1)


_INS = ['x', 'norm_mix', 'w_in', 'conv_w', 'a_log', 'dt_bias', 'gdn_norm', 'w_branch', 'w_out', 'norm_ffn',
        'dense_w_gate', 'dense_w_up', 'dense_w_down', 'router', 'moe_w_gate', 'moe_w_up', 'moe_w_down', 'final_norm']


def kernel(**inputs):
    import concourse.bacc as _bacc
    from concourse.bass_utils import run_bass_kernel_spmd as _run

    nc = _bacc.Bacc("TRN2", target_bir_lowering=False, num_devices=1)
    arrays, args = {}, []
    for name in _INS + ['shape_constants']:
        a = shape_constants() if name == 'shape_constants' else np.ascontiguousarray(inputs[name])
        arrays[f"in_{name}_dram"] = a
        args.append(nc.dram_tensor(f"in_{name}_dram", a.shape, mybir.dt.from_np(a.dtype), kind="ExternalInput").ap())
    o = nc.dram_tensor("out_0_dram", (1, SEQ, DM), mybir.dt.float32, kind="ExternalOutput").ap()
    build(nc, *args, o)
    r = _run(nc, [arrays], core_ids=[0])
    return r.results[0]["out_0_dram"]
```

```python
import math
from contextlib import ExitStack

import numpy as np
import concourse.bass as bass
from concourse import mybir

DM = 1024
SEQ = 256
DEPTH = 2
H = 4
DH = 128
CONV_K = 4
DFF = 2816
NEXP = 8
EPS = 1e-6
IN_COLS = 6152
P = 128
NT = SEQ // P
KD = DM // P
TH = NT * H

COL_RQ, COL_RK, COL_RV, COL_RG, COL_CONV, COL_GZ, COL_AB, COL_GATE = 0, 512, 1024, 1536, 2048, 3584, 4096, 4104

UNIT = 2048
SLOTS = 11
FF_CHUNK = 256
NCHUNK = DFF // FF_CHUNK
PASS_UNITS = 3 * NCHUNK
assert PASS_UNITS % SLOTS == 0
CONV_GROUPS = 3
FILL_GROUPS = [COL_RQ, COL_RK, COL_RV, COL_RG, COL_GZ]
GATE_GROUPS = 4
MIX_UNITS = 2 * (CONV_GROUPS + len(FILL_GROUPS) + GATE_GROUPS) + 4 + 4
LAYER0_UNITS = MIX_UNITS + PASS_UNITS
STATIC_UNITS = LAYER0_UNITS + MIX_UNITS

LEVELS = [1, 2, 4, 8, 16, 32, 64]
C_ID, C_ONE, C_TRI, C_MASK = 0, 128, 256, 384
C_ROT = C_MASK + 128 * len(LEVELS)
C_DEC = C_ROT + NT * 256
C_LOW = C_DEC + H * 256
C_IOTA = C_LOW + NEXP * NEXP
C_COLS = C_IOTA + P

ROUNDS = 2
NGATHER = NEXP + 1


def shape_constants():
    c = np.zeros((P, C_COLS), np.float32)
    j = np.arange(P)[:, None]
    i = np.arange(P)[None, :]
    c[:, C_ID:C_ID + P] = (i == j)
    c[:, C_ONE:C_ONE + P] = 1.0
    c[:, C_TRI:C_TRI + P] = (j <= i)
    for n, b in enumerate(LEVELS):
        same = (i // (2 * b)) == (j // (2 * b))
        c[:, C_MASK + n * P:C_MASK + (n + 1) * P] = same & (i // b > j // b)
    inv_freq = np.float32(10000.0) ** (-np.arange(0, DH, 2, dtype=np.float32) / np.float32(DH))
    ang = np.arange(SEQ, dtype=np.float32)[:, None] * inv_freq[None, :].astype(np.float32)
    cos, sin = np.cos(ang), np.sin(ang)
    for t in range(NT):
        o = C_ROT + t * 256
        rows = slice(t * P, (t + 1) * P)
        c[:, o:o + 64] = cos[rows]
        c[:, o + 64:o + 128] = cos[rows]
        c[:, o + 128:o + 192] = -sin[rows]
        c[:, o + 192:o + 256] = sin[rows]
    i2 = np.arange(2 * P)[None, :]
    for h in range(H):
        lg = math.log(1.0 - 2.0 ** (-5.0 - h))
        c[:, C_DEC + h * 256:C_DEC + (h + 1) * 256] = np.where(
            i2 >= j, np.exp(np.maximum(i2 - j, 0) * lg) * DH ** -0.5, 0.0)
    e = np.arange(NEXP)
    c[:, C_LOW:C_LOW + NEXP * NEXP] = (e[None, :] < e[:, None]).reshape(1, -1)
    c[:, C_IOTA:C_IOTA + P] = i
    return c


def build(nc, x, norm_mix, w_in, conv_w, a_log, dt_bias, gdn_norm, w_branch, w_out, norm_ffn,
          dense_w_gate, dense_w_up, dense_w_down, router, moe_w_gate, moe_w_up, moe_w_down,
          final_norm, consts, out):
    f32 = mybir.dt.float32
    ALU = mybir.AluOpType
    ACT = mybir.ActivationFunctionType
    AX = mybir.AxisListType

    ctx = ExitStack()
    with ctx:
        def sb(name, *shape):
            return ctx.enter_context(nc.sbuf_tensor(name, [P, *shape], f32))

        def sem(name):
            return ctx.enter_context(nc.semaphore(name))

        ring = sb("ring", SLOTS, UNIT)
        h = sb("h", NT, DM)
        hs = sb("hs", NT, DM)
        hnT = sb("hnT", KD, SEQ)
        cst = sb("cst", C_COLS)
        rows = sb("rows", P)
        par = sb("par", P)
        wab = sb("wab", DEPTH, KD, 8)
        wrt = sb("wrt", KD, NEXP)
        alog = sb("alog", DEPTH * H)
        dtb = sb("dtb", DEPTH * H)
        gnorm = sb("gnorm", DEPTH, DH)
        qkvT = sb("qkvT", 12, SEQ)
        th = sb("th", 2, 512)
        sq = sb("sq", 2, H, SEQ)
        work = sb("work", 4, TH * P)
        attnT = sb("attnT", TH, P)
        prod = qkvT[:, 8:12, :].rearrange("p a b -> p (a b)").rearrange("p (a b) -> p a b", b=P)
        umask = sb("umask", TH, P)
        rT = sb("rT", 2, H, SEQ)
        rv = sb("rv", NT, H * DH)
        rgs = sb("rgs", NT, H * DH)
        gzs = sb("gzs", NT, H * DH)
        st0 = umask[:, :, :].rearrange("p a b -> p (a b)").rearrange("p (h n) -> p h n", h=H)
        st1 = sb("st1", H, P)
        bv = sb("bv", NT, H * DH)
        kdec = sb("kdec", H, DH)
        sm = sb("sm", 640)
        decay, un, dinv, einv = (work[:, n, :].rearrange("p (a b) -> p a b", b=P) for n in range(4))
        vnew = work[:, 2, :].rearrange("p (t n) -> p t n", t=NT)
        fnorm = work[:, 0, :]
        gates = work[:, :, :].rearrange("p a n -> p (a n)").rearrange("p (t n) -> p t n", t=NT)
        rrot = hs[:, :, :].rearrange("p a (b n) -> p a b n", b=NT)
        o_ret = sq[:, 0, :, :].rearrange("p a b -> p (a b)").rearrange("p (t n) -> p t n", t=NT)
        o_gdn = sq[:, 1, :, :].rearrange("p a b -> p (a b)").rearrange("p (t n) -> p t n", t=NT)
        state = sb("state", H, DH)
        over_i = ctx.enter_context(nc.sbuf_tensor("over_i", [P, 1], mybir.dt.int32))
        rhs1 = prod[:, 0:4, :].rearrange("p a b -> p (a b)")
        qs_sb = prod[:, 4:8, :].rearrange("p a b -> p (a b)")
        a1 = rT[:, :, :, :].rearrange("p a b c -> p (a b c)").rearrange("p (a n) -> p a n", n=512)
        act_sb = a1[:, 2:4, :].rearrange("p a (j n) -> p a j n", j=2)

        xgT = attnT
        gsel = bv[:, 0, 0:NT * P].rearrange("p (t n) -> p t n", t=NT)
        gselT = bv[:, 1, 0:NT * P].rearrange("p (t n) -> p t n", t=NT)
        a_tok = rgs[:, 0, :].rearrange("p (b n) -> p b n", b=2)
        actT = gzs[:, :, 0:2 * P].rearrange("p b (j n) -> p b j n", j=2)
        y_sb = rv[:, :, :].rearrange("p a n -> p (a n)")

        ident = cst[:, C_ID:C_ID + P]
        ones = cst[:, C_ONE:C_ONE + P]
        tri = cst[:, C_TRI:C_TRI + P]

        at = [0]

        def small(n):
            at[0] += n
            assert at[0] <= 640
            return sm[:, at[0] - n:at[0]]

        ss, rs = small(NT), small(NT)
        mhalf = small(16)
        gx, nx, e1, den, s1, s2, poly, sp = (small(TH) for _ in range(8))
        ea = small(DEPTH * H)
        tb, beta, gcol, gcs, ngc, cneg, hbeta = (small(TH) for _ in range(7))
        rr0, rr = small(2 * TH), small(2 * TH)
        kdarg, kdfac, eg, ceg = (small(H) for _ in range(4))
        rqs = small(TH)
        oss, ors = small(2 * TH), small(2 * TH)
        rqsq = small(TH)
        logit, rank, sel = small(NT * NEXP), small(NT * NEXP), small(NT * NEXP)
        gw = small(NT * NEXP)
        top = small(NT * 8)
        pd, p0, p1 = small(NT), small(NT), small(NT)
        gcur = small(NT)
        posm = sm[:, at[0]:at[0] + NT * NGATHER]
        at[0] += NT * NGATHER
        selm, pcur, cntm, over_f = small(NT * NEXP), small(NT), small(1), small(1)
        cmp1 = prod[:, 0, :].rearrange("p (t n) -> p t n", t=NT)
        cmp2 = prod[:, 1, :].rearrange("p (t n) -> p t n", t=NT)

        ps = [ctx.enter_context(nc.psum_tensor(f"ps{n}", [P, 512], f32)) for n in range(8)]

        def quad(ap, n=4):
            return ap.rearrange("p (a b) -> p a b", a=n)

        def over(ap, n):
            return ap.unsqueeze(2).to_broadcast([P, ap.shape[1], n])

        def tiled(ap, n):
            return ap.unsqueeze(1).to_broadcast([P, n, ap.shape[1]])

        PER_LAYER = dict(
            sumsq=2, rstd=2, hs_ready=4, hT_ps=8, hnT_ready=8,
            ab_ps=1, gat_in=1, gat_e=1, g_ready=1, beta_ready=1, trig_ready=1, diagc_ready=1,
            gc_ps=1, bc_ps=2, bcc_ps=2, dec_arg=1, kd_in=1, dec_exp=3, decay_ready=1,
            tap0=12, conv_out=3, th_conv=3, qkv_act=3, sq_ready=2, ssq_ps=1, rr_in=1, rr_ready=1,
            vtok_ps=2, ktok_ps=1, bv_ready=2, kdec_ready=1, dec_beta=2,
            kk_ps=2, qk_ps=2, un_ready=2, attn_ready=2, umask_ready=7, e1_ready=1, d1_ps=2, d1_ready=2,
            p_ps=12, p_ready=12, de_ps=12, de_ready=12,
            proj_first=9, rope_done=4, rv_done=2, th_g=4, rg_done=2, gz_half=2, gz_done=2, gate_done=8,
            vn_ps=2, vn_ready=2, st_ps=1, st_ready=1, ks_ps=1, rhs1_ready=1, qs_ps=1,
            rqT_ps=1, rkT_ps=1, rqT_ready=1, rkT_ready=1, s_ps=3, s_ready=3,
            ro_ps=2, go_ps=2, ro_sb=2, go_sb=2, rms_in=1, rms_ready=1, br_ready=2, rt_ps=2, rt_ready=2,
            ya_use=1, m_ready=2, mT_ps=4, mT_ready=4, h_upd=4,
            rope_ps=4, qs_done=1)
        S = {name: sem("s_" + name) for name in PER_LAYER}
        N_CONST = 11
        s_const = sem("s_const")
        s_fnorm = sem("s_fnorm")
        s_zero = sem("s_zero")
        s_par_ps = sem("s_par_ps")
        s_par = sem("s_par")
        s_ea = sem("s_ea")
        unit_used = sem("unit_used")
        loaded = [sem(f"loaded{n}") for n in range(SLOTS)]
        dve_chain = sem("dve_chain")
        pool_chain = sem("pool_chain")
        ffn_th = sem("ffn_th")
        ffn_a1 = sem("ffn_a1")
        ffn_act = sem("ffn_act")
        ffn_drained = sem("ffn_drained")
        gcur_ready = sem("gcur_ready")
        pcur_ready = sem("pcur_ready")
        sel_ready = sem("sel_ready")
        pos_ps = sem("pos_ps")
        over_ready = sem("over_ready")
        g_built = sem("g_built")
        xg_ps = sem("xg_ps")
        gt_ps = sem("gt_ps")
        xg_ready = sem("xg_ready")
        gt_ready = sem("gt_ready")
        aT_ps = sem("aT_ps")
        aT_ready = sem("aT_ready")
        y_ready = sem("y_ready")
        sc_ps = sem("sc_ps")
        moe_drained = sem("moe_drained")
        router_ps = sem("router_ps")
        router_e = sem("router_e")
        router_in = sem("router_in")
        s_fin_ss = sem("s_fin_ss")
        s_fin_rs = sem("s_fin_rs")
        s_final = sem("s_final")
        s_out = sem("s_out")

        def upto(layer, name, k):
            assert 0 <= k < PER_LAYER[name], (name, k)
            return layer * PER_LAYER[name] + k + 1

        def unit(i):
            return ring[:, i % SLOTS, :]

        def block_of(i):
            return unit(i).rearrange("p (k n) -> p k n", k=4)

        def w_in_units(layer, col):
            v = w_in[layer, :, col:col + 512].rearrange("(k p) n -> p k n", p=P)
            return [v[:, 0:4, :], v[:, 4:8, :]]

        def mixer_units(layer):
            u = []
            for g in range(CONV_GROUPS):
                u += w_in_units(layer, COL_CONV + 512 * g)
            for col in FILL_GROUPS:
                u += w_in_units(layer, col)
            for g in range(GATE_GROUPS):
                u += w_in_units(layer, COL_GATE + 512 * g)
            for r in range(2):
                v = w_branch[layer, r, :, :].rearrange("(k p) n -> p k n", p=P)
                u += [v[:, 0:2, :], v[:, 2:4, :]]
            v = w_out[layer, :, :].rearrange("(k p) n -> p k n", p=P)
            u += [v[:, 2 * n:2 * n + 2, :] for n in range(4)]
            assert len(u) == MIX_UNITS
            return u

        def pass_order():
            o = []
            for c in range(NCHUNK):
                o += [("gate", c), ("up", c)]
                if c:
                    o.append(("down", c - 1))
            return o + [("down", NCHUNK - 1)]

        def pass_unit(wg, wu, wd, kind, c):
            cols = slice(c * FF_CHUNK, (c + 1) * FF_CHUNK)
            if kind == "down":
                return wd(cols).rearrange("(j p) n -> p j n", p=P)
            return (wg if kind == "gate" else wu)(cols).rearrange("(k p) n -> p k n", p=P)

        block = ctx.enter_context(nc.Block())

        @block.sync
        def _(sp):
            for dst, src in [
                    (h[:, :, :], x[0, :, :].rearrange("(t p) n -> p t n", p=P)),
                    (cst[:, :], consts),
                    (rows[0:16, :], norm_mix.rearrange("l (k p) -> (l k) p", p=P)),
                    (rows[16:32, :], norm_ffn.rearrange("l (k p) -> (l k) p", p=P)),
                    (rows[32:128, :], conv_w.rearrange("l t (k p) -> (l t k) p", p=P)),
                    (wab[:, 0, :, :], w_in[0, :, COL_AB:COL_AB + 8].rearrange("(k p) n -> p k n", p=P)),
                    (wab[:, 1, :, :], w_in[1, :, COL_AB:COL_AB + 8].rearrange("(k p) n -> p k n", p=P)),
                    (wrt[:, :, :], router[0, :, :].rearrange("(k p) n -> p k n", p=P)),
                    (alog[:, :], a_log.rearrange("(o l) n -> o (l n)", o=1).to_broadcast([P, DEPTH * H])),
                    (dtb[:, :], dt_bias.rearrange("(o l) n -> o (l n)", o=1).to_broadcast([P, DEPTH * H])),
                    (gnorm[:, :, :].rearrange("p l n -> p (l n)"),
                     gdn_norm.rearrange("(o l) n -> o (l n)", o=1).to_broadcast([P, DEPTH * DH]))]:

                sp.dma_start(dst, src).then_inc(s_const, 16)

            def load(i, src):
                if i >= SLOTS:
                    sp.wait_ge(unit_used, i - SLOTS + 1)
                shape = unit(i).rearrange("p (k n) -> p k n", k=src.shape[1])
                sp.dma_start(shape, src).then_inc(loaded[i % SLOTS], 16)

            i = 0
            for layer in range(DEPTH):
                for src in mixer_units(layer):
                    load(i, src)
                    i += 1
                if layer == 0:
                    for kind, c in pass_order():
                        load(i, pass_unit(lambda s: dense_w_gate[0, :, s], lambda s: dense_w_up[0, :, s],
                                          lambda s: dense_w_down[0, s, :], kind, c))
                        i += 1
            assert i == STATIC_UNITS

            def expert_round(rnd):
                with sp.Fori(0, NEXP) as e:
                    for j, (kind, c) in enumerate(pass_order()):
                        i = STATIC_UNITS + rnd * NEXP * PASS_UNITS + j
                        src = pass_unit(lambda s: moe_w_gate[0, e, :, s], lambda s: moe_w_up[0, e, :, s],
                                        lambda s: moe_w_down[0, e, s, :], kind, c)
                        sp.wait_ge(unit_used, e * PASS_UNITS + (i - SLOTS + 1))
                        shape = unit(i).rearrange("p (k n) -> p k n", k=src.shape[1])
                        sp.dma_start(shape, src).then_inc(loaded[i % SLOTS], 16)

            expert_round(0)
            sp.wait_ge(over_ready, 1)
            with sp.If(sp.value_load(over_i[0:1, 0:1], min_val=0, max_val=1)):
                expert_round(1)

            for t in range(NT):
                sp.wait_ge(s_final, t + 1)
                sp.dma_start(out[0, t * P:(t + 1) * P, :], hs[:, t, :]).then_inc(s_out, 16)
            sp.wait_ge(s_out, 16 * NT)

        @block.tensor
        def _(pe):
            mm = nc.tensor.matmul
            used = [0]

            def arrived(i):
                pe.wait_ge(loaded[i % SLOTS], 16 * (i // SLOTS + 1))

            def w(layer, name, k):
                pe.wait_ge(S[name], upto(layer, name, k))

            def norm_transposes(layer, n):
                w(layer, "hs_ready", 2 * n + 1)
                for m in range(4):
                    for k in (2 * m, 2 * m + 1):
                        for t in range(NT):
                            last = nc.tensor.transpose(ps[m][:, (k % 2) * SEQ + t * P:(k % 2) * SEQ + (t + 1) * P],
                                                       hs[:, t, k * P:(k + 1) * P], ident)
                    last.then_inc(S["hT_ps"], 1)

            def proj_block(layer, i, t, bank):
                if t == 0:
                    arrived(i)
                    arrived(i + 1)
                for k in range(KD):
                    m = mm(ps[bank][:, :], hnT[:, k, t * P:(t + 1) * P], block_of(i + k // 4)[:, k % 4, :],
                           start=(k == 0), stop=(k == KD - 1))
                    if t == 1 and k in (3, 7):
                        m.then_inc(unit_used, 1)
                    elif k == KD - 1:
                        m.then_inc(S["proj_first"], 1)

            def mixer(layer, base):
                norm_transposes(layer, 0)
                w(layer, "hnT_ready", 3)
                for t in range(NT):
                    for k in range(KD):
                        last = mm(ps[6][:, 8 * t:8 * t + 8], hnT[:, k, t * P:(t + 1) * P], wab[:, layer, k, :],
                                  start=(k == 0), stop=(k == KD - 1))
                last.then_inc(S["ab_ps"], 1)
                for g in range(CONV_GROUPS):
                    i = base + 2 * g
                    arrived(i)
                    arrived(i + 1)
                    for ct in range(4):
                        for k in range(KD):
                            m = mm(ps[2 * g + ct // 2][:, (ct % 2) * SEQ:(ct % 2 + 1) * SEQ],
                                   block_of(i + k // 4)[:, k % 4, ct * P:(ct + 1) * P], hnT[:, k, :],
                                   start=(k == 0), stop=(k == KD - 1))
                            if ct == 3 and k in (3, 7):
                                m.then_inc(unit_used, 1)
                w(layer, "g_ready", 0)
                mm(ps[6][:, 64:64 + TH], tri, gcol, start=True, stop=True).then_inc(S["gc_ps"], 1)
                w(layer, "trig_ready", 0)
                w(layer, "conv_out", 0)
                for t in range(NT):
                    mm(ps[t][:, :], ones, einv[:, 4 * t:4 * t + 4, :].rearrange("p a b -> p (a b)"),
                       start=True, stop=True).then_inc(S["bc_ps"], 1)
                w(layer, "sq_ready", 1)
                for g in range(2):
                    for t in range(NT):
                        for hh in range(H):
                            c = 32 + g * TH + t * H + hh
                            last = mm(ps[7][:, c:c + 1], sq[:, g, hh, t * P:(t + 1) * P], ones[:, 0:1],
                                      start=True, stop=True)
                last.then_inc(S["ssq_ps"], 1)
                w(layer, "conv_out", 1)
                for t in range(NT):
                    for hh in range(H):
                        kt = qkvT[:, 4 + hh, t * P:(t + 1) * P]
                        last = mm(ps[2 + t][:, hh * P:(hh + 1) * P], kt, kt, start=True, stop=True)
                    last.then_inc(S["kk_ps"], 1)
                w(layer, "qkv_act", 2)
                for t in range(NT):
                    for hh in range(H):
                        last = nc.tensor.transpose(ps[4 + t][:, hh * P:(hh + 1) * P],
                                                   qkvT[:, 8 + hh, t * P:(t + 1) * P], ident)
                    last.then_inc(S["vtok_ps"], 1)
                w(layer, "rr_in", 0)
                for hh in range(H):
                    last = nc.tensor.transpose(ps[7][:, hh * P:(hh + 1) * P], qkvT[:, 4 + hh, 0:P], ident)
                last.then_inc(S["ktok_ps"], 1)
                w(layer, "diagc_ready", 0)
                w(layer, "dec_arg", 0)
                for t in range(NT):
                    mm(ps[t][:, :], ones, umask[:, 4 * t:4 * t + 4, :].rearrange("p a b -> p (a b)"),
                       start=True, stop=True).then_inc(S["bcc_ps"], 1)
                w(layer, "bv_ready", 1)
                for t in range(NT):
                    for hh in range(H):
                        last = mm(ps[4 + t][:, hh * P:(hh + 1) * P], qkvT[:, 4 + hh, t * P:(t + 1) * P],
                                  qkvT[:, hh, t * P:(t + 1) * P], start=True, stop=True)
                    last.then_inc(S["qk_ps"], 1)
                w(layer, "e1_ready", 0)
                w(layer, "un_ready", 1)
                for t in range(NT):
                    for hh in range(H):
                        last = nc.tensor.transpose(ps[2 + t][:, hh * P:(hh + 1) * P], einv[:, 4 * t + hh, :], ident)
                    last.then_inc(S["d1_ps"], 1)
                fill = [(g, t) for g in range(len(FILL_GROUPS)) for t in range(NT)]
                fill_base = base + 2 * CONV_GROUPS
                free = {0: "rope_done", 1: "rope_done", 2: "rv_done", 3: "rg_done"}

                def filler():
                    if not fill:
                        return
                    g, t = fill.pop(0)
                    if g == 0:
                        w(layer, "un_ready", 1)
                    else:
                        name = free[g - 1]
                        w(layer, name, (2 * (g - 1) if name == "rope_done" else 0) + t)
                    proj_block(layer, fill_base + 2 * g, t, t)

                for lv in range(1, len(LEVELS)):
                    n = 2 * (lv - 1)
                    w(layer, "umask_ready", lv)
                    for t in range(NT):
                        if lv == 1:
                            w(layer, "d1_ready", t)
                        else:
                            w(layer, "de_ready", n - 2 + t)
                        for hh in range(H):
                            a = 4 * t + hh
                            last = mm(ps[2 + t][:, hh * P:(hh + 1) * P], umask[:, a, :], dinv[:, a, :],
                                      start=True, stop=True)
                        last.then_inc(S["p_ps"], 1)
                    filler()
                    for t in range(NT):
                        w(layer, "p_ready", n + t)
                        if lv == 1:
                            w(layer, "attn_ready", t)
                            w(layer, "kdec_ready", 0)
                        if lv < len(LEVELS) - 1:
                            for hh in range(H):
                                a = 4 * t + hh
                                mm(ps[4 + t][:, hh * P:(hh + 1) * P], einv[:, a, :], prod[:, a, :],
                                   start=True, stop=True)
                        for hh in range(H):
                            a = 4 * t + hh
                            last = mm(ps[6 + t][:, hh * P:(hh + 1) * P], prod[:, a, :], einv[:, a, :],
                                      start=True, stop=True)
                        last.then_inc(S["de_ps"], 1)
                    filler()
                assert not fill
                w(layer, "de_ready", 10)
                w(layer, "bv_ready", 1)
                for hh in range(H):
                    last = mm(ps[2][:, hh * P:(hh + 1) * P], einv[:, hh, :], bv[:, 0, hh * P:(hh + 1) * P],
                              start=True, stop=True)
                last.then_inc(S["vn_ps"], 1)
                w(layer, "rope_done", 3)
                w(layer, "gz_half", 1)
                for hh in range(H):
                    for t in range(NT):
                        last = nc.tensor.transpose(
                            ps[hh // 2][:, (hh % 2) * SEQ + t * P:(hh % 2) * SEQ + (t + 1) * P],
                            rrot[:, 0, t, hh * P:(hh + 1) * P], ident)
                last.then_inc(S["rqT_ps"], 1)
                w(layer, "vn_ready", 0)
                w(layer, "kdec_ready", 0)
                for hh in range(H):
                    last = mm(ps[3][:, hh * P:(hh + 1) * P], kdec[:, hh, :], vnew[:, 0, hh * P:(hh + 1) * P],
                              start=True, stop=True)
                last.then_inc(S["st_ps"], 1)
                for hh in range(H):
                    for t in range(NT):
                        last = nc.tensor.transpose(
                            ps[4 + hh // 2][:, (hh % 2) * SEQ + t * P:(hh % 2) * SEQ + (t + 1) * P],
                            rrot[:, 1, t, hh * P:(hh + 1) * P], ident)
                last.then_inc(S["rkT_ps"], 1)
                w(layer, "st_ready", 0)
                for hh in range(H):
                    last = mm(ps[2][:, hh * P:(hh + 1) * P], qkvT[:, 4 + hh, P:SEQ], state[:, hh, :],
                              start=True, stop=True)
                last.then_inc(S["ks_ps"], 1)
                w(layer, "rqT_ready", 0)
                w(layer, "rkT_ready", 0)
                for hh in range(H):
                    last = mm(ps[hh // 2][:, (hh % 2) * SEQ:(hh % 2 + 1) * SEQ], rT[:, 1, hh, 0:P], rT[:, 0, hh, :],
                              start=True, stop=True)
                    if hh % 2:
                        last.then_inc(S["s_ps"], 1)
                for hh in range(H):
                    last = mm(ps[3][:, hh * P:(hh + 1) * P], rT[:, 1, hh, P:SEQ], rT[:, 0, hh, P:SEQ],
                              start=True, stop=True)
                last.then_inc(S["s_ps"], 1)
                for hh in range(H):
                    last = mm(ps[5][:, hh * P:(hh + 1) * P], qkvT[:, hh, P:SEQ], state[:, hh, :],
                              start=True, stop=True)
                last.then_inc(S["qs_ps"], 1)
                w(layer, "rhs1_ready", 0)
                w(layer, "de_ready", 11)
                for hh in range(H):
                    last = mm(ps[4][:, hh * P:(hh + 1) * P], einv[:, 4 + hh, :], rhs1[:, hh * P:(hh + 1) * P],
                              start=True, stop=True)
                last.then_inc(S["vn_ps"], 1)
                w(layer, "s_ready", 2)
                w(layer, "rv_done", 1)
                for t in range(NT):
                    for hh in range(H):
                        c = slice(hh * P, (hh + 1) * P)
                        last = mm(ps[t][:, c], st0[:, hh, t * P:(t + 1) * P], rv[:, 0, c],
                                  start=True, stop=(t == 0))
                        if t == 1:
                            last = mm(ps[t][:, c], st1[:, hh, :], rv[:, 1, c], start=False, stop=True)
                    last.then_inc(S["ro_ps"], 1)
                for t in range(NT):
                    w(layer, "vn_ready", t)
                    for hh in range(H):
                        c = slice(hh * P, (hh + 1) * P)
                        last = mm(ps[6 + t][:, c], attnT[:, 4 * t + hh, :], vnew[:, t, c], start=True, stop=True)
                    last.then_inc(S["go_ps"], 1)
                i = fill_base + 2 * len(FILL_GROUPS)
                w(layer, "rhs1_ready", 0)
                for g in range(GATE_GROUPS):
                    for t in range(NT):
                        if g:
                            w(layer, "gate_done", 2 * (g - 1) + t)
                        proj_block(layer, i + 2 * g, t, 2 + t)
                w(layer, "qs_done", 0)
                for r, src in enumerate((o_ret, o_gdn)):
                    w(layer, "br_ready", r)
                    for hh in range(H):
                        for t in range(NT):
                            last = nc.tensor.transpose(
                                ps[4 + 2 * r + hh // 2][:, (hh % 2) * SEQ + t * P:(hh % 2) * SEQ + (t + 1) * P],
                                src[:, t, hh * P:(hh + 1) * P], ident)
                    last.then_inc(S["rt_ps"], 1)
                i += 2 * GATE_GROUPS
                w(layer, "gate_done", 7)
                for r in range(2):
                    w(layer, "rt_ready", r)
                    if r:
                        w(layer, "rt_ready", 1)
                    for n in range(2):
                        arrived(i)
                        v = unit(i).rearrange("p (k n) -> p k n", k=2)
                        for k in (2 * n, 2 * n + 1):
                            for t in range(NT):
                                for f in range(2):
                                    last = mm(ps[4 * r + 2 * t + f][:, :], rT[:, r, k, t * P:(t + 1) * P],
                                              v[:, k % 2, f * 512:(f + 1) * 512], start=(k == 0), stop=(k == 3))
                        last.then_inc(unit_used, 1)
                        i += 1
                w(layer, "m_ready", 1)
                for m in range(4):
                    for k in (2 * m, 2 * m + 1):
                        for t in range(NT):
                            last = nc.tensor.transpose(ps[m][:, (k % 2) * SEQ + t * P:(k % 2) * SEQ + (t + 1) * P],
                                                       hs[:, t, k * P:(k + 1) * P], ident)
                    last.then_inc(S["mT_ps"], 1)
                for n in range(4):
                    arrived(i)
                    w(layer, "mT_ready", n)
                    v = unit(i).rearrange("p (k n) -> p k n", k=2)
                    for k in (2 * n, 2 * n + 1):
                        for t in range(NT):
                            for f in range(2):
                                last = mm(ps[4 + 2 * t + f][:, :], hnT[:, k, t * P:(t + 1) * P],
                                          v[:, k % 2, f * 512:(f + 1) * 512], start=(k == 0), stop=(k == KD - 1))
                    last.then_inc(unit_used, 1)
                    i += 1
                assert i == base + MIX_UNITS

            def dense_pass(base):
                for j, (kind, c) in enumerate(pass_order()):
                    i = base + j
                    arrived(i)
                    if kind == "down":
                        pe.wait_ge(ffn_act, c + 1)
                        v = unit(i).rearrange("p (j n) -> p j n", j=2)
                        for jj in range(2):
                            for t in range(NT):
                                for f in range(2):
                                    last = mm(ps[4 + 2 * t + f][:, :], act_sb[:, c % 2, jj, t * P:(t + 1) * P],
                                              v[:, jj, f * 512:(f + 1) * 512],
                                              start=(c == 0 and jj == 0), stop=(c == NCHUNK - 1 and jj == 1))
                    else:
                        n = 2 * (c % 2) + (kind == "up")
                        if c >= 2:
                            pe.wait_ge(ffn_act, c - 1)
                        v = unit(i).rearrange("p (k n) -> p k n", k=KD)
                        for jj in range(2):
                            for k in range(KD):
                                last = mm(ps[n][:, jj * SEQ:(jj + 1) * SEQ], v[:, k, jj * P:(jj + 1) * P],
                                          hnT[:, k, :], start=(k == 0), stop=(k == KD - 1))
                    last.then_inc(unit_used, 1)

            def gather():
                for k in range(KD):
                    for t in range(NT):
                        last = mm(ps[6 + k // 4][:, (k % 4) * P:(k % 4 + 1) * P], hs[:, t, k * P:(k + 1) * P],
                                  gsel[:, t, :], start=(t == 0), stop=(t == NT - 1))
                    if k % 4 == 3:
                        last.then_inc(xg_ps, 1)
                for t in range(NT):
                    last = nc.tensor.transpose(ps[1][:, t * P:(t + 1) * P], gsel[:, t, :], ident)
                last.then_inc(gt_ps, 1)

            def transpose_act(q, c):
                pe.wait_ge(ffn_act, q * NCHUNK + NCHUNK + c + 1)
                if c >= 2:
                    pe.wait_ge(aT_ready, q * NCHUNK + c - 1)
                for jj in range(2):
                    last = nc.tensor.transpose(ps[6 + c % 2][:, jj * P:(jj + 1) * P],
                                               a_tok[:, c % 2, jj * P:(jj + 1) * P], ident)
                last.then_inc(aT_ps, 1)

            def expert_pass(rnd, e):
                q = e + rnd * NEXP
                g = e + rnd * NGATHER
                pe.wait_ge(xg_ready, 2 * g + 2)
                pe.wait_ge(gt_ready, g + 1)
                for j, (kind, c) in enumerate(pass_order()):
                    i = STATIC_UNITS + rnd * NEXP * PASS_UNITS + j
                    if kind == "down" and c == NCHUNK - 1:
                        transpose_act(q, c)
                    pe.wait_ge(loaded[i % SLOTS], e * (16 * PASS_UNITS // SLOTS) + 16 * (i // SLOTS + 1))
                    if kind == "down":
                        pe.wait_ge(aT_ready, q * NCHUNK + c + 1)
                        if c == 0:
                            pe.wait_ge(moe_drained, q * 2 + 1)
                        v = unit(i).rearrange("p (j n) -> p j n", j=2)
                        for jj in range(2):
                            for f in range(2):
                                last = mm(ps[4 + f][:, :], actT[:, c % 2, jj, :], v[:, jj, f * 512:(f + 1) * 512],
                                          start=(c == 0 and jj == 0), stop=(c == NCHUNK - 1 and jj == 1))
                    else:
                        n = 2 * (c % 2) + (kind == "up")
                        if kind == "gate":
                            pe.wait_ge(ffn_act, q * NCHUNK + NCHUNK + c - 1)
                            if c == 1:
                                pe.wait_ge(moe_drained, q * 2 + 1)
                        v = unit(i).rearrange("p (k n) -> p k n", k=KD)
                        for k in range(KD):
                            last = mm(ps[n][:, 0:FF_CHUNK], xgT[:, k, :], v[:, k, :],
                                      start=(k == 0), stop=(k == KD - 1))
                    last.then_inc(unit_used, 1)
                    if kind == "gate" and c:
                        transpose_act(q, c - 1)
                pe.wait_ge(g_built, g + 2)
                gather()
                pe.wait_ge(y_ready, q + 1)
                for t in range(NT):
                    for f in range(2):
                        last = mm(ps[4 - 2 * t + f][:, :], gselT[:, t, :], y_sb[:, f * 512:(f + 1) * 512],
                                  start=True, stop=True)
                    last.then_inc(sc_ps, 1)

            def expert_round(rnd):
                pe.wait_ge(g_built, rnd * NGATHER + 1)
                if rnd:
                    pe.wait_ge(xg_ready, 2 * NGATHER)
                    pe.wait_ge(gt_ready, NGATHER)
                gather()
                with pe.Fori(0, NEXP) as e:
                    expert_pass(rnd, e)

            pe.wait_ge(s_const, 16 * N_CONST)
            nc.tensor.transpose(ps[7][:, 0:P], rows[:, :], ident).then_inc(s_par_ps, 1)
            mixer(0, 0)
            norm_transposes(0, 1)
            w(0, "hnT_ready", 7)
            dense_pass(MIX_UNITS)
            mixer(1, LAYER0_UNITS)
            norm_transposes(1, 1)
            w(1, "hnT_ready", 7)
            for t in range(NT):
                for k in range(KD):
                    last = mm(ps[0][:, t * 8:(t + 1) * 8], hnT[:, k, t * P:(t + 1) * P], wrt[:, k, :],
                              start=(k == 0), stop=(k == KD - 1))
            last.then_inc(router_ps, 1)
            pe.wait_ge(sel_ready, 1)
            mm(ps[0][:, 0:NEXP], tri, selm[:, 0:NEXP], start=True, stop=True)
            mm(ps[0][:, NEXP:2 * NEXP], tri, selm[:, NEXP:2 * NEXP], start=True, stop=False)
            mm(ps[0][:, NEXP:2 * NEXP], ones, selm[:, 0:NEXP], start=False, stop=True)
            mm(ps[0][:, 2 * NEXP:3 * NEXP], ones, selm[:, 0:NEXP], start=True, stop=False)
            mm(ps[0][:, 2 * NEXP:3 * NEXP], ones, selm[:, NEXP:2 * NEXP], start=False, stop=True).then_inc(pos_ps, 1)
            expert_round(0)
            pe.wait_ge(over_ready, 1)
            with pe.If(pe.value_load(over_i[0:1, 0:1], min_val=0, max_val=1)):
                expert_round(1)

        @block.scalar
        def _(act):
            go = nc.scalar.activation

            def w(layer, name, k):
                act.wait_ge(S[name], upto(layer, name, k))

            def scale_rows(layer, n):
                for t in range(NT):
                    w(layer, "rstd", n)
                    go(hs[:, t, :], h[:, t, :], ACT.Copy, scale=rs[:, t:t + 1]).then_inc(S["hs_ready"], 1)

            def mixer(layer, base):
                scale_rows(layer, 0)
                w(layer, "gat_in", 0)
                go(e1, nx, ACT.Exp)
                go(tb, ps[6][:, 0:16].rearrange("p (t n) -> p t n", t=NT)[:, :, 4:8], ACT.Tanh,
                   scale=0.5).then_inc(S["gat_e"], 1)
                for g in range(CONV_GROUPS):
                    act.wait_ge(unit_used, base + 2 * g + 2)
                    for ct in range(4):
                        col = 32 + layer * 48 + 3 * 12 + 4 * g + ct
                        go(qkvT[:, 4 * g + ct, :], ps[2 * g + ct // 2][:, (ct % 2) * SEQ:(ct % 2 + 1) * SEQ],
                           ACT.Copy, scale=par[:, col:col + 1]).then_inc(S["tap0"], 1)
                    w(layer, "conv_out", g)
                    if g:
                        w(layer, "qkv_act", g - 1)
                    go(th[:, :, :].rearrange("p a b -> p (a b)"),
                       qkvT[:, 4 * g:4 * g + 4, :].rearrange("p a b -> p (a b)"), ACT.Tanh,
                       scale=0.5).then_inc(S["th_conv"], 1)
                w(layer, "dec_arg", 0)
                go(decay, decay, ACT.Exp).then_inc(S["dec_exp"], 1)
                w(layer, "kd_in", 0)
                go(kdfac, kdarg, ACT.Exp).then_inc(S["dec_exp"], 1)
                go(eg, gcs[:, H:TH], ACT.Exp).then_inc(S["dec_exp"], 1)
                for t in range(NT):
                    w(layer, "d1_ps", t)
                    go(dinv[:, 4 * t:4 * t + 4, :].rearrange("p a b -> p (a b)"), ps[2 + t][:, :],
                       ACT.Copy).then_inc(S["d1_ready"], 1)
                fill = [(g, t) for g in range(len(FILL_GROUPS)) for t in range(NT)]

                def filler():
                    if not fill:
                        return
                    g, t = fill.pop(0)
                    if g < 2:
                        return
                    if t == 0:
                        w(layer, "proj_first", g)
                    else:
                        act.wait_ge(unit_used, base + 2 * CONV_GROUPS + 2 * g + 2)
                    if g == 2:
                        go(rv[:, t, :], ps[t][:, :], ACT.Copy).then_inc(S["rv_done"], 1)
                    else:
                        n = 2 * (g - 3) + t
                        w(layer, "rope_done" if g == 3 else "rg_done", 3 if g == 3 else t)
                        go(th[:, t, :], ps[t][:, :], ACT.Tanh, scale=0.5).then_inc(S["th_g"], 1)

                for lv in range(1, len(LEVELS)):
                    for t in range(NT):
                        n = 2 * (lv - 1) + t
                        w(layer, "p_ps", n)
                        if n >= 2:
                            w(layer, "de_ps", n - 2)
                        go(prod[:, 4 * t:4 * t + 4, :].rearrange("p a b -> p (a b)"), ps[2 + t][:, :],
                           ACT.Copy).then_inc(S["p_ready"], 1)
                    filler()
                    filler()
                w(layer, "vn_ps", 0)
                go(vnew[:, 0, :], ps[2][:, :], ACT.Copy).then_inc(S["vn_ready"], 1)
                w(layer, "rqT_ps", 0)
                go(rT[:, 0, 0:2, :], quad(ps[0][:, :], 2), ACT.Copy)
                go(rT[:, 0, 2:4, :], quad(ps[1][:, :], 2), ACT.Copy).then_inc(S["rqT_ready"], 1)
                w(layer, "st_ps", 0)
                go(state[:, :, :], quad(ps[3][:, :]), ACT.Copy).then_inc(S["st_ready"], 1)
                w(layer, "rkT_ps", 0)
                go(rT[:, 1, 0:2, :], quad(ps[4][:, :], 2), ACT.Copy)
                go(rT[:, 1, 2:4, :], quad(ps[5][:, :], 2), ACT.Copy).then_inc(S["rkT_ready"], 1)
                w(layer, "vn_ps", 1)
                go(vnew[:, 1, :], ps[4][:, :], ACT.Copy).then_inc(S["vn_ready"], 1)
                w(layer, "go_ps", 1)
                for g in range(GATE_GROUPS):
                    for t in range(NT):
                        if t == 0:
                            w(layer, "proj_first", 5 + g)
                        else:
                            act.wait_ge(unit_used, base + 2 * (CONV_GROUPS + len(FILL_GROUPS) + g) + 2)
                        go(gates[:, t, g * 512:(g + 1) * 512], ps[2 + t][:, :], ACT.Tanh,
                           scale=0.5).then_inc(S["gate_done"], 1)
                for r in range(2):
                    w(layer, "rt_ps", r)
                    go(rT[:, r, 0:2, :], quad(ps[4 + 2 * r][:, :], 2), ACT.Copy)
                    go(rT[:, r, 2:4, :], quad(ps[5 + 2 * r][:, :], 2), ACT.Copy).then_inc(S["rt_ready"], 1)
                for m in range(4):
                    w(layer, "mT_ps", m)
                    go(hnT[:, 2 * m:2 * m + 2, :], quad(ps[m][:, :], 2), ACT.Copy).then_inc(S["mT_ready"], 1)

            def dense_pass(base):
                order = pass_order()
                for c in range(NCHUNK):
                    act.wait_ge(unit_used, base + order.index(("gate", c)) + 1)
                    if c >= 2:
                        act.wait_ge(ffn_a1, c - 1)
                    go(th[:, c % 2, :], ps[2 * (c % 2)][:, :], ACT.Tanh, scale=0.5).then_inc(ffn_th, 1)

            def copy_actT(q, c):
                act.wait_ge(aT_ps, q * NCHUNK + c + 1)
                if c >= 2:
                    act.wait_ge(unit_used, q * PASS_UNITS + STATIC_UNITS + pass_order().index(("down", c - 2)) + 1)
                go(actT[:, c % 2, :, :], quad(ps[6 + c % 2][:, 0:2 * P], 2), ACT.Copy).then_inc(aT_ready, 1)

            def copy_gselT(g):
                act.wait_ge(gt_ps, g + 1)
                go(gselT, quad(ps[1][:, 0:NT * P], NT), ACT.Copy).then_inc(gt_ready, 1)

            def expert_pass(rnd, e):
                q = e + rnd * NEXP
                off = q * PASS_UNITS + STATIC_UNITS
                order = pass_order()
                for c in range(NCHUNK):
                    act.wait_ge(unit_used, off + order.index(("gate", c)) + 1)
                    act.wait_ge(ffn_a1, q * NCHUNK + NCHUNK + c - 1)
                    go(th[:, c % 2, 0:FF_CHUNK], ps[2 * (c % 2)][:, 0:FF_CHUNK], ACT.Tanh,
                       scale=0.5).then_inc(ffn_th, 1)
                    if c:
                        copy_actT(q, c - 1)
                copy_actT(q, NCHUNK - 1)
                act.wait_ge(unit_used, off + PASS_UNITS)
                for f in range(2):
                    last = go(y_sb[:, f * 512:(f + 1) * 512], ps[4 + f][:, :], ACT.Copy)
                last.then_inc(y_ready, 1)
                act.wait_ge(sc_ps, q * 2 + 2)
                copy_gselT(e + (rnd * NGATHER + 1))

            def expert_round(rnd):
                copy_gselT(rnd * NGATHER)
                with act.Fori(0, NEXP) as e:
                    expert_pass(rnd, e)

            act.wait_ge(s_const, 16 * N_CONST)
            go(ea, alog[:, :], ACT.Exp).then_inc(s_ea, 1)
            act.wait_ge(s_par, 1)
            mixer(0, 0)
            scale_rows(0, 1)
            dense_pass(MIX_UNITS)
            mixer(1, LAYER0_UNITS)
            scale_rows(1, 1)
            act.wait_ge(S["m_ready"], upto(1, "m_ready", 1))
            act.dma_start(fnorm, final_norm.rearrange("(o n) -> o n", o=1).to_broadcast([P, DM])).then_inc(s_fnorm, 16)
            act.wait_ge(router_in, 1)
            go(pd, p0, ACT.Exp).then_inc(router_e, 1)
            expert_round(0)
            act.wait_ge(over_ready, 1)
            with act.If(act.value_load(over_i[0:1, 0:1], min_val=0, max_val=1)):
                expert_round(1)

        @block.gpsimd
        def _(pool):
            tt, tsc = nc.gpsimd.tensor_tensor, nc.gpsimd.tensor_scalar
            n_chain = [0]

            def link(ins):
                n_chain[0] += 1
                ins.then_inc(pool_chain, 1)
                pool.wait_ge(pool_chain, n_chain[0])

            def w(layer, name, k):
                pool.wait_ge(S[name], upto(layer, name, k))

            def rstd(layer, n):
                w(layer, "sumsq", n)
                link(tsc(rs, ss, 1.0 / DM, EPS, ALU.mult, ALU.add))
                tt(rs, rs, mhalf[:, 0:NT], ALU.pow).then_inc(S["rstd"], 1)

            def mixer(layer, base):
                rstd(layer, 0)
                w(layer, "g_ready", 0)
                tt(einv, tiled(tri, TH), over(gcol, P), ALU.mult).then_inc(S["trig_ready"], 1)
                w(layer, "dec_exp", 0)
                tt(decay, decay, tiled(tri, TH), ALU.mult).then_inc(S["decay_ready"], 1)
                w(layer, "rr_in", 0)
                tt(rr, rr0, mhalf, ALU.pow).then_inc(S["rr_ready"], 1)
                w(layer, "rr_ready", 0)
                w(layer, "beta_ready", 0)
                link(tt(cneg, rr[:, TH:2 * TH], beta, ALU.mult))
                link(tsc(cneg, cneg, -1.0, None, ALU.mult))
                tt(umask[:, :, :], tiled(ident, TH), over(cneg, P), ALU.mult).then_inc(S["diagc_ready"], 1)
                w(layer, "un_ready", 1)
                for lv in range(len(LEVELS)):
                    if lv == 0:
                        w(layer, "bcc_ps", 1)
                    elif lv == 1:
                        w(layer, "e1_ready", 0)
                    else:
                        w(layer, "p_ps", 2 * (lv - 2) + 1)
                    tt(umask[:, :, :], un, tiled(cst[:, C_MASK + lv * P:C_MASK + (lv + 1) * P], TH),
                       ALU.mult).then_inc(S["umask_ready"], 1)
                for t in range(NT):
                    w(layer, "gz_half", t)
                    tt(quad(gzs[:, t, :]), quad(gzs[:, t, :]), tiled(gnorm[:, layer, :], H),
                       ALU.mult).then_inc(S["gz_done"], 1)
                w(layer, "rms_in", 0)
                tt(ors, oss, mhalf, ALU.pow).then_inc(S["rms_ready"], 1)

            pool.memset(mhalf, -0.5).then_inc(s_zero, 1)
            pool.wait_ge(s_zero, 1)
            pool.wait_ge(s_const, 16 * N_CONST)
            for layer in range(DEPTH):
                mixer(layer, 0)
                rstd(layer, 1)
            pool.wait_ge(s_fin_ss, 1)
            link(tsc(rs, ss, 1.0 / DM, EPS, ALU.mult, ALU.add))
            tt(rs, rs, mhalf[:, 0:NT], ALU.pow).then_inc(s_fin_rs, 1)

        @block.vector
        def _(dve):
            V = nc.vector
            tt, tsc, stt = V.tensor_tensor, V.tensor_scalar, V.scalar_tensor_tensor
            n_chain = [0]

            def link(ins):
                n_chain[0] += 1
                ins.then_inc(dve_chain, 1)
                dve.wait_ge(dve_chain, n_chain[0])

            def sig(ins, name):
                return ins.then_inc(S[name], 1)

            def w(layer, name, k):
                dve.wait_ge(S[name], upto(layer, name, k))

            def sumsq(signal):
                for t in range(NT):
                    last = V.tensor_tensor_reduce(out=hs[:, t, :], in0=h[:, t, :], in1=h[:, t, :], scale=1.0,
                                                  scalar=0.0, op0=ALU.mult, op1=ALU.add, accum_out=ss[:, t:t + 1])
                last.then_inc(signal, 1)

            def norm(layer, n):
                sumsq(S["sumsq"])
                for m in range(4):
                    w(layer, "hT_ps", 4 * n + m)
                    col = 16 * n + layer * KD + 2 * m
                    sig(tt(hnT[:, 2 * m:2 * m + 2, :], quad(ps[m][:, :], 2), over(par[:, col:col + 2], SEQ),
                           ALU.mult), "hnT_ready")

            def mixer(layer, base):
                norm(layer, 0)
                w(layer, "ab_ps", 0)
                ab = ps[6][:, 0:16].rearrange("p (t n) -> p t n", t=NT)
                dt2 = tiled(dtb[:, layer * H:(layer + 1) * H], NT)
                ea2 = tiled(ea[:, layer * H:(layer + 1) * H], NT)
                gx2 = quad(gx, NT)
                link(tt(gx2, ab[:, :, 0:H], dt2, ALU.add))
                link(tsc(nx, gx, -1.0, None, ALU.mult))
                sig(tt(nx, nx, gx, ALU.min), "gat_in")
                w(layer, "gat_e", 0)
                link(tsc(beta, tb, 0.5, 0.5, ALU.mult, ALU.add))
                link(tsc(hbeta, beta, 0.5, None, ALU.mult))
                link(tsc(den, e1, 2.0, None, ALU.add))
                link(V.reciprocal(den, den))
                link(tt(s1, e1, den, ALU.mult))
                link(tt(s2, s1, s1, ALU.mult))
                link(tsc(poly, s2, 1.0 / 19, None, ALU.mult))
                for k in range(8, 0, -1):
                    link(stt(poly, poly, 1.0 / (2 * k + 1), s2, ALU.add, ALU.mult))
                link(stt(poly, poly, 1.0, s1, ALU.add, ALU.mult))
                link(tsc(sp, gx, 0.0, None, ALU.max))
                link(stt(sp, poly, 2.0, sp, ALU.mult, ALU.add))
                if layer == 0:
                    dve.wait_ge(s_ea, 1)
                sig(stt(quad(gcol, NT), quad(sp, NT), -1.0, ea2, ALU.mult, ALU.mult), "g_ready")
                w(layer, "g_ready", 0)
                sig(V.tensor_copy(hbeta, hbeta), "beta_ready")
                for g in range(CONV_GROUPS):
                    for s in range(1, CONV_K):
                        for ct in range(4):
                            n = 4 * g + ct
                            if s == 1 and ct % 2 == 0:
                                w(layer, "tap0", n + 1)
                            col = 32 + layer * 48 + (3 - s) * 12 + n
                            src = ps[2 * g + ct // 2][:, (ct % 2) * SEQ:(ct % 2 + 1) * SEQ - s]
                            ins = stt(qkvT[:, n, s:SEQ], src, par[:, col:col + 1], qkvT[:, n, s:SEQ],
                                      ALU.mult, ALU.add)
                        if s < CONV_K - 1:
                            link(ins)
                        else:
                            sig(ins, "conv_out")
                    w(layer, "th_conv", g)
                    grp = qkvT[:, 4 * g:4 * g + 4, :].rearrange("p a b -> p (a b)")
                    sig(stt(grp, th[:, :, :].rearrange("p a b -> p (a b)"), 1.0, grp, ALU.add, ALU.mult),
                        "qkv_act")
                    w(layer, "qkv_act", g)
                    if g < 2:
                        sig(tt(sq[:, g, :, :].rearrange("p a b -> p (a b)"), grp, grp, ALU.mult), "sq_ready")
                w(layer, "gc_ps", 0)
                link(V.tensor_copy(gcs, ps[6][:, 64:64 + TH]))
                link(tsc(ngc, gcs, -1.0, None, ALU.mult))
                for t in range(NT):
                    w(layer, "bc_ps", t)
                    for hh in range(H):
                        a = 4 * t + hh
                        last = tsc(decay[:, a, :], ps[t][:, hh * P:(hh + 1) * P], ngc[:, a:a + 1], 0.0,
                                   ALU.add, ALU.min)
                    if t == 0:
                        sig(tt(kdarg, quad(ps[0][:, :])[:, :, P - 1], gcs[:, 0:H], ALU.subtract), "kd_in")
                sig(last, "dec_arg")
                w(layer, "ssq_ps", 0)
                sig(tsc(rr0, ps[7][:, 32:48], 4 * EPS, None, ALU.add), "rr_in")
                for t in range(NT):
                    w(layer, "vtok_ps", t)
                    sig(tt(quad(bv[:, t, :]), quad(ps[4 + t][:, :]), over(hbeta[:, 4 * t:4 * t + 4], DH),
                           ALU.mult), "bv_ready")
                w(layer, "rr_ready", 0)
                w(layer, "dec_exp", 2)
                w(layer, "ktok_ps", 0)
                w(layer, "diagc_ready", 0)
                link(tt(kdfac, kdfac, rr[:, TH:TH + H], ALU.mult))
                sig(tt(kdec[:, :, :], quad(ps[7][:, :]), over(kdfac, DH), ALU.mult), "kdec_ready")
                link(tt(ceg, cneg[:, H:TH], eg, ALU.mult))
                link(tsc(rqs, rr[:, 0:TH], DH ** -0.5, None, ALU.mult))
                link(tt(rqsq, rqs, rqs, ALU.mult))
                w(layer, "decay_ready", 0)
                for t in range(NT):
                    w(layer, "bcc_ps", t)
                    sig(tt(quad(attnT[:, 4 * t:4 * t + 4, :].rearrange("p a b -> p (a b)")),
                           quad(ps[t][:, :]), decay[:, 4 * t:4 * t + 4, :], ALU.mult), "dec_beta")
                for t in range(NT):
                    w(layer, "kk_ps", t)
                    w(layer, "dec_beta", t)
                    for hh in range(H):
                        a = 4 * t + hh
                        last = stt(un[:, a, :], ps[2 + t][:, hh * P:(hh + 1) * P], rr[:, TH + a:TH + a + 1],
                                   attnT[:, a, :], ALU.mult, ALU.mult)
                    sig(last, "un_ready")
                w(layer, "un_ready", 1)
                for t in range(NT):
                    w(layer, "qk_ps", t)
                    for hh in range(H):
                        a = 4 * t + hh
                        last = stt(attnT[:, a, :], ps[4 + t][:, hh * P:(hh + 1) * P], rr[:, TH + a:TH + a + 1],
                                   decay[:, a, :], ALU.mult, ALU.mult)
                    sig(last, "attn_ready")
                w(layer, "umask_ready", 0)
                sig(tt(einv, umask[:, :, :], tiled(ident, TH), ALU.add), "e1_ready")
                fill = [(g, t) for g in range(len(FILL_GROUPS)) for t in range(NT)]

                def filler():
                    if not fill:
                        return
                    g, t = fill.pop(0)
                    if g == 2:
                        return
                    if g < 2:
                        if t == 0:
                            w(layer, "proj_first", g)
                        else:
                            dve.wait_ge(unit_used, base + 2 * CONV_GROUPS + 2 * g + 2)
                        rot = C_ROT + t * 256
                        v = ps[t][:, :].rearrange("p (h s n) -> p h s n", h=H, s=2)
                        tv = th[:, t, :].rearrange("p (h s n) -> p h s n", h=H, s=2)
                        dst = rrot[:, g, t, :]
                        for s in range(2):
                            last = tt(tv[:, :, s, :], v[:, :, 1 - s, :],
                                      tiled(cst[:, rot + 128 + 64 * s:rot + 192 + 64 * s], H), ALU.mult)
                        link(last)
                        link(tt(quad(dst), quad(ps[t][:, :]), tiled(cst[:, rot:rot + 128], H), ALU.mult))
                        sig(tt(dst, dst, th[:, t, :], ALU.add), "rope_done")
                    else:
                        n = 2 * (g - 3) + t
                        w(layer, "th_g", n)
                        dst, name = (rgs, "rg_done") if g == 3 else (gzs, "gz_half")
                        sig(stt(dst[:, t, :], th[:, t, :], 1.0, ps[t][:, :], ALU.add, ALU.mult), name)

                for lv in range(1, len(LEVELS)):
                    filler()
                    if lv == 1:
                        w(layer, "e1_ready", 0)
                    for t in range(NT):
                        n = 2 * (lv - 1) + t
                        w(layer, "de_ps", n)
                        if n >= 2:
                            w(layer, "de_ready", n - 2)
                        sl = slice(4 * t, 4 * t + 4)
                        if lv < len(LEVELS) - 1:
                            tt(dinv[:, sl, :], dinv[:, sl, :], quad(ps[4 + t][:, :]), ALU.add)
                        sig(tt(einv[:, sl, :], einv[:, sl, :], quad(ps[6 + t][:, :]), ALU.add), "de_ready")
                    filler()
                w(layer, "ks_ps", 0)
                for hh in range(H):
                    c = slice(hh * P, (hh + 1) * P)
                    last = stt(rhs1[:, c], ps[2][:, c], ceg[:, hh:hh + 1], bv[:, 1, c], ALU.mult, ALU.add)
                sig(last, "rhs1_ready")
                for n in range(2):
                    w(layer, "s_ps", n)
                    dec = cst[:, C_DEC + n * 512:C_DEC + (n + 1) * 512]
                    sig(tt(st0[:, 2 * n:2 * n + 2, :].rearrange("p a b -> p (a b)"), ps[n][:, :], dec, ALU.mult),
                        "s_ready")
                w(layer, "s_ps", 2)
                dec = cst[:, C_DEC:C_DEC + H * 256].rearrange("p (a b) -> p a b", a=H)[:, :, 0:P]
                sig(tt(st1[:, :, :], quad(ps[3][:, :]), dec, ALU.mult), "s_ready")
                w(layer, "qs_ps", 0)
                sig(tt(quad(qs_sb[:, :]), quad(ps[5][:, :]), over(eg, DH), ALU.mult), "qs_done")
                for t in range(NT):
                    w(layer, "ro_ps", t)
                    sig(V.tensor_copy(o_ret[:, t, :], ps[t][:, :]), "ro_sb")
                w(layer, "go_ps", 0)
                sig(V.tensor_copy(o_gdn[:, 0, :], ps[6][:, :]), "go_sb")
                w(layer, "go_ps", 1)
                w(layer, "qs_done", 0)
                sig(tt(o_gdn[:, 1, :], ps[7][:, :], qs_sb[:, :], ALU.add), "go_sb")
                w(layer, "ro_sb", 1)
                w(layer, "go_sb", 1)
                sqv = st0[:, :, :].rearrange("p a b -> p (a b)")
                for r, src in enumerate((o_ret, o_gdn)):
                    flat = src.rearrange("p t n -> p (t n)")
                    link(tt(sqv, flat, flat, ALU.mult))
                    link(V.tensor_reduce(oss[:, r * TH:(r + 1) * TH], quad(sqv, TH), AX.X, ALU.add))
                link(tt(oss[:, TH:2 * TH], oss[:, TH:2 * TH], rqsq, ALU.mult))
                sig(tsc(oss, oss, 1.0 / DH, EPS, ALU.mult, ALU.add), "rms_in")
                w(layer, "rms_ready", 0)
                link(tt(ors[:, TH:2 * TH], ors[:, TH:2 * TH], rqs, ALU.mult))
                link(tsc(ors, ors, 0.5, None, ALU.mult))
                w(layer, "gz_done", 1)
                w(layer, "gz_half", 1)
                for r, (src, gate) in enumerate(((o_ret, rgs), (o_gdn, gzs))):
                    v = src.rearrange("p t n -> p (t n)")
                    link(tt(quad(v, TH), quad(v, TH), over(ors[:, r * TH:(r + 1) * TH], DH), ALU.mult))
                    sig(tt(v, v, gate[:, :, :].rearrange("p t n -> p (t n)"), ALU.mult), "br_ready")
                dve.wait_ge(unit_used, base + MIX_UNITS - 6)
                w(layer, "gate_done", 7)
                for t in range(NT):
                    for f in range(2):
                        g = gates[:, t, f * 512:(f + 1) * 512]
                        last = stt(g, g, 1.0, ps[2 * t + f][:, :], ALU.add, ALU.mult)
                sig(last, "ya_use")
                dve.wait_ge(unit_used, base + MIX_UNITS - 4)
                for t in range(NT):
                    for f in range(2):
                        g = gates[:, t, DM + f * 512:DM + (f + 1) * 512]
                        last = stt(g, g, 1.0, ps[4 + 2 * t + f][:, :], ALU.add, ALU.mult)
                link(last)
                w(layer, "ya_use", 0)
                for t in range(NT):
                    sig(tt(hs[:, t, :], gates[:, t, 0:DM], gates[:, t, DM:2 * DM], ALU.add), "m_ready")
                dve.wait_ge(unit_used, base + MIX_UNITS)
                for t in range(NT):
                    for f in range(2):
                        c = slice(f * 512, (f + 1) * 512)
                        sig(stt(h[:, t, c], ps[4 + 2 * t + f][:, :], 0.5, h[:, t, c], ALU.mult, ALU.add), "h_upd")
                w(layer, "h_upd", 3)

            def dense_pass(base):
                order = pass_order()
                for c in range(NCHUNK):
                    b = c % 2
                    dve.wait_ge(ffn_th, c + 1)
                    stt(a1[:, b, :], th[:, b, :], 1.0, ps[2 * b][:, :], ALU.add, ALU.mult).then_inc(ffn_a1, 1)
                    dve.wait_ge(ffn_a1, c + 1)
                    dve.wait_ge(unit_used, base + order.index(("up", c)) + 1)
                    if c >= 2:
                        dve.wait_ge(unit_used, base + order.index(("down", c - 2)) + 1)
                    stt(act_sb[:, b, :, :].rearrange("p j n -> p (j n)"), a1[:, b, :], 0.5, ps[2 * b + 1][:, :],
                        ALU.mult, ALU.mult).then_inc(ffn_act, 1)
                dve.wait_ge(unit_used, base + PASS_UNITS)
                for t in range(NT):
                    for f in range(2):
                        c = slice(f * 512, (f + 1) * 512)
                        tt(h[:, t, c], h[:, t, c], ps[4 + 2 * t + f][:, :], ALU.add).then_inc(ffn_drained, 1)
                dve.wait_ge(ffn_drained, 4)

            def build_gsel(g, e):
                V.tensor_copy(pcur.unsqueeze(2), quad(posm, NT)[:, :, bass.ds(e, 1)]).then_inc(pcur_ready, 1)
                dve.wait_ge(pcur_ready, g + 1)
                for t in range(NT):
                    last = tsc(gsel[:, t, :], cst[:, C_IOTA:C_IOTA + P], pcur[:, t:t + 1], None, ALU.is_equal)
                last.then_inc(g_built, 1)

            def copy_gathered(g):
                for m in range(2):
                    dve.wait_ge(xg_ps, g * 2 + m + 1)
                    col = 16 + KD + 4 * m
                    tt(xgT[:, 4 * m:4 * m + 4, :], quad(ps[6 + m][:, :]), over(par[:, col:col + 4], P),
                       ALU.mult).then_inc(xg_ready, 1)

            def expert_pass(rnd, e):
                q = e + rnd * NEXP
                g = e + (rnd * NGATHER + 1)
                off = q * PASS_UNITS + STATIC_UNITS
                order = pass_order()
                V.tensor_copy(gcur.unsqueeze(2), quad(gw, NT)[:, :, bass.ds(e, 1)]).then_inc(gcur_ready, 1)
                for c in range(NCHUNK):
                    b = c % 2
                    dve.wait_ge(ffn_th, q * NCHUNK + NCHUNK + c + 1)
                    stt(a1[:, b, 0:FF_CHUNK], th[:, b, 0:FF_CHUNK], 1.0, ps[2 * b][:, 0:FF_CHUNK],
                        ALU.add, ALU.mult).then_inc(ffn_a1, 1)
                    dve.wait_ge(ffn_a1, q * NCHUNK + NCHUNK + c + 1)
                    dve.wait_ge(unit_used, off + order.index(("up", c)) + 1)
                    if c >= 2:
                        dve.wait_ge(aT_ps, q * NCHUNK + c - 1)
                    stt(a_tok[:, b, :], a1[:, b, 0:FF_CHUNK], 0.5, ps[2 * b + 1][:, 0:FF_CHUNK],
                        ALU.mult, ALU.mult).then_inc(ffn_act, 1)
                dve.wait_ge(gt_ps, g)
                build_gsel(g, e + 1)
                copy_gathered(g)
                dve.wait_ge(gcur_ready, q + 1)
                for t in range(NT):
                    dve.wait_ge(sc_ps, q * 2 + t + 1)
                    for f in range(2):
                        c = slice(f * 512, (f + 1) * 512)
                        last = stt(h[:, t, c], ps[4 - 2 * t + f][:, :], gcur[:, t:t + 1], h[:, t, c],
                                   ALU.mult, ALU.add)
                    last.then_inc(moe_drained, 1)
                dve.wait_ge(moe_drained, q * 2 + 3)

            def expert_round(rnd):
                if rnd:
                    link(tsc(posm, posm, -float(P), None, ALU.add))
                    dve.wait_ge(gt_ps, NGATHER)
                build_gsel(rnd * NGATHER, 0)
                copy_gathered(rnd * NGATHER)
                with dve.Fori(0, NEXP) as e:
                    expert_pass(rnd, e)

            dve.wait_ge(s_par_ps, 1)
            V.tensor_copy(par[:, :], ps[7][:, 0:P]).then_inc(s_par, 1)
            dve.wait_ge(s_par, 1)
            mixer(0, 0)
            norm(0, 1)
            dense_pass(MIX_UNITS)
            mixer(1, LAYER0_UNITS)
            norm(1, 1)
            dve.wait_ge(router_ps, 1)
            link(V.tensor_copy(logit, ps[0][:, 0:16]))
            for t in range(NT):
                lg = logit[:, t * NEXP:(t + 1) * NEXP]
                a, b = over(lg, NEXP), tiled(lg, NEXP)
                g1, g2 = quad(cmp1[:, t, :], NEXP), quad(cmp2[:, t, :], NEXP)
                tt(g1, b, a, ALU.is_gt)
                link(tt(g2, b, a, ALU.is_equal))
                link(tt(g2, g2, quad(cst[:, C_LOW:C_LOW + 64], NEXP), ALU.mult))
                link(tt(g1, g1, g2, ALU.add))
                link(V.tensor_reduce(rank[:, t * NEXP:(t + 1) * NEXP], g1, AX.X, ALU.add))
                link(V.max(top[:, t * 8:(t + 1) * 8], lg))
            tv = quad(top, NT)
            tt(p0, tv[:, :, 1], tv[:, :, 0], ALU.subtract).then_inc(router_in, 1)
            dve.wait_ge(router_e, 1)
            link(tsc(p0, pd, 1.0, None, ALU.add))
            link(V.reciprocal(p0, p0))
            link(tt(p1, pd, p0, ALU.mult))
            link(tsc(sel, rank, 0.0, None, ALU.is_equal))
            link(tt(quad(gw, NT), quad(sel, NT), over(p0, NEXP), ALU.mult))
            link(tsc(sel, rank, 1.0, None, ALU.is_equal))
            link(tt(quad(sel, NT), quad(sel, NT), over(p1, NEXP), ALU.mult))
            link(tt(gw, gw, sel, ALU.add))
            tsc(selm, rank, 1.0, None, ALU.is_le).then_inc(sel_ready, 1)
            dve.wait_ge(sel_ready, 1)
            link(V.memset(posm, 0.0))
            dve.wait_ge(pos_ps, 1)
            pv = quad(posm, NT)[:, :, 0:NEXP]
            link(tt(pv, quad(ps[0][:, 0:NT * NEXP], NT), quad(selm, NT), ALU.mult))
            tsc(posm, posm, -1.0, None, ALU.add).then_inc(moe_drained, 1)
            dve.wait_ge(moe_drained, 1)
            link(V.tensor_reduce(cntm, ps[0][:, 2 * NEXP:3 * NEXP], AX.X, ALU.max))
            link(tsc(over_f, cntm, float(P), None, ALU.is_gt))
            V.tensor_copy(over_i[:, :], over_f).then_inc(over_ready, 1)
            expert_round(0)
            dve.wait_ge(over_ready, 1)
            with dve.If(dve.value_load(over_i[0:1, 0:1], min_val=0, max_val=1)):
                expert_round(1)
            sumsq(s_fin_ss)
            dve.wait_ge(s_fnorm, 16)
            dve.wait_ge(s_fin_rs, 1)
            for t in range(NT):
                stt(hs[:, t, :], h[:, t, :], rs[:, t:t + 1], fnorm, ALU.mult, ALU.mult).then_inc(s_final, 1)


_INS = ['x', 'norm_mix', 'w_in', 'conv_w', 'a_log', 'dt_bias', 'gdn_norm', 'w_branch', 'w_out', 'norm_ffn',
        'dense_w_gate', 'dense_w_up', 'dense_w_down', 'router', 'moe_w_gate', 'moe_w_up', 'moe_w_down', 'final_norm']


def kernel(**inputs):
    import concourse.bacc as _bacc
    from concourse.bass_utils import run_bass_kernel_spmd as _run

    nc = _bacc.Bacc("TRN2", target_bir_lowering=False, num_devices=1)
    arrays, args = {}, []
    for name in _INS + ['shape_constants']:
        a = shape_constants() if name == 'shape_constants' else np.ascontiguousarray(inputs[name])
        arrays[f"in_{name}_dram"] = a
        args.append(nc.dram_tensor(f"in_{name}_dram", a.shape, mybir.dt.from_np(a.dtype), kind="ExternalInput").ap())
    o = nc.dram_tensor("out_0_dram", (1, SEQ, DM), mybir.dt.float32, kind="ExternalOutput").ap()
    build(nc, *args, o)
    r = _run(nc, [arrays], core_ids=[0])
    return r.results[0]["out_0_dram"]
```

```python
import math
from contextlib import ExitStack

import numpy as np
import concourse.bass as bass
from concourse import mybir

DM = 1024
SEQ = 256
DEPTH = 2
H = 4
DH = 128
CONV_K = 4
DFF = 2816
NEXP = 8
EPS = 1e-6
IN_COLS = 6152
P = 128
NT = SEQ // P
KD = DM // P
TH = NT * H

COL_RQ, COL_RK, COL_RV, COL_RG, COL_CONV, COL_GZ, COL_AB, COL_GATE = 0, 512, 1024, 1536, 2048, 3584, 4096, 4104

UNIT = 2048
SLOTS = 11
FF_CHUNK = 256
NCHUNK = DFF // FF_CHUNK
PASS_UNITS = 3 * NCHUNK
assert PASS_UNITS % SLOTS == 0
CONV_GROUPS = 3
FILL_GROUPS = [COL_RQ, COL_RK, COL_RV, COL_RG, COL_GZ]
GATE_GROUPS = 4
MIX_UNITS = 2 * (CONV_GROUPS + len(FILL_GROUPS) + GATE_GROUPS) + 4 + 4
LAYER0_UNITS = MIX_UNITS + PASS_UNITS
STATIC_UNITS = LAYER0_UNITS + MIX_UNITS

LEVELS = [1, 2, 4, 8, 16, 32, 64]
C_ID, C_ONE, C_TRI, C_MASK = 0, 128, 256, 384
C_ROT = C_MASK + 128 * len(LEVELS)
C_DEC = C_ROT + NT * 256
C_LOW = C_DEC + H * 256
C_IOTA = C_LOW + NEXP * NEXP
C_COLS = C_IOTA + P

ROUNDS = 2

SPLITS = 3
MIX_SLOTS = 3
assert PASS_UNITS % SPLITS == 0


def shape_constants():
    c = np.zeros((P, C_COLS), np.float32)
    j = np.arange(P)[:, None]
    i = np.arange(P)[None, :]
    c[:, C_ID:C_ID + P] = (i == j)
    c[:, C_ONE:C_ONE + P] = 1.0
    c[:, C_TRI:C_TRI + P] = (j <= i)
    for n, b in enumerate(LEVELS):
        same = (i // (2 * b)) == (j // (2 * b))
        c[:, C_MASK + n * P:C_MASK + (n + 1) * P] = same & (i // b > j // b)
    inv_freq = np.float32(10000.0) ** (-np.arange(0, DH, 2, dtype=np.float32) / np.float32(DH))
    ang = np.arange(SEQ, dtype=np.float32)[:, None] * inv_freq[None, :].astype(np.float32)
    cos, sin = np.cos(ang), np.sin(ang)
    for t in range(NT):
        o = C_ROT + t * 256
        rows = slice(t * P, (t + 1) * P)
        c[:, o:o + 64] = cos[rows]
        c[:, o + 64:o + 128] = cos[rows]
        c[:, o + 128:o + 192] = -sin[rows]
        c[:, o + 192:o + 256] = sin[rows]
    i2 = np.arange(2 * P)[None, :]
    for h in range(H):
        lg = math.log(1.0 - 2.0 ** (-5.0 - h))
        c[:, C_DEC + h * 256:C_DEC + (h + 1) * 256] = np.where(
            i2 >= j, np.exp(np.maximum(i2 - j, 0) * lg) * DH ** -0.5, 0.0)
    e = np.arange(NEXP)
    c[:, C_LOW:C_LOW + NEXP * NEXP] = (e[None, :] < e[:, None]).reshape(1, -1)
    c[:, C_IOTA:C_IOTA + P] = i
    return c


def build(nc, x, norm_mix, w_in, conv_w, a_log, dt_bias, gdn_norm, w_branch, w_out, norm_ffn,
          dense_w_gate, dense_w_up, dense_w_down, router, moe_w_gate, moe_w_up, moe_w_down,
          final_norm, consts, out):
    f32 = mybir.dt.float32
    f32r = mybir.dt.float32r
    ALU = mybir.AluOpType
    ACT = mybir.ActivationFunctionType
    AX = mybir.AxisListType

    ctx = ExitStack()
    with ctx:
        def sb(name, *shape):
            return ctx.enter_context(nc.sbuf_tensor(name, [P, *shape], f32))

        def sem(name):
            return ctx.enter_context(nc.semaphore(name))

        def ground():
            return (nc.sbuf_base + 31) // 32 * 32

        ring_at = ground()
        ring = sb("ring", SLOTS, UNIT)
        h = sb("h", NT, DM)
        hs_at = ground()
        hs = sb("hs", NT, DM)
        hnT_at = ground()
        hnT = sb("hnT", KD, SEQ)
        cst_at = ground()
        cst = sb("cst", C_COLS)
        rows = sb("rows", P)
        par = sb("par", P)
        wab = sb("wab", DEPTH, KD, 8)
        wrt = sb("wrt", KD, NEXP)
        alog = sb("alog", DEPTH * H)
        dtb = sb("dtb", DEPTH * H)
        gnorm = sb("gnorm", DEPTH, DH)
        sm = sb("sm", 640)
        over_i = ctx.enter_context(nc.sbuf_tensor("over_i", [P, 1], mybir.dt.int32))
        phase_base = ground()
        qkvT = sb("qkvT", 12, SEQ)
        th = sb("th", 2, 512)
        sq = sb("sq", 2, H, SEQ)
        work = sb("work", 4, TH * P)
        attnT_at = ground()
        attnT = sb("attnT", TH, P)
        prod = qkvT[:, 8:12, :].rearrange("p a b -> p (a b)").rearrange("p (a b) -> p a b", b=P)
        umask_at = ground()
        umask = sb("umask", TH, P)
        rT_at = ground()
        rT = sb("rT", 2, H, SEQ)
        rv = sb("rv", NT, H * DH)
        rgs = sb("rgs", NT, H * DH)
        gzs = sb("gzs", NT, H * DH)
        st0 = umask[:, :, :].rearrange("p a b -> p (a b)").rearrange("p (h n) -> p h n", h=H)
        st1 = sb("st1", H, P)
        bv = sb("bv", NT, H * DH)
        kdec = sb("kdec", H, DH)
        decay, un, dinv, einv = (work[:, n, :].rearrange("p (a b) -> p a b", b=P) for n in range(4))
        vnew = work[:, 2, :].rearrange("p (t n) -> p t n", t=NT)
        gates = work[:, :, :].rearrange("p a n -> p (a n)").rearrange("p (t n) -> p t n", t=NT)
        rrot = hs[:, :, :].rearrange("p a (b n) -> p a b n", b=NT)
        o_ret = sq[:, 0, :, :].rearrange("p a b -> p (a b)").rearrange("p (t n) -> p t n", t=NT)
        o_gdn = sq[:, 1, :, :].rearrange("p a b -> p (a b)").rearrange("p (t n) -> p t n", t=NT)
        state = sb("state", H, DH)
        rhs1 = prod[:, 0:4, :].rearrange("p a b -> p (a b)")
        qs_sb = prod[:, 4:8, :].rearrange("p a b -> p (a b)")

        place = [phase_base]

        def phase(name, dt, *shape, at=None):
            if at is None:
                at = place[0]
                place[0] += 4 * int(np.prod(shape))
            return nc.alloc_sbuf_tensor_at(name, [P, *shape], dt, offset=at)

        w_hi = phase("w_hi", f32r, SPLITS, UNIT)
        w_lo = phase("w_lo", f32r, SPLITS, UNIT)
        th_f = phase("th_f", f32, 2, 2 * FF_CHUNK)
        a1 = phase("a1", f32, 2, 2 * FF_CHUNK)
        both = place[0]
        x_hi = phase("x_hi", f32r, KD, SEQ)
        x_lo = phase("x_lo", f32r, KD, SEQ)
        dense_end = place[0]
        place[0] = both
        xg_hi = phase("xg_hi", f32r, KD, P)
        xg_lo = phase("xg_lo", f32r, KD, P)
        y_hi = phase("y_hi", f32r, DM)
        y_lo = phase("y_lo", f32r, DM)
        gsel = phase("gsel", f32r, NT, P)
        gselT = phase("gselT", f32r, NT, P)
        hs_hi = phase("hs_hi", f32r, NT, DM, at=hs_at)
        hs_lo = phase("hs_lo", f32r, NT, DM, at=cst_at + 4 * C_MASK)
        assert C_MASK + NT * DM <= C_LOW
        a_tok = phase("a_tok", f32, 2, FF_CHUNK)
        assert max(dense_end, place[0]) <= nc.sbuf_usable_end
        m_hi = phase("m_hi", f32r, SPLITS, UNIT, at=ring_at + 4 * UNIT * MIX_SLOTS)
        m_lo = phase("m_lo", f32r, SPLITS, UNIT, at=ring_at + 4 * UNIT * (MIX_SLOTS + SPLITS))
        mx_hi = phase("mx_hi", f32r, KD, SEQ, at=ring_at + 4 * UNIT * (MIX_SLOTS + 2 * SPLITS))
        mx_lo = phase("mx_lo", f32r, KD, SEQ, at=ring_at + 4 * UNIT * (MIX_SLOTS + 2 * SPLITS + 1))
        assert MIX_SLOTS + 2 * SPLITS + 2 <= SLOTS and KD * SEQ == UNIT
        br_hi = phase("br_hi", f32r, 2, H, SEQ, at=rT_at)
        br_lo = [phase("br_lo0", f32r, H, SEQ, at=attnT_at), phase("br_lo1", f32r, H, SEQ, at=umask_at)]
        hn_at = hnT_at
        act_hi = phase("act_hi", f32r, 2, 2, SEQ, at=hn_at)
        act_lo = phase("act_lo", f32r, 2, 2, SEQ, at=hn_at + 4 * 4 * SEQ)
        actT_hi = phase("actT_hi", f32r, 2, 2, P, at=hn_at)
        actT_lo = phase("actT_lo", f32r, 2, 2, P, at=hn_at + 4 * 4 * P)
        fnorm_t = phase("fnorm_t", f32, DM, at=hn_at + 4 * 8 * P)
        fnorm = fnorm_t[:, :]

        ident = cst[:, C_ID:C_ID + P]
        ones = cst[:, C_ONE:C_ONE + P]
        tri = cst[:, C_TRI:C_TRI + P]

        at = [0]

        def small(n):
            at[0] += n
            assert at[0] <= 640
            return sm[:, at[0] - n:at[0]]

        ss, rs = small(NT), small(NT)
        mhalf = small(16)
        gx, nx, e1, den, s1, s2, poly, sp = (small(TH) for _ in range(8))
        ea = small(DEPTH * H)
        tb, beta, gcol, gcs, ngc, cneg, hbeta = (small(TH) for _ in range(7))
        rr0, rr = small(2 * TH), small(2 * TH)
        kdarg, kdfac, eg, ceg = (small(H) for _ in range(4))
        rqs = small(TH)
        oss, ors = small(2 * TH), small(2 * TH)
        rqsq = small(TH)
        logit, rank, sel = small(NT * NEXP), small(NT * NEXP), small(NT * NEXP)
        gw = small(NT * NEXP)
        top = small(NT * 8)
        pd, p0, p1 = small(NT), small(NT), small(NT)
        gcur = small(NT)
        posm = sm[:, at[0]:at[0] + NT * NEXP]
        at[0] += NT * NEXP
        selm, pcur, cntm, over_f = small(NT * NEXP), small(NT), small(1), small(1)
        cmp1 = a_tok[:, 0, 0:NT * NEXP * NEXP].rearrange("p (t n) -> p t n", t=NT)
        cmp2 = a_tok[:, 1, 0:NT * NEXP * NEXP].rearrange("p (t n) -> p t n", t=NT)

        ps = [ctx.enter_context(nc.psum_tensor(f"ps{n}", [P, 512], f32)) for n in range(8)]

        def quad(ap, n=4):
            return ap.rearrange("p (a b) -> p a b", a=n)

        def over(ap, n):
            return ap.unsqueeze(2).to_broadcast([P, ap.shape[1], n])

        def tiled(ap, n):
            return ap.unsqueeze(1).to_broadcast([P, n, ap.shape[1]])

        PER_LAYER = dict(
            sumsq=2, rstd=2, hs_ready=4, hT_ps=8, hnT_ready=8,
            ab_ps=1, gat_in=1, gat_e=1, g_ready=1, beta_ready=1, trig_ready=1, diagc_ready=1,
            gc_ps=1, bc_ps=2, bcc_ps=2, dec_arg=1, kd_in=1, dec_exp=3, decay_ready=1,
            tap0=12, conv_out=3, th_conv=3, qkv_act=3, sq_ready=2, ssq_ps=1, rr_in=1, rr_ready=1,
            vtok_ps=2, ktok_ps=1, bv_ready=2, kdec_ready=1, dec_beta=2,
            kk_ps=2, qk_ps=2, un_ready=2, attn_ready=2, umask_ready=6, e1_ready=1, d1_ps=2, d1_ready=2,
            p_ps=12, p_ready=12, de_ps=12, de_ready=12,
            proj_first=9, rope_done=4, rv_done=2, th_g=4, rg_done=2, gz_half=2, gz_done=2, gate_done=8,
            vn_ps=2, vn_ready=2, st_ps=1, st_ready=1, ks_ps=1, rhs1_ready=1, qs_ps=1,
            rqT_ps=1, rkT_ps=1, rqT_ready=1, rkT_ready=1, s_ps=3, s_ready=3,
            ro_ps=2, go_ps=2, ro_sb=2, go_sb=2, rms_in=1, rms_ready=1, br_ready=2, rt_ps=2,
            mx_hi=8, mx_lo=8, br_hi=2, br_lo=2, ya_use=1, m_ready=2, mT_ps=4, h_upd=4,
            rope_ps=4, qs_done=1)
        S = {name: sem("s_" + name) for name in PER_LAYER}
        N_FIRST, N_CONST = 7, 4
        s_first = sem("s_first")
        s_const = sem("s_const")
        s_fnorm = sem("s_fnorm")
        s_zero = sem("s_zero")
        s_par_ps = sem("s_par_ps")
        s_par = sem("s_par")
        s_ea = sem("s_ea")
        unit_used = sem("unit_used")
        loaded = [sem(f"loaded{n}") for n in range(SLOTS)]
        dve_chain = sem("dve_chain")
        pool_chain = sem("pool_chain")
        ffn_th = sem("ffn_th")
        ffn_a1 = sem("ffn_a1")
        ffn_act = sem("ffn_act")
        ffn_drained = sem("ffn_drained")
        gcur_ready = sem("gcur_ready")
        pcur_ready = sem("pcur_ready")
        sel_ready = sem("sel_ready")
        pos_ps = sem("pos_ps")
        over_ready = sem("over_ready")
        hi_ready = sem("hi_ready")
        lo_ready = sem("lo_ready")
        x_hi_ready = sem("x_hi_ready")
        x_lo_ready = sem("x_lo_ready")
        act_hi_ready = sem("act_hi_ready")
        act_lo_ready = sem("act_lo_ready")
        s_h = sem("s_h")
        hs_ps = sem("hs_ps")
        hs_hi_ready = sem("hs_hi_ready")
        hs_lo_ready = sem("hs_lo_ready")
        g_built = sem("g_built")
        xg_ps = sem("xg_ps")
        gt_ps = sem("gt_ps")
        xg_hi_ready = sem("xg_hi_ready")
        xg_lo_ready = sem("xg_lo_ready")
        gt_ready = sem("gt_ready")
        aT_ps = sem("aT_ps")
        aT_hi_ready = sem("aT_hi_ready")
        aT_lo_ready = sem("aT_lo_ready")
        y_hi_ready = sem("y_hi_ready")
        y_lo_ready = sem("y_lo_ready")
        sc_ps = sem("sc_ps")
        moe_drained = sem("moe_drained")
        router_ps = sem("router_ps")
        router_e = sem("router_e")
        router_in = sem("router_in")
        s_fin_ss = sem("s_fin_ss")
        s_fin_rs = sem("s_fin_rs")
        s_final = sem("s_final")
        s_out = sem("s_out")

        def upto(layer, name, k):
            assert 0 <= k < PER_LAYER[name], (name, k)
            return layer * PER_LAYER[name] + k + 1

        plan, fill_count, last_unit = [], [0] * SLOTS, [None] * SLOTS
        for i in range(STATIC_UNITS):
            if MIX_UNITS <= i < LAYER0_UNITS:
                slot = (i - MIX_UNITS) % SLOTS
            else:
                slot = (i if i < MIX_UNITS else i - LAYER0_UNITS) % MIX_SLOTS
            fill_count[slot] += 16
            plan.append((slot, fill_count[slot], last_unit[slot]))
            last_unit[slot] = i

        def expert_load_value(q, j):
            return q * (16 * PASS_UNITS // SLOTS) + (fill_count[j % SLOTS] + 16 * (j // SLOTS + 1))

        def mixer_split(n, k):
            return tuple(m[:, n % SPLITS, :].rearrange("p (k n) -> p k n", k=k) for m in (m_hi, m_lo))

        def w_in_units(layer, col):
            v = w_in[layer, :, col:col + 512].rearrange("(k p) n -> p k n", p=P)
            return [v[:, 0:4, :], v[:, 4:8, :]]

        def mixer_units(layer):
            u = []
            for g in range(CONV_GROUPS):
                u += w_in_units(layer, COL_CONV + 512 * g)
            for col in FILL_GROUPS:
                u += w_in_units(layer, col)
            for g in range(GATE_GROUPS):
                u += w_in_units(layer, COL_GATE + 512 * g)
            for r in range(2):
                v = w_branch[layer, r, :, :].rearrange("(k p) n -> p k n", p=P)
                u += [v[:, 0:2, :], v[:, 2:4, :]]
            v = w_out[layer, :, :].rearrange("(k p) n -> p k n", p=P)
            u += [v[:, 2 * n:2 * n + 2, :] for n in range(4)]
            assert len(u) == MIX_UNITS
            return u

        def pass_order():
            o = []
            for c in range(NCHUNK):
                o += [("gate", c), ("up", c)]
                if c:
                    o.append(("down", c - 1))
            return o + [("down", NCHUNK - 1)]

        def split_of(j):
            return w_hi[:, j % SPLITS, :], w_lo[:, j % SPLITS, :]

        def pass_unit(wg, wu, wd, kind, c):
            cols = slice(c * FF_CHUNK, (c + 1) * FF_CHUNK)
            if kind == "down":
                return wd(cols).rearrange("(j p) n -> p j n", p=P)
            return (wg if kind == "gate" else wu)(cols).rearrange("(k p) n -> p k n", p=P)

        block = ctx.enter_context(nc.Block())

        @block.sync
        def _(sp):
            sp.dma_start(h[:, :, :], x[0, :, :].rearrange("(t p) n -> p t n", p=P)).then_inc(s_h, 16)
            for dst, src in [
                    (cst[:, 0:C_MASK], consts[:, 0:C_MASK]),
                    (rows[0:16, :], norm_mix.rearrange("l (k p) -> (l k) p", p=P)),
                    (rows[16:32, :], norm_ffn.rearrange("l (k p) -> (l k) p", p=P)),
                    (rows[32:128, :], conv_w.rearrange("l t (k p) -> (l t k) p", p=P)),
                    (wab[:, 0, :, :], w_in[0, :, COL_AB:COL_AB + 8].rearrange("(k p) n -> p k n", p=P)),
                    (alog[:, :], a_log.rearrange("(o l) n -> o (l n)", o=1).to_broadcast([P, DEPTH * H])),
                    (dtb[:, :], dt_bias.rearrange("(o l) n -> o (l n)", o=1).to_broadcast([P, DEPTH * H]))]:
                sp.dma_start(dst, src).then_inc(s_first, 16)

            def other_constants():
                for dst, src in [
                        (cst[:, C_MASK:C_COLS], consts[:, C_MASK:C_COLS]),
                        (gnorm[:, :, :].rearrange("p l n -> p (l n)"),
                         gdn_norm.rearrange("(o l) n -> o (l n)", o=1).to_broadcast([P, DEPTH * DH])),
                        (wab[:, 1, :, :], w_in[1, :, COL_AB:COL_AB + 8].rearrange("(k p) n -> p k n", p=P)),
                        (wrt[:, :, :], router[0, :, :].rearrange("(k p) n -> p k n", p=P))]:
                    sp.dma_start(dst, src).then_inc(s_const, 16)

            def load(i, src):
                slot, value, before = plan[i]
                if before is not None:
                    sp.wait_ge(lo_ready, before + 1)
                if MIX_UNITS + MIX_SLOTS <= i < MIX_UNITS + SLOTS:
                    sp.wait_ge(unit_used, MIX_UNITS)
                shape = ring[:, slot, :].rearrange("p (k n) -> p k n", k=src.shape[1])
                sp.dma_start(shape, src).then_inc(loaded[slot], 16)

            i = 0
            for layer in range(DEPTH):
                for src in mixer_units(layer):
                    if i == MIX_SLOTS:
                        other_constants()
                    load(i, src)
                    i += 1
                if layer == 0:
                    for kind, c in pass_order():
                        load(i, pass_unit(lambda s: dense_w_gate[0, :, s], lambda s: dense_w_up[0, :, s],
                                          lambda s: dense_w_down[0, s, :], kind, c))
                        i += 1
            assert i == STATIC_UNITS

            def expert_round(rnd):
                with sp.Fori(0, NEXP) as e:
                    for j, (kind, c) in enumerate(pass_order()):
                        i = STATIC_UNITS + rnd * NEXP * PASS_UNITS + j
                        src = pass_unit(lambda s: moe_w_gate[0, e, :, s], lambda s: moe_w_up[0, e, :, s],
                                        lambda s: moe_w_down[0, e, s, :], kind, c)
                        sp.wait_ge(lo_ready, e * PASS_UNITS + (i - SLOTS + 1))
                        shape = ring[:, j % SLOTS, :].rearrange("p (k n) -> p k n", k=src.shape[1])
                        sp.dma_start(shape, src).then_inc(loaded[j % SLOTS], 16)

            sp.wait_ge(unit_used, STATIC_UNITS)
            expert_round(0)
            sp.wait_ge(over_ready, 1)
            with sp.If(sp.value_load(over_i[0:1, 0:1], min_val=0, max_val=1)):
                expert_round(1)

            for t in range(NT):
                sp.wait_ge(s_final, t + 1)
                sp.dma_start(out[0, t * P:(t + 1) * P, :], hs[:, t, :]).then_inc(s_out, 16)
            sp.wait_ge(s_out, 16 * NT)

        @block.tensor
        def _(pe):
            mm = nc.tensor.matmul
            used = [0]

            def product(dst, xh, xl, yh, yl, start, stop):
                mm(dst, xh, yh, start=start, stop=False)
                mm(dst, xh, yl, start=False, stop=False)
                return mm(dst, xl, yh, start=False, stop=stop)

            def w(layer, name, k):
                pe.wait_ge(S[name], upto(layer, name, k))

            def norm_transposes(layer, n):
                w(layer, "hs_ready", 2 * n + 1)
                for m in range(4):
                    for k in (2 * m, 2 * m + 1):
                        for t in range(NT):
                            last = nc.tensor.transpose(ps[m][:, (k % 2) * SEQ + t * P:(k % 2) * SEQ + (t + 1) * P],
                                                       hs[:, t, k * P:(k + 1) * P], ident)
                    last.then_inc(S["hT_ps"], 1)

            def proj_block(layer, base, n, t, bank):
                tok = slice(t * P, (t + 1) * P)
                for k in range(KD):
                    if t == 0 and k % 4 == 0:
                        pe.wait_ge(lo_ready, base + n + k // 4 + 1)
                    vh, vl = mixer_split(n + k // 4, 4)
                    m = product(ps[bank][:, :], mx_hi[:, k, tok], mx_lo[:, k, tok],
                                vh[:, k % 4, :], vl[:, k % 4, :], k == 0, k == KD - 1)
                    if t == 1 and k in (3, 7):
                        m.then_inc(unit_used, 1)
                    elif k == KD - 1:
                        m.then_inc(S["proj_first"], 1)

            def mixer(layer, base):
                norm_transposes(layer, 0)
                w(layer, "hnT_ready", 3)
                for t in range(NT):
                    for k in range(KD):
                        last = mm(ps[6][:, 8 * t:8 * t + 8], hnT[:, k, t * P:(t + 1) * P], wab[:, layer, k, :],
                                  start=(k == 0), stop=(k == KD - 1))
                last.then_inc(S["ab_ps"], 1)
                w(layer, "mx_lo", 3)
                for g in range(CONV_GROUPS):
                    for ct in range(4):
                        for k in range(KD):
                            n = 2 * g + k // 4
                            if ct == 0 and k % 4 == 0:
                                pe.wait_ge(lo_ready, base + n + 1)
                            vh, vl = (v[:, k % 4, ct * P:(ct + 1) * P] for v in mixer_split(n, 4))
                            m = product(ps[2 * g + ct // 2][:, (ct % 2) * SEQ:(ct % 2 + 1) * SEQ], vh, vl,
                                        mx_hi[:, k, :], mx_lo[:, k, :], k == 0, k == KD - 1)
                            if ct == 3 and k in (3, 7):
                                m.then_inc(unit_used, 1)
                    if g == 0:
                        w(layer, "g_ready", 0)
                        mm(ps[6][:, 64:64 + TH], tri, gcol, start=True, stop=True).then_inc(S["gc_ps"], 1)
                w(layer, "sq_ready", 1)
                for g in range(2):
                    for t in range(NT):
                        for hh in range(H):
                            c = 32 + g * TH + t * H + hh
                            last = mm(ps[7][:, c:c + 1], sq[:, g, hh, t * P:(t + 1) * P], ones[:, 0:1],
                                      start=True, stop=True)
                last.then_inc(S["ssq_ps"], 1)
                w(layer, "trig_ready", 0)
                w(layer, "conv_out", 0)
                for t in range(NT):
                    mm(ps[t][:, :], ones, einv[:, 4 * t:4 * t + 4, :].rearrange("p a b -> p (a b)"),
                       start=True, stop=True).then_inc(S["bc_ps"], 1)
                w(layer, "conv_out", 1)
                for t in range(NT):
                    for hh in range(H):
                        kt = qkvT[:, 4 + hh, t * P:(t + 1) * P]
                        last = mm(ps[2 + t][:, hh * P:(hh + 1) * P], kt, kt, start=True, stop=True)
                    last.then_inc(S["kk_ps"], 1)
                w(layer, "rr_in", 0)
                for hh in range(H):
                    last = nc.tensor.transpose(ps[7][:, hh * P:(hh + 1) * P], qkvT[:, 4 + hh, 0:P], ident)
                last.then_inc(S["ktok_ps"], 1)
                fill = [(g, t) for g in range(len(FILL_GROUPS)) for t in range(NT)]
                fill_base = 2 * CONV_GROUPS
                free = {0: "rope_done", 1: "rope_done", 2: "rv_done", 3: "rg_done"}

                def filler(bank=None):
                    if not fill:
                        return
                    g, t = fill.pop(0)
                    if g == 0 and bank is None:
                        w(layer, "dec_beta", 1)
                    elif g:
                        name = free[g - 1]
                        w(layer, name, (2 * (g - 1) if name == "rope_done" else 0) + t)
                    proj_block(layer, base, fill_base + 2 * g, t, t if bank is None else bank)

                w(layer, "dec_arg", 0)
                filler(6)
                w(layer, "diagc_ready", 0)
                for t in range(NT):
                    mm(ps[t][:, :], ones, umask[:, 4 * t:4 * t + 4, :].rearrange("p a b -> p (a b)"),
                       start=True, stop=True).then_inc(S["bcc_ps"], 1)
                w(layer, "conv_out", 2)
                for t in range(NT):
                    for hh in range(H):
                        last = mm(ps[4 + t][:, hh * P:(hh + 1) * P], qkvT[:, 4 + hh, t * P:(t + 1) * P],
                                  qkvT[:, hh, t * P:(t + 1) * P], start=True, stop=True)
                    last.then_inc(S["qk_ps"], 1)
                w(layer, "e1_ready", 0)
                w(layer, "un_ready", 1)
                for t in range(NT):
                    for hh in range(H):
                        last = nc.tensor.transpose(ps[2 + t][:, hh * P:(hh + 1) * P], einv[:, 4 * t + hh, :], ident)
                    last.then_inc(S["d1_ps"], 1)
                w(layer, "qkv_act", 2)
                w(layer, "attn_ready", 1)
                for t in range(NT):
                    for hh in range(H):
                        last = nc.tensor.transpose(ps[4 + t][:, hh * P:(hh + 1) * P],
                                                   qkvT[:, 8 + hh, t * P:(t + 1) * P], ident)
                    last.then_inc(S["vtok_ps"], 1)
                for lv in range(1, len(LEVELS)):
                    n = 2 * (lv - 1)
                    w(layer, "umask_ready", lv - 1)
                    for t in range(NT):
                        if lv == 1:
                            w(layer, "d1_ready", t)
                        else:
                            w(layer, "de_ready", n - 2 + t)
                        for hh in range(H):
                            a = 4 * t + hh
                            last = mm(ps[2 + t][:, hh * P:(hh + 1) * P], umask[:, a, :], dinv[:, a, :],
                                      start=True, stop=True)
                        last.then_inc(S["p_ps"], 1)
                    filler()
                    for t in range(NT):
                        w(layer, "p_ready", n + t)
                        if lv == 1:
                            w(layer, "bv_ready", t)
                            w(layer, "kdec_ready", 0)
                            w(layer, "rope_done", 0)
                        if lv < len(LEVELS) - 1:
                            for hh in range(H):
                                a = 4 * t + hh
                                mm(ps[4 + t][:, hh * P:(hh + 1) * P], einv[:, a, :], prod[:, a, :],
                                   start=True, stop=True)
                        for hh in range(H):
                            a = 4 * t + hh
                            last = mm(ps[6 + t][:, hh * P:(hh + 1) * P], prod[:, a, :], einv[:, a, :],
                                      start=True, stop=True)
                        last.then_inc(S["de_ps"], 1)
                    filler()
                assert not fill
                w(layer, "de_ready", 10)
                w(layer, "bv_ready", 1)
                for hh in range(H):
                    last = mm(ps[2][:, hh * P:(hh + 1) * P], einv[:, hh, :], bv[:, 0, hh * P:(hh + 1) * P],
                              start=True, stop=True)
                last.then_inc(S["vn_ps"], 1)
                w(layer, "rope_done", 3)
                w(layer, "gz_half", 1)
                for hh in range(H):
                    for t in range(NT):
                        last = nc.tensor.transpose(
                            ps[hh // 2][:, (hh % 2) * SEQ + t * P:(hh % 2) * SEQ + (t + 1) * P],
                            rrot[:, 0, t, hh * P:(hh + 1) * P], ident)
                last.then_inc(S["rqT_ps"], 1)
                w(layer, "vn_ready", 0)
                w(layer, "kdec_ready", 0)
                for hh in range(H):
                    last = mm(ps[3][:, hh * P:(hh + 1) * P], kdec[:, hh, :], vnew[:, 0, hh * P:(hh + 1) * P],
                              start=True, stop=True)
                last.then_inc(S["st_ps"], 1)
                for hh in range(H):
                    for t in range(NT):
                        last = nc.tensor.transpose(
                            ps[4 + hh // 2][:, (hh % 2) * SEQ + t * P:(hh % 2) * SEQ + (t + 1) * P],
                            rrot[:, 1, t, hh * P:(hh + 1) * P], ident)
                last.then_inc(S["rkT_ps"], 1)
                w(layer, "st_ready", 0)
                for hh in range(H):
                    last = mm(ps[2][:, hh * P:(hh + 1) * P], qkvT[:, 4 + hh, P:SEQ], state[:, hh, :],
                              start=True, stop=True)
                last.then_inc(S["ks_ps"], 1)
                w(layer, "rqT_ready", 0)
                w(layer, "rkT_ready", 0)
                for hh in range(H):
                    last = mm(ps[hh // 2][:, (hh % 2) * SEQ:(hh % 2 + 1) * SEQ], rT[:, 1, hh, 0:P], rT[:, 0, hh, :],
                              start=True, stop=True)
                    if hh % 2:
                        last.then_inc(S["s_ps"], 1)
                for hh in range(H):
                    last = mm(ps[3][:, hh * P:(hh + 1) * P], rT[:, 1, hh, P:SEQ], rT[:, 0, hh, P:SEQ],
                              start=True, stop=True)
                last.then_inc(S["s_ps"], 1)
                for hh in range(H):
                    last = mm(ps[5][:, hh * P:(hh + 1) * P], qkvT[:, hh, P:SEQ], state[:, hh, :],
                              start=True, stop=True)
                last.then_inc(S["qs_ps"], 1)
                w(layer, "rhs1_ready", 0)
                w(layer, "de_ready", 11)
                for hh in range(H):
                    last = mm(ps[4][:, hh * P:(hh + 1) * P], einv[:, 4 + hh, :], rhs1[:, hh * P:(hh + 1) * P],
                              start=True, stop=True)
                last.then_inc(S["vn_ps"], 1)
                w(layer, "s_ready", 2)
                w(layer, "rv_done", 1)
                for t in range(NT):
                    for hh in range(H):
                        c = slice(hh * P, (hh + 1) * P)
                        last = mm(ps[t][:, c], st0[:, hh, t * P:(t + 1) * P], rv[:, 0, c],
                                  start=True, stop=(t == 0))
                        if t == 1:
                            last = mm(ps[t][:, c], st1[:, hh, :], rv[:, 1, c], start=False, stop=True)
                    last.then_inc(S["ro_ps"], 1)
                for t in range(NT):
                    w(layer, "vn_ready", t)
                    for hh in range(H):
                        c = slice(hh * P, (hh + 1) * P)
                        last = mm(ps[6 + t][:, c], attnT[:, 4 * t + hh, :], vnew[:, t, c], start=True, stop=True)
                    last.then_inc(S["go_ps"], 1)
                n = fill_base + 2 * len(FILL_GROUPS)
                w(layer, "rhs1_ready", 0)
                for g in range(GATE_GROUPS):
                    for t in range(NT):
                        if g:
                            w(layer, "gate_done", 2 * (g - 1) + t)
                        proj_block(layer, base, n + 2 * g, t, 2 + t)
                w(layer, "qs_done", 0)
                for r, src in enumerate((o_ret, o_gdn)):
                    w(layer, "br_ready", r)
                    for hh in range(H):
                        for t in range(NT):
                            last = nc.tensor.transpose(
                                ps[4 + 2 * r + hh // 2][:, (hh % 2) * SEQ + t * P:(hh % 2) * SEQ + (t + 1) * P],
                                src[:, t, hh * P:(hh + 1) * P], ident)
                    last.then_inc(S["rt_ps"], 1)
                n += 2 * GATE_GROUPS
                w(layer, "gate_done", 7)
                w(layer, "br_lo", 1)
                for r in range(2):
                    for half in range(2):
                        pe.wait_ge(lo_ready, base + n + 1)
                        vh, vl = mixer_split(n, 2)
                        for k in (2 * half, 2 * half + 1):
                            for t in range(NT):
                                tok = slice(t * P, (t + 1) * P)
                                for f in range(2):
                                    col = slice(f * 512, (f + 1) * 512)
                                    last = product(ps[4 * r + 2 * t + f][:, :], br_hi[:, r, k, tok],
                                                   br_lo[r][:, k, tok], vh[:, k % 2, col], vl[:, k % 2, col],
                                                   k == 0, k == 3)
                        last.then_inc(unit_used, 1)
                        n += 1
                w(layer, "m_ready", 1)
                for m in range(4):
                    for k in (2 * m, 2 * m + 1):
                        for t in range(NT):
                            last = nc.tensor.transpose(ps[m][:, (k % 2) * SEQ + t * P:(k % 2) * SEQ + (t + 1) * P],
                                                       hs[:, t, k * P:(k + 1) * P], ident)
                    last.then_inc(S["mT_ps"], 1)
                for m in range(4):
                    w(layer, "mx_lo", 4 + m)
                    pe.wait_ge(lo_ready, base + n + 1)
                    vh, vl = mixer_split(n, 2)
                    for k in (2 * m, 2 * m + 1):
                        for t in range(NT):
                            tok = slice(t * P, (t + 1) * P)
                            for f in range(2):
                                col = slice(f * 512, (f + 1) * 512)
                                last = product(ps[4 + 2 * t + f][:, :], mx_hi[:, k, tok], mx_lo[:, k, tok],
                                               vh[:, k % 2, col], vl[:, k % 2, col], k == 0, k == KD - 1)
                    last.then_inc(unit_used, 1)
                    n += 1
                assert n == MIX_UNITS

            def dense_pass(base):
                pe.wait_ge(x_lo_ready, 4)
                for j, (kind, c) in enumerate(pass_order()):
                    pe.wait_ge(lo_ready, base + j + 1)
                    wh, wl = split_of(j)
                    if kind == "down":
                        pe.wait_ge(act_lo_ready, c + 1)
                        vh, vl = (v.rearrange("p (j n) -> p j n", j=2) for v in (wh, wl))
                        for jj in range(2):
                            for t in range(NT):
                                tok = slice(t * P, (t + 1) * P)
                                for f in range(2):
                                    col = slice(f * 512, (f + 1) * 512)
                                    last = product(ps[4 + 2 * t + f][:, :], act_hi[:, c % 2, jj, tok],
                                                   act_lo[:, c % 2, jj, tok], vh[:, jj, col], vl[:, jj, col],
                                                   c == 0 and jj == 0, c == NCHUNK - 1 and jj == 1)
                    else:
                        n = 2 * (c % 2) + (kind == "up")
                        if c >= 2:
                            pe.wait_ge(ffn_act, c - 1)
                        vh, vl = (v.rearrange("p (k n) -> p k n", k=KD) for v in (wh, wl))
                        for jj in range(2):
                            ff = slice(jj * P, (jj + 1) * P)
                            for k in range(KD):
                                last = product(ps[n][:, jj * SEQ:(jj + 1) * SEQ], vh[:, k, ff], vl[:, k, ff],
                                               x_hi[:, k, :], x_lo[:, k, :], k == 0, k == KD - 1)
                    last.then_inc(unit_used, 1)

            def gather():
                for k in range(KD):
                    for t in range(NT):
                        dst, col = ps[6 + k // 4][:, (k % 4) * P:(k % 4 + 1) * P], slice(k * P, (k + 1) * P)
                        mm(dst, hs_hi[:, t, col], gsel[:, t, :], start=(t == 0), stop=False)
                        last = mm(dst, hs_lo[:, t, col], gsel[:, t, :], start=False, stop=(t == NT - 1))
                    if k % 4 == 3:
                        last.then_inc(xg_ps, 1)
                for t in range(NT):
                    last = nc.tensor.transpose(ps[1][:, t * P:(t + 1) * P], gsel[:, t, :].bitcast(f32), ident)
                last.then_inc(gt_ps, 1)

            def transpose_act(q, c):
                pe.wait_ge(ffn_act, q * NCHUNK + NCHUNK + c + 1)
                if c >= 2:
                    pe.wait_ge(aT_lo_ready, q * NCHUNK + c - 1)
                for jj in range(2):
                    last = nc.tensor.transpose(ps[6 + c % 2][:, jj * P:(jj + 1) * P],
                                               a_tok[:, c % 2, jj * P:(jj + 1) * P], ident)
                last.then_inc(aT_ps, 1)

            def expert_pass(rnd, e, final):
                q = e + rnd * NEXP
                pe.wait_ge(xg_lo_ready, 2 * q + 2)
                pe.wait_ge(gt_ready, q + 1)
                for j, (kind, c) in enumerate(pass_order()):
                    if kind == "down" and c == NCHUNK - 1:
                        transpose_act(q, c)
                    pe.wait_ge(lo_ready, q * PASS_UNITS + STATIC_UNITS + j + 1)
                    wh, wl = split_of(j)
                    if kind == "down":
                        pe.wait_ge(aT_lo_ready, q * NCHUNK + c + 1)
                        if c == 0:
                            pe.wait_ge(moe_drained, q * 2 + 1)
                        vh, vl = (v.rearrange("p (j n) -> p j n", j=2) for v in (wh, wl))
                        for jj in range(2):
                            for f in range(2):
                                col = slice(f * 512, (f + 1) * 512)
                                last = product(ps[4 + f][:, :], actT_hi[:, c % 2, jj, :], actT_lo[:, c % 2, jj, :],
                                               vh[:, jj, col], vl[:, jj, col],
                                               c == 0 and jj == 0, c == NCHUNK - 1 and jj == 1)
                    else:
                        n = 2 * (c % 2) + (kind == "up")
                        if kind == "gate":
                            pe.wait_ge(ffn_act, q * NCHUNK + NCHUNK + c - 1)
                            if c == 1:
                                pe.wait_ge(moe_drained, q * 2 + 1)
                        vh, vl = (v.rearrange("p (k n) -> p k n", k=KD) for v in (wh, wl))
                        for k in range(KD):
                            last = product(ps[n][:, 0:FF_CHUNK], xg_hi[:, k, :], xg_lo[:, k, :],
                                           vh[:, k, :], vl[:, k, :], k == 0, k == KD - 1)
                    last.then_inc(unit_used, 1)
                    if kind == "gate" and c:
                        transpose_act(q, c - 1)
                if not final:
                    pe.wait_ge(g_built, q + 2)
                    gather()
                pe.wait_ge(y_lo_ready, q * 2 + 2)
                for t in range(NT):
                    for f in range(2):
                        dst, col = ps[4 - 2 * t + f][:, :], slice(f * 512, (f + 1) * 512)
                        mm(dst, gselT[:, t, :], y_hi[:, col], start=True, stop=False)
                        last = mm(dst, gselT[:, t, :], y_lo[:, col], start=False, stop=True)
                    last.then_inc(sc_ps, 1)

            def expert_round(rnd):
                pe.wait_ge(hs_lo_ready, 4)
                pe.wait_ge(g_built, rnd * NEXP + 1)
                gather()
                with pe.Fori(0, NEXP - 1) as e:
                    expert_pass(rnd, e, False)
                expert_pass(rnd, NEXP - 1, True)

            pe.wait_ge(s_first, 16 * N_FIRST)
            nc.tensor.transpose(ps[7][:, 0:P], rows[:, :], ident).then_inc(s_par_ps, 1)
            mixer(0, 0)
            norm_transposes(0, 1)
            w(0, "hnT_ready", 7)
            pe.wait_ge(s_const, 16 * N_CONST)
            dense_pass(MIX_UNITS)
            mixer(1, LAYER0_UNITS)
            norm_transposes(1, 1)
            w(1, "hnT_ready", 7)
            for t in range(NT):
                for k in range(KD):
                    last = mm(ps[0][:, t * 8:(t + 1) * 8], hnT[:, k, t * P:(t + 1) * P], wrt[:, k, :],
                              start=(k == 0), stop=(k == KD - 1))
            last.then_inc(router_ps, 1)
            for t in range(NT):
                for m in range(2):
                    for k in range(4 * m, 4 * m + 4):
                        last = nc.tensor.transpose(ps[2 + 2 * t + m][:, (k % 4) * P:(k % 4 + 1) * P],
                                                   hnT[:, k, t * P:(t + 1) * P], ident)
                    last.then_inc(hs_ps, 1)
            pe.wait_ge(sel_ready, 1)
            mm(ps[0][:, 0:NEXP], tri, selm[:, 0:NEXP], start=True, stop=True)
            mm(ps[0][:, NEXP:2 * NEXP], tri, selm[:, NEXP:2 * NEXP], start=True, stop=False)
            mm(ps[0][:, NEXP:2 * NEXP], ones, selm[:, 0:NEXP], start=False, stop=True)
            mm(ps[0][:, 2 * NEXP:3 * NEXP], ones, selm[:, 0:NEXP], start=True, stop=False)
            mm(ps[0][:, 2 * NEXP:3 * NEXP], ones, selm[:, NEXP:2 * NEXP], start=False, stop=True).then_inc(pos_ps, 1)
            expert_round(0)
            pe.wait_ge(over_ready, 1)
            with pe.If(pe.value_load(over_i[0:1, 0:1], min_val=0, max_val=1)):
                expert_round(1)

        @block.scalar
        def _(act):
            go = nc.scalar.activation

            def w(layer, name, k):
                act.wait_ge(S[name], upto(layer, name, k))

            def scale_rows(layer, n):
                for t in range(NT):
                    w(layer, "rstd", n)
                    go(hs[:, t, :], h[:, t, :], ACT.Copy, scale=rs[:, t:t + 1]).then_inc(S["hs_ready"], 1)

            def mixer(layer, base):
                n_split = [0]

                def split_upto(n):
                    while n_split[0] <= n:
                        i = base + n_split[0]
                        slot, value, _ = plan[i]
                        act.wait_ge(loaded[slot], value)
                        if i >= SPLITS:
                            act.wait_ge(unit_used, i - SPLITS + 1)
                        if n_split[0] < SPLITS and base:
                            act.wait_ge(unit_used, base)
                        go(m_hi[:, n_split[0] % SPLITS, :], ring[:, slot, :], ACT.Copy).then_inc(hi_ready, 1)
                        n_split[0] += 1

                if layer:
                    split_upto(0)
                scale_rows(layer, 0)
                split_upto(1)
                for m in range(4):
                    w(layer, "hnT_ready", m)
                    go(mx_hi[:, 2 * m:2 * m + 2, :], hnT[:, 2 * m:2 * m + 2, :], ACT.Copy).then_inc(S["mx_hi"], 1)
                split_upto(2)
                w(layer, "gat_in", 0)
                go(e1, nx, ACT.Exp)
                go(tb, ps[6][:, 0:16].rearrange("p (t n) -> p t n", t=NT)[:, :, 4:8], ACT.Tanh,
                   scale=0.5).then_inc(S["gat_e"], 1)
                for g in range(CONV_GROUPS):
                    split_upto(2 * g + 3)
                    act.wait_ge(unit_used, base + 2 * g + 2)
                    split_upto(2 * g + 4)
                    for ct in range(4):
                        col = 32 + layer * 48 + 3 * 12 + 4 * g + ct
                        go(qkvT[:, 4 * g + ct, :], ps[2 * g + ct // 2][:, (ct % 2) * SEQ:(ct % 2 + 1) * SEQ],
                           ACT.Copy, scale=par[:, col:col + 1]).then_inc(S["tap0"], 1)
                    if g == 2:
                        w(layer, "dec_arg", 0)
                        go(decay, decay, ACT.Exp).then_inc(S["dec_exp"], 1)
                        w(layer, "kd_in", 0)
                        go(kdfac, kdarg, ACT.Exp).then_inc(S["dec_exp"], 1)
                        go(eg, gcs[:, H:TH], ACT.Exp).then_inc(S["dec_exp"], 1)
                    w(layer, "conv_out", g)
                    if g:
                        w(layer, "qkv_act", g - 1)
                    go(th[:, :, :].rearrange("p a b -> p (a b)"),
                       qkvT[:, 4 * g:4 * g + 4, :].rearrange("p a b -> p (a b)"), ACT.Tanh,
                       scale=0.5).then_inc(S["th_conv"], 1)
                for t in range(NT):
                    w(layer, "d1_ps", t)
                    go(dinv[:, 4 * t:4 * t + 4, :].rearrange("p a b -> p (a b)"), ps[2 + t][:, :],
                       ACT.Copy).then_inc(S["d1_ready"], 1)
                fill = [(g, t) for g in range(len(FILL_GROUPS)) for t in range(NT)]

                def filler():
                    if not fill:
                        return
                    g, t = fill.pop(0)
                    split_upto(2 * (CONV_GROUPS + g) + 2 + t)
                    if g < 2:
                        return
                    if t == 0:
                        w(layer, "proj_first", g)
                    else:
                        act.wait_ge(unit_used, base + 2 * CONV_GROUPS + 2 * g + 2)
                    if g == 2:
                        go(rv[:, t, :], ps[t][:, :], ACT.Copy).then_inc(S["rv_done"], 1)
                    else:
                        n = 2 * (g - 3) + t
                        w(layer, "rope_done" if g == 3 else "rg_done", 3 if g == 3 else t)
                        go(th[:, t, :], ps[t][:, :], ACT.Tanh, scale=0.5).then_inc(S["th_g"], 1)

                filler()
                for lv in range(1, len(LEVELS)):
                    for t in range(NT):
                        n = 2 * (lv - 1) + t
                        w(layer, "p_ps", n)
                        if n >= 2:
                            w(layer, "de_ps", n - 2)
                        go(prod[:, 4 * t:4 * t + 4, :].rearrange("p a b -> p (a b)"), ps[2 + t][:, :],
                           ACT.Copy).then_inc(S["p_ready"], 1)
                    filler()
                    filler()
                w(layer, "vn_ps", 0)
                go(vnew[:, 0, :], ps[2][:, :], ACT.Copy).then_inc(S["vn_ready"], 1)
                w(layer, "rqT_ps", 0)
                go(rT[:, 0, 0:2, :], quad(ps[0][:, :], 2), ACT.Copy)
                go(rT[:, 0, 2:4, :], quad(ps[1][:, :], 2), ACT.Copy).then_inc(S["rqT_ready"], 1)
                w(layer, "st_ps", 0)
                go(state[:, :, :], quad(ps[3][:, :]), ACT.Copy).then_inc(S["st_ready"], 1)
                w(layer, "rkT_ps", 0)
                go(rT[:, 1, 0:2, :], quad(ps[4][:, :], 2), ACT.Copy)
                go(rT[:, 1, 2:4, :], quad(ps[5][:, :], 2), ACT.Copy).then_inc(S["rkT_ready"], 1)
                w(layer, "vn_ps", 1)
                go(vnew[:, 1, :], ps[4][:, :], ACT.Copy).then_inc(S["vn_ready"], 1)
                w(layer, "go_ps", 1)
                for g in range(GATE_GROUPS):
                    for t in range(NT):
                        split_upto(2 * (CONV_GROUPS + len(FILL_GROUPS) + g) + 2 + t)
                        if t == 0:
                            w(layer, "proj_first", 5 + g)
                        else:
                            act.wait_ge(unit_used, base + 2 * (CONV_GROUPS + len(FILL_GROUPS) + g) + 2)
                        go(gates[:, t, g * 512:(g + 1) * 512], ps[2 + t][:, :], ACT.Tanh,
                           scale=0.5).then_inc(S["gate_done"], 1)
                for r in range(2):
                    w(layer, "rt_ps", r)
                    go(br_hi[:, r, 0:2, :], quad(ps[4 + 2 * r][:, :], 2), ACT.Copy)
                    go(br_hi[:, r, 2:4, :], quad(ps[5 + 2 * r][:, :], 2), ACT.Copy).then_inc(S["br_hi"], 1)
                split_upto(30)
                for m in range(4):
                    w(layer, "mT_ps", m)
                    go(mx_hi[:, 2 * m:2 * m + 2, :], quad(ps[m][:, :], 2), ACT.Copy).then_inc(S["mx_hi"], 1)
                split_upto(31)

            def split_high(off, j, load_value):
                act.wait_ge(loaded[j % SLOTS], load_value)
                act.wait_ge(unit_used, off + (j - SPLITS + 1))
                go(split_of(j)[0], ring[:, j % SLOTS, :], ACT.Copy).then_inc(hi_ready, 1)

            def dense_load_value(j):
                return plan[MIX_UNITS + j][1]

            def dense_pass(base):
                for m in range(4):
                    w(0, "hnT_ready", 4 + m)
                    go(x_hi[:, 2 * m:2 * m + 2, :], hnT[:, 2 * m:2 * m + 2, :], ACT.Copy).then_inc(x_hi_ready, 1)
                for j, (kind, c) in enumerate(pass_order()):
                    if kind == "gate":
                        act.wait_ge(unit_used, base + j + 1)
                        if c >= 2:
                            act.wait_ge(ffn_a1, c - 1)
                        go(th_f[:, c % 2, :], ps[2 * (c % 2)][:, :], ACT.Tanh, scale=0.5).then_inc(ffn_th, 1)
                    elif kind == "up":
                        act.wait_ge(ffn_act, c + 1)
                        if c == 0:
                            act.wait_ge(x_lo_ready, 4)
                        if c >= 2:
                            act.wait_ge(unit_used, base + pass_order().index(("down", c - 2)) + 1)
                        go(act_hi[:, c % 2, :, :].rearrange("p j n -> p (j n)"), a1[:, c % 2, :],
                           ACT.Copy).then_inc(act_hi_ready, 1)
                    if j + SPLITS < PASS_UNITS:
                        split_high(base, j + SPLITS, dense_load_value(j + SPLITS))

            def copy_actT(q, c):
                act.wait_ge(aT_ps, q * NCHUNK + c + 1)
                if c >= 2:
                    act.wait_ge(unit_used, q * PASS_UNITS + STATIC_UNITS + pass_order().index(("down", c - 2)) + 1)
                go(actT_hi[:, c % 2, :, :], quad(ps[6 + c % 2][:, 0:2 * P], 2), ACT.Copy).then_inc(aT_hi_ready, 1)

            def copy_gathered(g):
                for m in range(2):
                    act.wait_ge(xg_ps, g * 2 + m + 1)
                    go(xg_hi[:, 4 * m:4 * m + 4, :], quad(ps[6 + m][:, :]), ACT.Copy).then_inc(xg_hi_ready, 1)

            def copy_gselT(g):
                act.wait_ge(gt_ps, g + 1)
                go(gselT[:, :, :], quad(ps[1][:, 0:NT * P], NT), ACT.Copy).then_inc(gt_ready, 1)

            def expert_pass(rnd, e, final):
                q = e + rnd * NEXP
                off = q * PASS_UNITS + STATIC_UNITS
                for j, (kind, c) in enumerate(pass_order()):
                    if kind == "gate":
                        act.wait_ge(unit_used, off + j + 1)
                        act.wait_ge(ffn_a1, q * NCHUNK + NCHUNK + c - 1)
                        go(th_f[:, c % 2, 0:FF_CHUNK], ps[2 * (c % 2)][:, 0:FF_CHUNK], ACT.Tanh,
                           scale=0.5).then_inc(ffn_th, 1)
                        if c:
                            copy_actT(q, c - 1)
                    elif (kind, c) == ("down", NCHUNK - 2):
                        copy_actT(q, NCHUNK - 1)
                    elif (kind, c) == ("down", NCHUNK - 1):
                        act.wait_ge(unit_used, off + PASS_UNITS)
                        for f in range(2):
                            go(y_hi[:, f * 512:(f + 1) * 512], ps[4 + f][:, :], ACT.Copy).then_inc(y_hi_ready, 1)
                        if not final:
                            copy_gathered(q + 1)
                    if j + SPLITS < PASS_UNITS:
                        split_high(off, j + SPLITS, expert_load_value(q, j + SPLITS))
                    elif not final:
                        jn = j + SPLITS - PASS_UNITS
                        split_high(off + PASS_UNITS, jn, expert_load_value(q + 1, jn))
                act.wait_ge(sc_ps, q * 2 + 2)
                if not final:
                    copy_gselT(q + 1)

            def expert_round(rnd):
                q = rnd * NEXP
                copy_gathered(q)
                if rnd:
                    for j in range(SPLITS):
                        split_high(q * PASS_UNITS + STATIC_UNITS, j, expert_load_value(q, j))
                copy_gselT(q)
                with act.Fori(0, NEXP - 1) as e:
                    expert_pass(rnd, e, False)
                expert_pass(rnd, NEXP - 1, True)

            act.wait_ge(s_first, 16 * N_FIRST)
            go(ea, alog[:, :], ACT.Exp).then_inc(s_ea, 1)
            act.wait_ge(s_par, 1)
            mixer(0, 0)
            act.wait_ge(unit_used, MIX_UNITS)
            split_high(MIX_UNITS, 0, dense_load_value(0))
            scale_rows(0, 1)
            split_high(MIX_UNITS, 1, dense_load_value(1))
            split_high(MIX_UNITS, 2, dense_load_value(2))
            dense_pass(MIX_UNITS)
            mixer(1, LAYER0_UNITS)
            act.wait_ge(unit_used, STATIC_UNITS)
            split_high(STATIC_UNITS, 0, expert_load_value(0, 0))
            scale_rows(1, 1)
            split_high(STATIC_UNITS, 1, expert_load_value(0, 1))
            split_high(STATIC_UNITS, 2, expert_load_value(0, 2))
            for t in range(NT):
                for m in range(2):
                    act.wait_ge(hs_ps, 2 * t + m + 1)
                    go(hs_hi[:, t, m * 512:(m + 1) * 512], ps[2 + 2 * t + m][:, :], ACT.Copy).then_inc(hs_hi_ready, 1)
            act.wait_ge(router_in, 1)
            go(pd, p0, ACT.Exp).then_inc(router_e, 1)
            act.wait_ge(hs_lo_ready, 4)
            act.dma_start(fnorm, final_norm.rearrange("(o n) -> o n", o=1).to_broadcast([P, DM])).then_inc(s_fnorm, 16)
            expert_round(0)
            act.wait_ge(over_ready, 1)
            with act.If(act.value_load(over_i[0:1, 0:1], min_val=0, max_val=1)):
                expert_round(1)

        @block.gpsimd
        def _(pool):
            tt, tsc = nc.gpsimd.tensor_tensor, nc.gpsimd.tensor_scalar
            n_chain = [0]

            def link(ins):
                n_chain[0] += 1
                ins.then_inc(pool_chain, 1)
                pool.wait_ge(pool_chain, n_chain[0])

            def w(layer, name, k):
                pool.wait_ge(S[name], upto(layer, name, k))

            def rstd(layer, n):
                w(layer, "sumsq", n)
                link(tsc(rs, ss, 1.0 / DM, EPS, ALU.mult, ALU.add))
                tt(rs, rs, mhalf[:, 0:NT], ALU.pow).then_inc(S["rstd"], 1)

            def mixer(layer, base):
                rstd(layer, 0)
                if layer == 0:
                    pool.wait_ge(s_first, 16 * N_FIRST)
                w(layer, "g_ready", 0)
                tt(einv, tiled(tri, TH), over(gcol, P), ALU.mult).then_inc(S["trig_ready"], 1)
                w(layer, "rr_in", 0)
                tt(rr, rr0, mhalf, ALU.pow).then_inc(S["rr_ready"], 1)
                w(layer, "rr_ready", 0)
                w(layer, "beta_ready", 0)
                link(tt(cneg, rr[:, TH:2 * TH], beta, ALU.mult))
                link(tsc(cneg, cneg, -1.0, None, ALU.mult))
                tt(umask[:, :, :], tiled(ident, TH), over(cneg, P), ALU.mult).then_inc(S["diagc_ready"], 1)
                w(layer, "un_ready", 1)
                w(layer, "bcc_ps", 1)
                if layer == 0:
                    pool.wait_ge(s_const, 16 * N_CONST)
                for lv in range(1, len(LEVELS)):
                    if lv > 1:
                        w(layer, "p_ps", 2 * (lv - 2) + 1)
                    tt(umask[:, :, :], un, tiled(cst[:, C_MASK + lv * P:C_MASK + (lv + 1) * P], TH),
                       ALU.mult).then_inc(S["umask_ready"], 1)
                for t in range(NT):
                    w(layer, "gz_half", t)
                    tt(quad(gzs[:, t, :]), quad(gzs[:, t, :]), tiled(gnorm[:, layer, :], H),
                       ALU.mult).then_inc(S["gz_done"], 1)
                w(layer, "rms_in", 0)
                tt(ors, oss, mhalf, ALU.pow).then_inc(S["rms_ready"], 1)

            pool.memset(mhalf, -0.5).then_inc(s_zero, 1)
            pool.wait_ge(s_zero, 1)
            for layer in range(DEPTH):
                mixer(layer, 0)
                rstd(layer, 1)
            pool.wait_ge(s_fin_ss, 1)
            link(tsc(rs, ss, 1.0 / DM, EPS, ALU.mult, ALU.add))
            tt(rs, rs, mhalf[:, 0:NT], ALU.pow).then_inc(s_fin_rs, 1)

        @block.vector
        def _(dve):
            V = nc.vector
            tt, tsc, stt = V.tensor_tensor, V.tensor_scalar, V.scalar_tensor_tensor
            n_chain = [0]

            def link(ins):
                n_chain[0] += 1
                ins.then_inc(dve_chain, 1)
                dve.wait_ge(dve_chain, n_chain[0])

            def sig(ins, name):
                return ins.then_inc(S[name], 1)

            def w(layer, name, k):
                dve.wait_ge(S[name], upto(layer, name, k))

            def sumsq(signal):
                for t in range(NT):
                    last = V.tensor_tensor_reduce(out=hs[:, t, :], in0=h[:, t, :], in1=h[:, t, :], scale=1.0,
                                                  scalar=0.0, op0=ALU.mult, op1=ALU.add, accum_out=ss[:, t:t + 1])
                last.then_inc(signal, 1)

            def norm(layer, n, between):
                sumsq(S["sumsq"])
                between()
                for m in range(4):
                    w(layer, "hT_ps", 4 * n + m)
                    col = 16 * n + layer * KD + 2 * m
                    sig(tt(hnT[:, 2 * m:2 * m + 2, :], quad(ps[m][:, :], 2), over(par[:, col:col + 2], SEQ),
                           ALU.mult), "hnT_ready")

            def mixer(layer, base):
                n_split = [0]

                def split_upto(n):
                    while n_split[0] <= n:
                        i = base + n_split[0]
                        dve.wait_ge(hi_ready, i + 1)
                        if i >= SPLITS:
                            dve.wait_ge(unit_used, i - SPLITS + 1)
                        if n_split[0] < SPLITS and base:
                            dve.wait_ge(unit_used, base)
                        b = n_split[0] % SPLITS
                        tt(m_lo[:, b, :], ring[:, plan[i][0], :], m_hi[:, b, :].bitcast(f32),
                           ALU.subtract).then_inc(lo_ready, 1)
                        n_split[0] += 1

                def between():
                    if layer == 0:
                        dve.wait_ge(s_par_ps, 1)
                        V.tensor_copy(par[:, :], ps[7][:, 0:P]).then_inc(s_par, 1)
                        dve.wait_ge(s_par, 1)
                    split_upto(1)

                norm(layer, 0, between)
                for m in range(4):
                    w(layer, "mx_hi", m)
                    w(layer, "hnT_ready", m)
                    sig(tt(mx_lo[:, 2 * m:2 * m + 2, :], hnT[:, 2 * m:2 * m + 2, :],
                           mx_hi[:, 2 * m:2 * m + 2, :].bitcast(f32), ALU.subtract), "mx_lo")
                split_upto(2)
                w(layer, "ab_ps", 0)
                ab = ps[6][:, 0:16].rearrange("p (t n) -> p t n", t=NT)
                dt2 = tiled(dtb[:, layer * H:(layer + 1) * H], NT)
                ea2 = tiled(ea[:, layer * H:(layer + 1) * H], NT)
                gx2 = quad(gx, NT)
                link(tt(gx2, ab[:, :, 0:H], dt2, ALU.add))
                link(tsc(nx, gx, -1.0, None, ALU.mult))
                sig(tt(nx, nx, gx, ALU.min), "gat_in")
                w(layer, "gat_e", 0)
                link(tsc(beta, tb, 0.5, 0.5, ALU.mult, ALU.add))
                link(tsc(hbeta, beta, 0.5, None, ALU.mult))
                link(tsc(den, e1, 2.0, None, ALU.add))
                link(V.reciprocal(den, den))
                link(tt(s1, e1, den, ALU.mult))
                link(tt(s2, s1, s1, ALU.mult))
                link(tsc(poly, s2, 1.0 / 19, None, ALU.mult))
                for k in range(8, 0, -1):
                    link(stt(poly, poly, 1.0 / (2 * k + 1), s2, ALU.add, ALU.mult))
                link(stt(poly, poly, 1.0, s1, ALU.add, ALU.mult))
                link(tsc(sp, gx, 0.0, None, ALU.max))
                link(stt(sp, poly, 2.0, sp, ALU.mult, ALU.add))
                if layer == 0:
                    dve.wait_ge(s_ea, 1)
                sig(stt(quad(gcol, NT), quad(sp, NT), -1.0, ea2, ALU.mult, ALU.mult), "g_ready")
                w(layer, "g_ready", 0)
                sig(V.tensor_copy(hbeta, hbeta), "beta_ready")
                def conv(g):
                    for s in range(1, CONV_K):
                        for ct in range(4):
                            n = 4 * g + ct
                            if s == 1 and ct % 2 == 0:
                                w(layer, "tap0", n + 1)
                            col = 32 + layer * 48 + (3 - s) * 12 + n
                            src = ps[2 * g + ct // 2][:, (ct % 2) * SEQ:(ct % 2 + 1) * SEQ - s]
                            ins = stt(qkvT[:, n, s:SEQ], src, par[:, col:col + 1], qkvT[:, n, s:SEQ],
                                      ALU.mult, ALU.add)
                        if s < CONV_K - 1:
                            link(ins)
                        else:
                            sig(ins, "conv_out")

                def silu(g):
                    w(layer, "th_conv", g)
                    w(layer, "conv_out", g)
                    grp = qkvT[:, 4 * g:4 * g + 4, :].rearrange("p a b -> p (a b)")
                    sig(stt(grp, th[:, :, :].rearrange("p a b -> p (a b)"), 1.0, grp, ALU.add, ALU.mult),
                        "qkv_act")
                    if g < 2:
                        w(layer, "qkv_act", g)
                        sig(tt(sq[:, g, :, :].rearrange("p a b -> p (a b)"), grp, grp, ALU.mult), "sq_ready")

                for g in range(2):
                    split_upto(2 * g + 3)
                    split_upto(2 * g + 4)
                    conv(g)
                    silu(g)
                split_upto(7)
                w(layer, "ssq_ps", 0)
                sig(tsc(rr0, ps[7][:, 32:48], 4 * EPS, None, ALU.add), "rr_in")
                w(layer, "gc_ps", 0)
                link(V.tensor_copy(gcs, ps[6][:, 64:64 + TH]))
                link(tsc(ngc, gcs, -1.0, None, ALU.mult))
                for t in range(NT):
                    w(layer, "bc_ps", t)
                    for hh in range(H):
                        a = 4 * t + hh
                        last = tsc(decay[:, a, :], ps[t][:, hh * P:(hh + 1) * P], ngc[:, a:a + 1], 0.0,
                                   ALU.add, ALU.min)
                    if t == 0:
                        sig(tt(kdarg, quad(ps[0][:, :])[:, :, P - 1], gcs[:, 0:H], ALU.subtract), "kd_in")
                sig(last, "dec_arg")
                conv(2)
                split_upto(8)
                w(layer, "dec_exp", 2)
                sig(tt(decay, decay, tiled(tri, TH), ALU.mult), "decay_ready")
                w(layer, "decay_ready", 0)
                w(layer, "rr_ready", 0)
                w(layer, "ktok_ps", 0)
                w(layer, "diagc_ready", 0)
                for t in range(NT):
                    w(layer, "bcc_ps", t)
                    sig(tt(quad(attnT[:, 4 * t:4 * t + 4, :].rearrange("p a b -> p (a b)")),
                           quad(ps[t][:, :]), decay[:, 4 * t:4 * t + 4, :], ALU.mult), "dec_beta")
                for t in range(NT):
                    w(layer, "kk_ps", t)
                    w(layer, "dec_beta", t)
                    for hh in range(H):
                        a = 4 * t + hh
                        last = stt(un[:, a, :], ps[2 + t][:, hh * P:(hh + 1) * P], rr[:, TH + a:TH + a + 1],
                                   attnT[:, a, :], ALU.mult, ALU.mult)
                    sig(last, "un_ready")
                w(layer, "un_ready", 1)
                if layer == 0:
                    dve.wait_ge(s_const, 16 * N_CONST)
                link(tt(einv, un, tiled(cst[:, C_MASK:C_MASK + P], TH), ALU.mult))
                sig(tt(einv, einv, tiled(ident, TH), ALU.add), "e1_ready")
                for t in range(NT):
                    w(layer, "qk_ps", t)
                    for hh in range(H):
                        a = 4 * t + hh
                        last = stt(attnT[:, a, :], ps[4 + t][:, hh * P:(hh + 1) * P], rr[:, TH + a:TH + a + 1],
                                   decay[:, a, :], ALU.mult, ALU.mult)
                    sig(last, "attn_ready")
                silu(2)
                link(tt(kdfac, kdfac, rr[:, TH:TH + H], ALU.mult))
                sig(tt(kdec[:, :, :], quad(ps[7][:, :]), over(kdfac, DH), ALU.mult), "kdec_ready")
                link(tt(ceg, cneg[:, H:TH], eg, ALU.mult))
                link(tsc(rqs, rr[:, 0:TH], DH ** -0.5, None, ALU.mult))
                link(tt(rqsq, rqs, rqs, ALU.mult))
                fill = [(g, t) for g in range(len(FILL_GROUPS)) for t in range(NT)]

                def filler():
                    if not fill:
                        return
                    g, t = fill.pop(0)
                    split_upto(2 * (CONV_GROUPS + g) + 2 + t)
                    if g == 2:
                        return
                    if g < 2:
                        if t == 0:
                            w(layer, "proj_first", g)
                        else:
                            dve.wait_ge(unit_used, base + 2 * CONV_GROUPS + 2 * g + 2)
                        rot = C_ROT + t * 256
                        src = ps[6 if (g, t) == (0, 0) else t][:, :]
                        v = src.rearrange("p (h s n) -> p h s n", h=H, s=2)
                        tv = th[:, t, :].rearrange("p (h s n) -> p h s n", h=H, s=2)
                        dst = rrot[:, g, t, :]
                        for s in range(2):
                            last = tt(tv[:, :, s, :], v[:, :, 1 - s, :],
                                      tiled(cst[:, rot + 128 + 64 * s:rot + 192 + 64 * s], H), ALU.mult)
                        link(last)
                        link(tt(quad(dst), quad(src), tiled(cst[:, rot:rot + 128], H), ALU.mult))
                        sig(tt(dst, dst, th[:, t, :], ALU.add), "rope_done")
                    else:
                        n = 2 * (g - 3) + t
                        w(layer, "th_g", n)
                        dst, name = (rgs, "rg_done") if g == 3 else (gzs, "gz_half")
                        sig(stt(dst[:, t, :], th[:, t, :], 1.0, ps[t][:, :], ALU.add, ALU.mult), name)

                filler()
                for t in range(NT):
                    w(layer, "vtok_ps", t)
                    sig(tt(quad(bv[:, t, :]), quad(ps[4 + t][:, :]), over(hbeta[:, 4 * t:4 * t + 4], DH),
                           ALU.mult), "bv_ready")
                for lv in range(1, len(LEVELS)):
                    filler()
                    if lv == 1:
                        w(layer, "e1_ready", 0)
                    for t in range(NT):
                        n = 2 * (lv - 1) + t
                        w(layer, "de_ps", n)
                        if n >= 2:
                            w(layer, "de_ready", n - 2)
                        sl = slice(4 * t, 4 * t + 4)
                        if lv < len(LEVELS) - 1:
                            tt(dinv[:, sl, :], dinv[:, sl, :], quad(ps[4 + t][:, :]), ALU.add)
                        sig(tt(einv[:, sl, :], einv[:, sl, :], quad(ps[6 + t][:, :]), ALU.add), "de_ready")
                    filler()
                w(layer, "ks_ps", 0)
                for hh in range(H):
                    c = slice(hh * P, (hh + 1) * P)
                    last = stt(rhs1[:, c], ps[2][:, c], ceg[:, hh:hh + 1], bv[:, 1, c], ALU.mult, ALU.add)
                sig(last, "rhs1_ready")
                for n in range(2):
                    w(layer, "s_ps", n)
                    dec = cst[:, C_DEC + n * 512:C_DEC + (n + 1) * 512]
                    sig(tt(st0[:, 2 * n:2 * n + 2, :].rearrange("p a b -> p (a b)"), ps[n][:, :], dec, ALU.mult),
                        "s_ready")
                w(layer, "s_ps", 2)
                dec = cst[:, C_DEC:C_DEC + H * 256].rearrange("p (a b) -> p a b", a=H)[:, :, 0:P]
                sig(tt(st1[:, :, :], quad(ps[3][:, :]), dec, ALU.mult), "s_ready")
                w(layer, "qs_ps", 0)
                sig(tt(quad(qs_sb[:, :]), quad(ps[5][:, :]), over(eg, DH), ALU.mult), "qs_done")
                for t in range(NT):
                    w(layer, "ro_ps", t)
                    sig(V.tensor_copy(o_ret[:, t, :], ps[t][:, :]), "ro_sb")
                w(layer, "go_ps", 0)
                sig(V.tensor_copy(o_gdn[:, 0, :], ps[6][:, :]), "go_sb")
                w(layer, "go_ps", 1)
                w(layer, "qs_done", 0)
                sig(tt(o_gdn[:, 1, :], ps[7][:, :], qs_sb[:, :], ALU.add), "go_sb")
                w(layer, "ro_sb", 1)
                w(layer, "go_sb", 1)
                sqv = st0[:, :, :].rearrange("p a b -> p (a b)")
                for r, src in enumerate((o_ret, o_gdn)):
                    flat = src.rearrange("p t n -> p (t n)")
                    link(tt(sqv, flat, flat, ALU.mult))
                    link(V.tensor_reduce(oss[:, r * TH:(r + 1) * TH], quad(sqv, TH), AX.X, ALU.add))
                link(tt(oss[:, TH:2 * TH], oss[:, TH:2 * TH], rqsq, ALU.mult))
                sig(tsc(oss, oss, 1.0 / DH, EPS, ALU.mult, ALU.add), "rms_in")
                w(layer, "rms_ready", 0)
                link(tt(ors[:, TH:2 * TH], ors[:, TH:2 * TH], rqs, ALU.mult))
                link(tsc(ors, ors, 0.5, None, ALU.mult))
                w(layer, "gz_done", 1)
                w(layer, "gz_half", 1)
                for r, (src, gate) in enumerate(((o_ret, rgs), (o_gdn, gzs))):
                    v = src.rearrange("p t n -> p (t n)")
                    link(tt(quad(v, TH), quad(v, TH), over(ors[:, r * TH:(r + 1) * TH], DH), ALU.mult))
                    sig(tt(v, v, gate[:, :, :].rearrange("p t n -> p (t n)"), ALU.mult), "br_ready")
                split_upto(25)
                for r in range(2):
                    w(layer, "br_hi", r)
                    for half in range(2):
                        sl = slice(2 * half, 2 * half + 2)
                        last = tt(br_lo[r][:, sl, :], quad(ps[4 + 2 * r + half][:, :], 2),
                                  br_hi[:, r, sl, :].bitcast(f32), ALU.subtract)
                    sig(last, "br_lo")
                split_upto(28)
                dve.wait_ge(unit_used, base + MIX_UNITS - 6)
                w(layer, "gate_done", 7)
                for t in range(NT):
                    for f in range(2):
                        g = gates[:, t, f * 512:(f + 1) * 512]
                        last = stt(g, g, 1.0, ps[2 * t + f][:, :], ALU.add, ALU.mult)
                sig(last, "ya_use")
                split_upto(29)
                dve.wait_ge(unit_used, base + MIX_UNITS - 4)
                for t in range(NT):
                    for f in range(2):
                        g = gates[:, t, DM + f * 512:DM + (f + 1) * 512]
                        last = stt(g, g, 1.0, ps[4 + 2 * t + f][:, :], ALU.add, ALU.mult)
                link(last)
                w(layer, "ya_use", 0)
                for t in range(NT):
                    sig(tt(hs[:, t, :], gates[:, t, 0:DM], gates[:, t, DM:2 * DM], ALU.add), "m_ready")
                split_upto(30)
                for m in range(4):
                    w(layer, "mx_hi", 4 + m)
                    sig(tt(mx_lo[:, 2 * m:2 * m + 2, :], quad(ps[m][:, :], 2),
                           mx_hi[:, 2 * m:2 * m + 2, :].bitcast(f32), ALU.subtract), "mx_lo")
                split_upto(31)
                dve.wait_ge(unit_used, base + MIX_UNITS)
                for t in range(NT):
                    for f in range(2):
                        c = slice(f * 512, (f + 1) * 512)
                        sig(stt(h[:, t, c], ps[4 + 2 * t + f][:, :], 0.5, h[:, t, c], ALU.mult, ALU.add), "h_upd")
                w(layer, "h_upd", 3)

            def split_low(off, j):
                dve.wait_ge(hi_ready, off + (j + 1))
                dve.wait_ge(unit_used, off + (j - SPLITS + 1))
                wh, wl = split_of(j)
                tt(wl, ring[:, j % SLOTS, :], wh.bitcast(f32), ALU.subtract).then_inc(lo_ready, 1)

            def dense_pass(base):
                for m in range(4):
                    dve.wait_ge(x_hi_ready, m + 1)
                    w(0, "hnT_ready", 4 + m)
                    tt(x_lo[:, 2 * m:2 * m + 2, :], hnT[:, 2 * m:2 * m + 2, :],
                       x_hi[:, 2 * m:2 * m + 2, :].bitcast(f32), ALU.subtract).then_inc(x_lo_ready, 1)
                split_low(base, 2)
                for j, (kind, c) in enumerate(pass_order()):
                    b = c % 2
                    if kind == "gate":
                        dve.wait_ge(ffn_th, c + 1)
                        if c >= 2:
                            dve.wait_ge(act_lo_ready, c - 1)
                        stt(a1[:, b, :], th_f[:, b, :], 1.0, ps[2 * b][:, :], ALU.add, ALU.mult).then_inc(ffn_a1, 1)
                    elif kind == "up":
                        dve.wait_ge(ffn_a1, c + 1)
                        dve.wait_ge(unit_used, base + j + 1)
                        stt(a1[:, b, :], a1[:, b, :], 0.5, ps[2 * b + 1][:, :],
                            ALU.mult, ALU.mult).then_inc(ffn_act, 1)
                        dve.wait_ge(act_hi_ready, c + 1)
                        dve.wait_ge(ffn_act, c + 1)
                        tt(act_lo[:, b, :, :].rearrange("p j n -> p (j n)"), a1[:, b, :],
                           act_hi[:, b, :, :].rearrange("p j n -> p (j n)").bitcast(f32),
                           ALU.subtract).then_inc(act_lo_ready, 1)
                    if j + SPLITS < PASS_UNITS:
                        split_low(base, j + SPLITS)
                dve.wait_ge(unit_used, base + PASS_UNITS)
                for t in range(NT):
                    for f in range(2):
                        c = slice(f * 512, (f + 1) * 512)
                        tt(h[:, t, c], h[:, t, c], ps[4 + 2 * t + f][:, :], ALU.add).then_inc(ffn_drained, 1)
                dve.wait_ge(ffn_drained, 4)

            def build_gsel(q, e):
                V.tensor_copy(pcur.unsqueeze(2), quad(posm, NT)[:, :, bass.ds(e, 1)]).then_inc(pcur_ready, 1)
                dve.wait_ge(pcur_ready, q + 1)
                for t in range(NT):
                    last = tsc(gsel[:, t, :], cst[:, C_IOTA:C_IOTA + P], pcur[:, t:t + 1], None, ALU.is_equal)
                last.then_inc(g_built, 1)

            def low_gathered(q):
                for m in range(2):
                    dve.wait_ge(xg_hi_ready, q * 2 + m + 1)
                    tt(xg_lo[:, 4 * m:4 * m + 4, :], quad(ps[6 + m][:, :]),
                       xg_hi[:, 4 * m:4 * m + 4, :].bitcast(f32), ALU.subtract).then_inc(xg_lo_ready, 1)

            def low_actT(q, c):
                dve.wait_ge(aT_hi_ready, q * NCHUNK + c + 1)
                tt(actT_lo[:, c % 2, :, :], quad(ps[6 + c % 2][:, 0:2 * P], 2),
                   actT_hi[:, c % 2, :, :].bitcast(f32), ALU.subtract).then_inc(aT_lo_ready, 1)

            def expert_pass(rnd, e, final):
                q = e + rnd * NEXP
                off = q * PASS_UNITS + STATIC_UNITS
                V.tensor_copy(gcur.unsqueeze(2), quad(gw, NT)[:, :, bass.ds(e, 1)]).then_inc(gcur_ready, 1)
                for j, (kind, c) in enumerate(pass_order()):
                    b = c % 2
                    if kind == "gate":
                        dve.wait_ge(ffn_th, q * NCHUNK + NCHUNK + c + 1)
                        stt(a1[:, b, 0:FF_CHUNK], th_f[:, b, 0:FF_CHUNK], 1.0, ps[2 * b][:, 0:FF_CHUNK],
                            ALU.add, ALU.mult).then_inc(ffn_a1, 1)
                        if c:
                            low_actT(q, c - 1)
                    elif kind == "up":
                        dve.wait_ge(ffn_a1, q * NCHUNK + NCHUNK + c + 1)
                        dve.wait_ge(unit_used, off + j + 1)
                        if c >= 2:
                            dve.wait_ge(aT_ps, q * NCHUNK + c - 1)
                        stt(a_tok[:, b, :], a1[:, b, 0:FF_CHUNK], 0.5, ps[2 * b + 1][:, 0:FF_CHUNK],
                            ALU.mult, ALU.mult).then_inc(ffn_act, 1)
                        if c == NCHUNK - 1 and not final:
                            dve.wait_ge(gt_ps, q + 1)
                            build_gsel(q + 1, e + 1)
                    elif c == NCHUNK - 2:
                        low_actT(q, NCHUNK - 1)
                    elif c == NCHUNK - 1:
                        for f in range(2):
                            dve.wait_ge(y_hi_ready, q * 2 + f + 1)
                            col = slice(f * 512, (f + 1) * 512)
                            tt(y_lo[:, col], ps[4 + f][:, :], y_hi[:, col].bitcast(f32),
                               ALU.subtract).then_inc(y_lo_ready, 1)
                        if not final:
                            low_gathered(q + 1)
                    if j + SPLITS < PASS_UNITS:
                        split_low(off, j + SPLITS)
                    elif not final:
                        split_low(off + PASS_UNITS, j + SPLITS - PASS_UNITS)
                dve.wait_ge(gcur_ready, q + 1)
                for t in range(NT):
                    dve.wait_ge(sc_ps, q * 2 + t + 1)
                    for f in range(2):
                        c = slice(f * 512, (f + 1) * 512)
                        last = stt(h[:, t, c], ps[4 - 2 * t + f][:, :], gcur[:, t:t + 1], h[:, t, c],
                                   ALU.mult, ALU.add)
                    last.then_inc(moe_drained, 1)
                dve.wait_ge(moe_drained, q * 2 + 3)

            def expert_round(rnd):
                q = rnd * NEXP
                if rnd:
                    link(tsc(posm, posm, -float(P), None, ALU.add))
                    dve.wait_ge(gt_ps, NEXP)
                build_gsel(q, 0)
                low_gathered(q)
                for j in range(SPLITS if rnd else 0):
                    split_low(q * PASS_UNITS + STATIC_UNITS, j)
                with dve.Fori(0, NEXP - 1) as e:
                    expert_pass(rnd, e, False)
                expert_pass(rnd, NEXP - 1, True)

            def split_two(off):
                split_low(off, 0)
                split_low(off, 1)

            dve.wait_ge(s_h, 16)
            mixer(0, 0)
            norm(0, 1, lambda: split_two(MIX_UNITS))
            dense_pass(MIX_UNITS)
            mixer(1, LAYER0_UNITS)
            norm(1, 1, lambda: split_two(STATIC_UNITS))
            dve.wait_ge(router_ps, 1)
            link(V.tensor_copy(logit, ps[0][:, 0:16]))
            for t in range(NT):
                lg = logit[:, t * NEXP:(t + 1) * NEXP]
                a, b = over(lg, NEXP), tiled(lg, NEXP)
                g1, g2 = quad(cmp1[:, t, :], NEXP), quad(cmp2[:, t, :], NEXP)
                tt(g1, b, a, ALU.is_gt)
                link(tt(g2, b, a, ALU.is_equal))
                link(tt(g2, g2, quad(cst[:, C_LOW:C_LOW + 64], NEXP), ALU.mult))
                link(tt(g1, g1, g2, ALU.add))
                link(V.tensor_reduce(rank[:, t * NEXP:(t + 1) * NEXP], g1, AX.X, ALU.add))
                link(V.max(top[:, t * 8:(t + 1) * 8], lg))
            tv = quad(top, NT)
            tt(p0, tv[:, :, 1], tv[:, :, 0], ALU.subtract).then_inc(router_in, 1)
            tsc(selm, rank, 1.0, None, ALU.is_le).then_inc(sel_ready, 1)
            split_low(STATIC_UNITS, 2)
            for t in range(NT):
                for m in range(2):
                    dve.wait_ge(hs_hi_ready, 2 * t + m + 1)
                    col = slice(m * 512, (m + 1) * 512)
                    tt(hs_lo[:, t, col], ps[2 + 2 * t + m][:, :], hs_hi[:, t, col].bitcast(f32),
                       ALU.subtract).then_inc(hs_lo_ready, 1)
            dve.wait_ge(router_e, 1)
            link(tsc(p0, pd, 1.0, None, ALU.add))
            link(V.reciprocal(p0, p0))
            link(tt(p1, pd, p0, ALU.mult))
            link(tsc(sel, rank, 0.0, None, ALU.is_equal))
            link(tt(quad(gw, NT), quad(sel, NT), over(p0, NEXP), ALU.mult))
            link(tsc(sel, rank, 1.0, None, ALU.is_equal))
            link(tt(quad(sel, NT), quad(sel, NT), over(p1, NEXP), ALU.mult))
            link(tt(gw, gw, sel, ALU.add))
            dve.wait_ge(sel_ready, 1)
            link(V.memset(posm, 0.0))
            dve.wait_ge(pos_ps, 1)
            pv = quad(posm, NT)[:, :, 0:NEXP]
            link(tt(pv, quad(ps[0][:, 0:NT * NEXP], NT), quad(selm, NT), ALU.mult))
            tsc(posm, posm, -1.0, None, ALU.add).then_inc(moe_drained, 1)
            dve.wait_ge(moe_drained, 1)
            link(V.tensor_reduce(cntm, ps[0][:, 2 * NEXP:3 * NEXP], AX.X, ALU.max))
            link(tsc(over_f, cntm, float(P), None, ALU.is_gt))
            V.tensor_copy(over_i[:, :], over_f).then_inc(over_ready, 1)
            expert_round(0)
            dve.wait_ge(over_ready, 1)
            with dve.If(dve.value_load(over_i[0:1, 0:1], min_val=0, max_val=1)):
                expert_round(1)
            sumsq(s_fin_ss)
            dve.wait_ge(s_fnorm, 16)
            dve.wait_ge(s_fin_rs, 1)
            for t in range(NT):
                stt(hs[:, t, :], h[:, t, :], rs[:, t:t + 1], fnorm, ALU.mult, ALU.mult).then_inc(s_final, 1)


_INS = ['x', 'norm_mix', 'w_in', 'conv_w', 'a_log', 'dt_bias', 'gdn_norm', 'w_branch', 'w_out', 'norm_ffn',
        'dense_w_gate', 'dense_w_up', 'dense_w_down', 'router', 'moe_w_gate', 'moe_w_up', 'moe_w_down', 'final_norm']


def kernel(**inputs):
    import concourse.bacc as _bacc
    from concourse.bass_utils import run_bass_kernel_spmd as _run

    nc = _bacc.Bacc("TRN2", target_bir_lowering=False, num_devices=1)
    arrays, args = {}, []
    for name in _INS + ['shape_constants']:
        a = shape_constants() if name == 'shape_constants' else np.ascontiguousarray(inputs[name])
        arrays[f"in_{name}_dram"] = a
        args.append(nc.dram_tensor(f"in_{name}_dram", a.shape, mybir.dt.from_np(a.dtype), kind="ExternalInput").ap())
    o = nc.dram_tensor("out_0_dram", (1, SEQ, DM), mybir.dt.float32, kind="ExternalOutput").ap()
    build(nc, *args, o)
    r = _run(nc, [arrays], core_ids=[0])
    return r.results[0]["out_0_dram"]
```
